# Optimizing a Trainium2 kernel written in Bass

```python
import jax, jax.numpy as jnp
from jax import lax
import numpy as np
import math
import jax
import jax.numpy as jnp

D_MODEL = 1024
BATCH = 1
SEQ = 512
DEPTH = 1

N_META = 16
BLOCK = 128
LEAD = BLOCK
FOX_HD = 64
FOX_HEADS = D_MODEL // FOX_HD
FOX_W = FOX_HEADS * FOX_HD
RET_HEADS = 4
RET_DK = D_MODEL // (2 * RET_HEADS)
RET_DV = 2 * RET_DK
RET_QK = RET_HEADS * RET_DK
RET_V = RET_HEADS * RET_DV
D_FF = ((8 * D_MODEL // 3 + 127) // 128) * 128
IN_SIZES = (FOX_W, FOX_W, FOX_W, FOX_HEADS, RET_QK, RET_QK, RET_V, RET_V, D_MODEL, D_MODEL)
N_IN = sum(IN_SIZES)
IN_SPLITS = [int(s) for s in np.cumsum(IN_SIZES)[:-1]]
EPS = 1e-6
GN_EPS = 1e-5
ROPE_BASE = 10000.0
FORGET_BIAS_INIT = 3.0
NEG = -1e30


def rmsnorm(x, g):
    xf = x.astype(jnp.float32)
    y = xf * lax.rsqrt(jnp.mean(xf * xf, axis=-1, keepdims=True) + EPS)
    return (y * g.astype(jnp.float32)).astype(x.dtype)

def swiglu(x, w_in, w_out):
    a, b = jnp.split(x @ w_in, 2, axis=-1)
    return (jax.nn.silu(a) * b) @ w_out

def rotary(x, pos):
    half = x.shape[-1] // 2
    inv = ROPE_BASE ** (-jnp.arange(half, dtype=jnp.float32) / half)
    ang = pos[:, None] * inv[None, :]
    cos, sin = jnp.cos(ang)[None, :, None, :], jnp.sin(ang)[None, :, None, :]
    xf = x.astype(jnp.float32)
    x1, x2 = xf[..., :half], xf[..., half:]
    return jnp.concatenate([x1 * cos - x2 * sin, x2 * cos + x1 * sin], axis=-1)

def forgetting_attention(q, k, v, logf, valid):
    B, H, P, hd = q.shape
    nb = P // BLOCK
    c = jnp.cumsum(logf, axis=-1)
    kpos = jnp.arange(P)
    scale = hd ** -0.5

    def block(i):
        s0 = i * BLOCK
        qb = lax.dynamic_slice_in_dim(q, s0, BLOCK, axis=2)
        cb = lax.dynamic_slice_in_dim(c, s0, BLOCK, axis=2)
        logits = jnp.einsum('bhqd,bhkd->bhqk', qb, k) * scale + cb[..., None] - c[:, :, None, :]
        qpos = s0 + jnp.arange(BLOCK)
        allowed = (kpos[None, :] <= qpos[:, None]) & (valid[None, :] | (kpos[None, :] == qpos[:, None]))
        p = jax.nn.softmax(jnp.where(allowed[None, None], logits, NEG), axis=-1)
        return jnp.einsum('bhqk,bhkd->bhqd', p, v)

    out = lax.map(block, jnp.arange(nb))
    return out.transpose(1, 2, 0, 3, 4).reshape(B, H, P, hd)

def retention(q, k, v, log_gamma):
    B, H, P, dk = q.shape
    dv = v.shape[-1]
    nc = P // BLOCK
    qc = q.reshape(B, H, nc, BLOCK, dk)
    kc = k.reshape(B, H, nc, BLOCK, dk)
    vc = v.reshape(B, H, nc, BLOCK, dv)
    n = jnp.arange(BLOCK, dtype=jnp.float32)
    diff = n[:, None] - n[None, :]
    lg = log_gamma[:, None, None]
    decay = jnp.where(diff >= 0, jnp.exp(lg * jnp.maximum(diff, 0.0)), 0.0)
    scores = jnp.einsum('bhcnd,bhcmd->bhcnm', qc, kc) * decay[None, :, None]
    out = jnp.einsum('bhcnm,bhcme->bhcne', scores, vc)
    zeta = jnp.exp(log_gamma[:, None] * (BLOCK - 1 - n)[None, :])
    kv = jnp.einsum('bhcmd,bhcme->cbhde', kc * zeta[None, :, None, :, None], vc)
    chunk_decay = jnp.exp(log_gamma * BLOCK)[None, :, None, None]

    def step(R, kv_c):
        return chunk_decay * R + kv_c, R

    _, r_prev = lax.scan(step, jnp.zeros((B, H, dk, dv), jnp.float32), kv)
    xi = jnp.exp(log_gamma[:, None] * (n + 1.0)[None, :])
    out = out + jnp.einsum('bhcnd,cbhde->bhcne', qc * xi[None, :, None, :, None], r_prev)
    return out.reshape(B, H, P, dv)

def head_groupnorm(y, g):
    mu = jnp.mean(y, axis=-1, keepdims=True)
    var = jnp.mean(jnp.square(y - mu), axis=-1, keepdims=True)
    yn = (y - mu) * lax.rsqrt(var + GN_EPS)
    B, H, P, dv = y.shape
    return yn.transpose(0, 2, 1, 3).reshape(B, P, H * dv) * g.astype(jnp.float32)

def hybrid_layer(h, valid, pos, log_gamma, norm_ffn1, w_ffn1_in, w_ffn1_out, norm_mix, w_in,
                 b_forget, b_gate, fox_q_norm, fox_k_norm, w_o_fox, ret_gn, w_o_ret, w_out,
                 norm_ffn2, w_ffn2_in, w_ffn2_out):
    dt = h.dtype
    B, P, _ = h.shape
    h = h + 0.5 * swiglu(rmsnorm(h, norm_ffn1), w_ffn1_in, w_ffn1_out)
    u = rmsnorm(h, norm_mix)
    fq, fk, fv, ff, rq, rk, rv, rg, ga, gb = jnp.split(u @ w_in, IN_SPLITS, axis=-1)
    vmask = valid[None, :, None, None].astype(jnp.float32)

    def fox_heads(t):
        return t.reshape(B, P, FOX_HEADS, FOX_HD)
    q_a = rmsnorm(fox_heads(fq), fox_q_norm).astype(jnp.float32).transpose(0, 2, 1, 3)
    k_a = rmsnorm(fox_heads(fk), fox_k_norm).astype(jnp.float32).transpose(0, 2, 1, 3)
    v_a = fox_heads(fv).astype(jnp.float32).transpose(0, 2, 1, 3)
    logf = jax.nn.log_sigmoid(ff.astype(jnp.float32) + b_forget.astype(jnp.float32))
    logf = jnp.where(valid[None, :, None], logf, 0.0).transpose(0, 2, 1)
    y_a = forgetting_attention(q_a, k_a, v_a, logf, valid)
    y_a = y_a.transpose(0, 2, 1, 3).reshape(B, P, FOX_W).astype(dt)

    q_b = rotary(rq.reshape(B, P, RET_HEADS, RET_DK), pos).transpose(0, 2, 1, 3)
    k_b = (rotary(rk.reshape(B, P, RET_HEADS, RET_DK), pos) * (RET_DK ** -0.5) * vmask).transpose(0, 2, 1, 3)
    v_b = (rv.reshape(B, P, RET_HEADS, RET_DV).astype(jnp.float32) * vmask).transpose(0, 2, 1, 3)
    y_b = head_groupnorm(retention(q_b, k_b, v_b, log_gamma), ret_gn)
    y_b = (jax.nn.silu(rg.astype(jnp.float32)) * y_b).astype(dt)

    g_a = jax.nn.sigmoid(ga + b_gate[:D_MODEL])
    g_b = jax.nn.sigmoid(gb + b_gate[D_MODEL:])
    mixed = g_a * (y_a @ w_o_fox) + g_b * (y_b @ w_o_ret)
    h = h + mixed @ w_out

    h = h + 0.5 * swiglu(rmsnorm(h, norm_ffn2), w_ffn2_in, w_ffn2_out)
    return h

def first_inputs(seed: int = 0) -> dict:
    key = jax.random.key(seed)
    ks = jax.random.split(key, 20)
    f32 = jnp.float32

    def w(k, shape, fan_in):
        return jax.random.normal(k, shape, f32) * fan_in ** -0.5

    def gain(k, shape):
        return 1.0 + 0.01 * jax.random.normal(k, shape, f32)

    L = DEPTH
    return {
        "x": jax.random.normal(ks[0], (BATCH, SEQ, D_MODEL), f32),
        "meta_tokens": jax.random.normal(ks[1], (N_META, D_MODEL), f32),
        "norm_ffn1": gain(ks[2], (L, D_MODEL)),
        "w_ffn1_in": w(ks[3], (L, D_MODEL, 2 * D_FF), D_MODEL),
        "w_ffn1_out": w(ks[4], (L, D_FF, D_MODEL), D_FF),
        "norm_mix": gain(ks[5], (L, D_MODEL)),
        "w_in": w(ks[6], (L, D_MODEL, N_IN), D_MODEL),
        "b_forget": FORGET_BIAS_INIT + 0.1 * jax.random.normal(ks[7], (L, FOX_HEADS), f32),
        "b_gate": 0.01 * jax.random.normal(ks[8], (L, 2 * D_MODEL), f32),
        "fox_q_norm": gain(ks[9], (L, FOX_HD)),
        "fox_k_norm": gain(ks[10], (L, FOX_HD)),
        "w_o_fox": w(ks[11], (L, FOX_W, D_MODEL), FOX_W),
        "ret_gn": gain(ks[12], (L, RET_V)),
        "w_o_ret": w(ks[13], (L, RET_V, D_MODEL), RET_V),
        "w_out": w(ks[14], (L, D_MODEL, D_MODEL), D_MODEL),
        "norm_ffn2": gain(ks[15], (L, D_MODEL)),
        "w_ffn2_in": w(ks[16], (L, D_MODEL, 2 * D_FF), D_MODEL),
        "w_ffn2_out": w(ks[17], (L, D_FF, D_MODEL), D_FF),
    }

def first_block(x, meta_tokens, norm_ffn1, w_ffn1_in, w_ffn1_out, norm_mix, w_in, b_forget, b_gate,
              fox_q_norm, fox_k_norm, w_o_fox, ret_gn, w_o_ret, w_out, norm_ffn2, w_ffn2_in,
              w_ffn2_out):
    B, S, D = x.shape
    n_empty = LEAD - N_META
    h = jnp.concatenate([
        jnp.zeros((B, n_empty, D), x.dtype),
        jnp.broadcast_to(meta_tokens.astype(x.dtype)[None], (B, N_META, D)),
        x], axis=1)
    P = h.shape[1]
    idx = jnp.arange(P)
    valid = idx >= n_empty
    pos = (idx - n_empty).astype(jnp.float32)
    log_gamma = jnp.log1p(-jnp.exp2(-5.0 - jnp.arange(RET_HEADS, dtype=jnp.float32)))
    for l in range(DEPTH):
        h = hybrid_layer(h, valid, pos, log_gamma, norm_ffn1[l], w_ffn1_in[l], w_ffn1_out[l],
                         norm_mix[l], w_in[l], b_forget[l], b_gate[l], fox_q_norm[l], fox_k_norm[l],
                         w_o_fox[l], ret_gn[l], w_o_ret[l], w_out[l], norm_ffn2[l], w_ffn2_in[l],
                         w_ffn2_out[l])
    return h[:, LEAD:]


_first_inputs = first_inputs


def first_inputs(seed=0):
    import zlib

    import numpy as np

    out = dict(_first_inputs(seed))
    spreads = {}
    factors = {'norm_ffn1': 8.0,
     'norm_mix': 7.94,
     'b_forget': 7.146,
     'b_gate': 8.0,
     'fox_q_norm': 8.0,
     'fox_k_norm': 8.0,
     'ret_gn': 8.0,
     'norm_ffn2': 8.0}
    for name, (base, spread) in spreads.items():
        noise = np.random.default_rng([zlib.crc32(name.encode()), seed]).standard_normal(out[name].shape)
        drawn = base * np.exp(spread * noise) if base else spread * noise
        out[name] = __import__('jax').numpy.asarray(drawn.astype(out[name].dtype))
    for name, factor in factors.items():
        out[name] = (out[name] * factor).astype(out[name].dtype)
    return out


_narrow_inputs = first_inputs


def first_inputs(seed=0):

    out = dict(_narrow_inputs(seed))
    wider = {'b_forget': 8.53,
     'b_gate': 6.56,
     'fox_q_norm': 5.1,
     'fox_k_norm': 5.23,
     'ret_gn': 7.32,
     'norm_ffn2': 8.86}
    for name, times in wider.items():
        mean = out[name].mean()
        out[name] = (mean + times * (out[name] - mean)).astype(out[name].dtype)
    return out


CHUNK = 64
EPS_2 = 1e-5
N_BRANCH = 2
GMLP_BLOCK = 128
GMLP_WIDTH = 1024
GMLP_GROUPS = 8
GMLP_GDIM = GMLP_WIDTH // GMLP_GROUPS
SSM_INNER = 2 * D_MODEL
SSM_HEAD_DIM = 64
SSM_HEADS = SSM_INNER // SSM_HEAD_DIM
SSM_GROUPS = 4
SSM_HPG = SSM_HEADS // SSM_GROUPS
SSM_STATE = 128
SSM_CONV = 4
SSM_CHUNK = CHUNK
SSM_XBC = SSM_INNER + 2 * SSM_GROUPS * SSM_STATE
D_FF_2 = 2816
FFN_CONV = 3
IN_COLS = N_BRANCH * D_MODEL + 2 * GMLP_WIDTH + SSM_INNER + SSM_XBC + SSM_HEADS


def rmsnorm_2(x, w):
    xf = x.astype(jnp.float32)
    y = xf * lax.rsqrt(jnp.mean(xf * xf, axis=-1, keepdims=True) + EPS_2)
    return (y * w.astype(jnp.float32)).astype(x.dtype)

def causal_dwconv(x, w, b):
    K, C = w.shape
    y = lax.conv_general_dilated(
        x, w[:, None, :].astype(x.dtype), window_strides=(1,), padding=[(K - 1, 0)],
        dimension_numbers=('NWC', 'WIO', 'NWC'), feature_group_count=C)
    return y + b.astype(x.dtype)

def gmlp_mixer(za, ln_w, ln_b, w_s, b_s):
    Bsz, S, _ = za.shape
    z = jax.nn.gelu(za)
    u, v = jnp.split(z, 2, axis=-1)
    nb = S // GMLP_BLOCK
    v = v.reshape(Bsz, nb, GMLP_BLOCK, GMLP_GROUPS, GMLP_GDIM)
    vf = v.astype(jnp.float32)
    mu = jnp.mean(vf, axis=-1, keepdims=True)
    var = jnp.mean(jnp.square(vf - mu), axis=-1, keepdims=True)
    v = ((vf - mu) * lax.rsqrt(var + EPS_2) * ln_w.astype(jnp.float32)
         + ln_b.astype(jnp.float32)).astype(z.dtype)
    chunk_id = jnp.arange(GMLP_BLOCK) // CHUNK
    mask = chunk_id[None, :] <= chunk_id[:, None]
    ws = jnp.where(mask[None], w_s, 0).astype(v.dtype)
    sv = jnp.einsum('gts,bnsgd->bntgd', ws, v) + b_s.T.astype(v.dtype)[None, None, :, :, None]
    return u * sv.reshape(Bsz, S, GMLP_WIDTH)

def ssd_scan(x, dt, A, Bm, Cm):
    Bsz, S = x.shape[:2]
    L = SSM_CHUNK
    nc = S // L
    f32 = jnp.float32
    x = x.astype(f32).reshape(Bsz, nc, L, SSM_GROUPS, SSM_HPG, SSM_HEAD_DIM)
    dt = dt.reshape(Bsz, nc, L, SSM_GROUPS, SSM_HPG)
    Bm = Bm.astype(f32).reshape(Bsz, nc, L, SSM_GROUPS, SSM_STATE)
    Cm = Cm.astype(f32).reshape(Bsz, nc, L, SSM_GROUPS, SSM_STATE)
    a_cum = jnp.cumsum(dt * A.reshape(SSM_GROUPS, SSM_HPG), axis=2)
    xdt = x * dt[..., None]
    seg = a_cum[:, :, :, None] - a_cum[:, :, None, :]
    causal = jnp.tril(jnp.ones((L, L), dtype=bool))
    decay = jnp.exp(jnp.where(causal[:, :, None, None], seg, -jnp.inf))
    cb = jnp.einsum('bclgn,bcsgn->bclsg', Cm, Bm)
    y_diag = jnp.einsum('bclsg,bclsgh,bcsghp->bclghp', cb, decay, xdt)
    decay_end = jnp.exp(a_cum[:, :, -1:] - a_cum)
    states = jnp.einsum('bcsgn,bcsgh,bcsghp->bcghpn', Bm, decay_end, xdt)
    chunk_decay = jnp.exp(a_cum[:, :, -1])

    def step(h, inp):
        st, dec = inp
        return h * dec[..., None, None] + st, h

    h0 = jnp.zeros((Bsz, SSM_GROUPS, SSM_HPG, SSM_HEAD_DIM, SSM_STATE), f32)
    _, prev = lax.scan(step, h0, (jnp.moveaxis(states, 1, 0), jnp.moveaxis(chunk_decay, 1, 0)))
    prev = jnp.moveaxis(prev, 0, 1)
    y_off = jnp.einsum('bclgn,bcghpn,bclgh->bclghp', Cm, prev, jnp.exp(a_cum))
    return (y_diag + y_off).reshape(Bsz, S, SSM_HEADS, SSM_HEAD_DIM)

def mamba2_mixer(z, xbc, dt_raw, conv_w, conv_b, dt_bias, a_log, d_skip, norm_w):
    Bsz, S, _ = z.shape
    xbc = jax.nn.silu(causal_dwconv(xbc, conv_w, conv_b))
    xs, Bm, Cm = jnp.split(xbc, [SSM_INNER, SSM_INNER + SSM_GROUPS * SSM_STATE], axis=-1)
    xs = xs.reshape(Bsz, S, SSM_HEADS, SSM_HEAD_DIM)
    Bm = Bm.reshape(Bsz, S, SSM_GROUPS, SSM_STATE)
    Cm = Cm.reshape(Bsz, S, SSM_GROUPS, SSM_STATE)
    dt = jax.nn.softplus(dt_raw.astype(jnp.float32) + dt_bias.astype(jnp.float32))
    A = -jnp.exp(a_log.astype(jnp.float32))
    y = ssd_scan(xs, dt, A, Bm, Cm) + d_skip.astype(jnp.float32)[:, None] * xs.astype(jnp.float32)
    y = y.reshape(Bsz, S, SSM_INNER) * jax.nn.silu(z.astype(jnp.float32))
    yg = y.reshape(Bsz, S, SSM_GROUPS, SSM_INNER // SSM_GROUPS)
    yg = yg * lax.rsqrt(jnp.mean(yg * yg, axis=-1, keepdims=True) + EPS_2)
    y = yg.reshape(Bsz, S, SSM_INNER) * norm_w.astype(jnp.float32)
    return y.astype(z.dtype)

def second_inputs(seed: int = 0) -> dict:
    key = jax.random.key(seed)
    ks = jax.random.split(key, 24)

    def nrm(k, shape, scale):
        return jax.random.normal(k, shape, jnp.float32) * scale

    def gain(k, shape):
        return 1.0 + 0.02 * jax.random.normal(k, shape, jnp.float32)

    dt0 = jnp.exp(jax.random.uniform(ks[12], (DEPTH, SSM_HEADS), jnp.float32,
                                     np.log(1e-3), np.log(1e-1)))
    dt_bias = dt0 + jnp.log(-jnp.expm1(-dt0))
    a_log = jnp.log(jax.random.uniform(ks[13], (DEPTH, SSM_HEADS), jnp.float32, 1.0, 16.0))
    return {
        "x": nrm(ks[0], (BATCH, SEQ, D_MODEL), 1.0),
        "mix_norm_w": gain(ks[1], (DEPTH, D_MODEL)),
        "w_in": nrm(ks[2], (DEPTH, D_MODEL, IN_COLS), D_MODEL ** -0.5),
        "gate_bias": nrm(ks[3], (DEPTH, N_BRANCH, D_MODEL), 0.01),
        "gmlp_ln_w": gain(ks[4], (DEPTH, GMLP_GROUPS, GMLP_GDIM)),
        "gmlp_ln_b": nrm(ks[5], (DEPTH, GMLP_GROUPS, GMLP_GDIM), 0.01),
        "gmlp_ws": nrm(ks[6], (DEPTH, GMLP_GROUPS, GMLP_BLOCK, GMLP_BLOCK), 0.5 * GMLP_BLOCK ** -0.5),
        "gmlp_bs": gain(ks[7], (DEPTH, GMLP_GROUPS, GMLP_BLOCK)),
        "ssm_conv_w": nrm(ks[8], (DEPTH, SSM_CONV, SSM_XBC), SSM_CONV ** -0.5),
        "ssm_conv_b": nrm(ks[9], (DEPTH, SSM_XBC), 0.01),
        "ssm_dt_bias": dt_bias,
        "ssm_a_log": a_log,
        "ssm_d": gain(ks[10], (DEPTH, SSM_HEADS)),
        "ssm_norm_w": gain(ks[11], (DEPTH, SSM_INNER)),
        "w_proj_a": nrm(ks[14], (DEPTH, GMLP_WIDTH, D_MODEL), GMLP_WIDTH ** -0.5),
        "w_proj_b": nrm(ks[15], (DEPTH, SSM_INNER, D_MODEL), SSM_INNER ** -0.5),
        "w_out": nrm(ks[16], (DEPTH, D_MODEL, D_MODEL), D_MODEL ** -0.5),
        "ffn_norm_w": gain(ks[17], (DEPTH, D_MODEL)),
        "ffn_w_up": nrm(ks[18], (DEPTH, D_MODEL, 2 * D_FF_2), D_MODEL ** -0.5),
        "ffn_conv_w": nrm(ks[19], (DEPTH, FFN_CONV, 2 * D_FF_2), FFN_CONV ** -0.5),
        "ffn_conv_b": nrm(ks[20], (DEPTH, 2 * D_FF_2), 0.01),
        "ffn_w_down": nrm(ks[21], (DEPTH, D_FF_2, D_MODEL), D_FF_2 ** -0.5),
        "final_norm_w": gain(ks[22], (D_MODEL,)),
    }

def second_block(x, mix_norm_w, w_in, gate_bias, gmlp_ln_w, gmlp_ln_b, gmlp_ws, gmlp_bs,
              ssm_conv_w, ssm_conv_b, ssm_dt_bias, ssm_a_log, ssm_d, ssm_norm_w,
              w_proj_a, w_proj_b, w_out, ffn_norm_w, ffn_w_up, ffn_conv_w, ffn_conv_b,
              ffn_w_down, final_norm_w):
    splits = [D_MODEL, 2 * D_MODEL, 2 * D_MODEL + 2 * GMLP_WIDTH,
              2 * D_MODEL + 2 * GMLP_WIDTH + SSM_INNER,
              2 * D_MODEL + 2 * GMLP_WIDTH + SSM_INNER + SSM_XBC]
    h = x
    for l in range(DEPTH):
        xn = rmsnorm_2(h, mix_norm_w[l])
        proj = xn @ w_in[l]
        g_a, g_b, za, z, xbc, dt_raw = jnp.split(proj, splits, axis=-1)
        y_a = gmlp_mixer(za, gmlp_ln_w[l], gmlp_ln_b[l], gmlp_ws[l], gmlp_bs[l]) @ w_proj_a[l]
        y_b = mamba2_mixer(z, xbc, dt_raw, ssm_conv_w[l], ssm_conv_b[l], ssm_dt_bias[l],
                           ssm_a_log[l], ssm_d[l], ssm_norm_w[l]) @ w_proj_b[l]
        merged = (jax.nn.sigmoid(g_a + gate_bias[l, 0]) * y_a
                  + jax.nn.sigmoid(g_b + gate_bias[l, 1]) * y_b)
        h = h + merged @ w_out[l]
        hn = rmsnorm_2(h, ffn_norm_w[l])
        up = causal_dwconv(hn @ ffn_w_up[l], ffn_conv_w[l], ffn_conv_b[l])
        gate, val = jnp.split(up, 2, axis=-1)
        h = h + (jax.nn.silu(gate) * val) @ ffn_w_down[l]
    return rmsnorm_2(h, final_norm_w)


_first_inputs_2 = second_inputs


def second_inputs(seed=0):
    import zlib

    import numpy as np

    out = dict(_first_inputs_2(seed))
    spreads = {}
    factors = {'mix_norm_w': 2.995,
     'gate_bias': 8.0,
     'gmlp_ln_w': 50.004,
     'gmlp_ln_b': 64.0,
     'gmlp_bs': 22.311,
     'ssm_conv_b': 36.475,
     'ssm_d': 59.112,
     'ssm_norm_w': 45.338,
     'ffn_norm_w': 12.085,
     'ffn_conv_b': 23.728,
     'final_norm_w': 7.973}
    for name, (base, spread) in spreads.items():
        noise = np.random.default_rng([zlib.crc32(name.encode()), seed]).standard_normal(out[name].shape)
        drawn = base * np.exp(spread * noise) if base else spread * noise
        out[name] = __import__('jax').numpy.asarray(drawn.astype(out[name].dtype))
    for name, factor in factors.items():
        out[name] = (out[name] * factor).astype(out[name].dtype)
    return out


_narrow_inputs_2 = second_inputs


def second_inputs(seed=0):

    out = dict(_narrow_inputs_2(seed))
    wider = {'gmlp_ln_w': 4.3,
     'gmlp_ln_b': 6.33,
     'gmlp_bs': 4.14,
     'ssm_d': 7.44,
     'ssm_norm_w': 4.27,
     'final_norm_w': 3.18}
    for name, times in wider.items():
        mean = out[name].mean()
        out[name] = (mean + times * (out[name] - mean)).astype(out[name].dtype)
    return out


HEAD_DIM = 64
NSA_HEADS = 8
NSA_KV_GROUPS = 2
NSA_HPG = NSA_HEADS // NSA_KV_GROUPS
RWKV_HEADS = 8
D_NSA = NSA_HEADS * HEAD_DIM
D_RWKV = RWKV_HEADS * HEAD_DIM
D_MIX = D_NSA + D_RWKV
D_KV = NSA_KV_GROUPS * HEAD_DIM
CMP_BLOCK = 32
CMP_STRIDE = 16
CMP_HIDDEN = 128
SEL_BLOCK = 64
SEL_TOPN = 16
WINDOW = 512
Q_BLOCK = 128
N_BUCKETS = 32
MAX_DISTANCE = 128
LORA_W = 64
LORA_A = 64
LORA_G = 128
D_FF_3 = 2816
CONV_W = 3
NORM_EPS = 1e-6
GN_EPS_3 = 64e-5
NEG_INF = -1e30
FORCE_SCORE = 1e9
NSA_SPLITS = (D_NSA, D_KV, D_KV, D_KV, D_KV, D_KV, D_KV, 3 * NSA_HEADS)
RWKV_SPLITS = (D_RWKV, D_RWKV, D_RWKV, LORA_W, LORA_A, LORA_G)
D_NSA_IN = sum(NSA_SPLITS)
D_RWKV_IN = sum(RWKV_SPLITS)
D_IN = D_NSA_IN + D_RWKV_IN


def rmsnorm_3(x, g, eps=NORM_EPS):
    xf = x.astype(jnp.float32)
    y = xf * lax.rsqrt(jnp.mean(xf * xf, axis=-1, keepdims=True) + eps)
    return (y * g).astype(x.dtype)

def t5_bucket(dist):
    n = jnp.maximum(dist, 0)
    max_exact = N_BUCKETS // 2
    nf = jnp.maximum(n, 1).astype(jnp.float32)
    large = max_exact + (jnp.log(nf / max_exact) / math.log(MAX_DISTANCE / max_exact)
                         * (N_BUCKETS - max_exact)).astype(jnp.int32)
    large = jnp.minimum(large, N_BUCKETS - 1)
    return jnp.where(n < max_exact, n, large)

def token_shift(z):
    return jnp.pad(z, ((0, 0), (1, 0), (0, 0)))[:, :-1]

def causal_dwconv_3(z, w, b):
    T = z.shape[1]
    zp = jnp.pad(z, ((0, 0), (CONV_W - 1, 0), (0, 0)))
    return b + sum(zp[:, i:i + T] * w[i] for i in range(CONV_W))

def compress(kv, pos, w1, b1, w2, b2):
    B, T, G, dh = kv.shape
    nc = (T - CMP_BLOCK) // CMP_STRIDE + 1
    idx = jnp.arange(nc)[:, None] * CMP_STRIDE + jnp.arange(CMP_BLOCK)[None, :]
    blk = kv[:, idx] + pos[None, None, :, None, :]
    blk = blk.transpose(0, 1, 3, 2, 4).reshape(B, nc, G, CMP_BLOCK * dh)
    return jax.nn.gelu(blk @ w1 + b1) @ w2 + b2

def nsa_attention(q, k_cmp, v_cmp, k_sel, v_sel, k_win, v_win, gates, rel_bias):
    B, T = q.shape[0], q.shape[1]
    G, R, dh = NSA_KV_GROUPS, NSA_HPG, HEAD_DIM
    nc = k_cmp.shape[1]
    ns = T // SEL_BLOCK
    n_top = min(SEL_TOPN, ns)
    scale = dh ** -0.5
    bias_grq = rel_bias.reshape(N_BUCKETS, G, R)
    bias_gbr = bias_grq.transpose(1, 0, 2)
    cmp_start = jnp.arange(nc) * CMP_STRIDE
    cmp_end = cmp_start + CMP_BLOCK - 1
    sel_start = jnp.arange(ns) * SEL_BLOCK
    overlap = ((cmp_start[:, None] < sel_start[None, :] + SEL_BLOCK)
               & (cmp_end[:, None] >= sel_start[None, :])).astype(jnp.float32)
    ks_blk = k_sel.reshape(B, ns, SEL_BLOCK, G, dh).transpose(0, 3, 1, 2, 4)
    vs_blk = v_sel.reshape(B, ns, SEL_BLOCK, G, dh).transpose(0, 3, 1, 2, 4)
    kw_pad = jnp.pad(k_win, ((0, 0), (WINDOW, 0), (0, 0), (0, 0)))
    vw_pad = jnp.pad(v_win, ((0, 0), (WINDOW, 0), (0, 0), (0, 0)))
    b_ix = jnp.arange(B)[:, None, None, None]
    g_ix = jnp.arange(G)[None, :, None, None]
    blk_ix = jnp.arange(SEL_BLOCK)
    win_ix = jnp.arange(Q_BLOCK + WINDOW)
    sel_ix = jnp.arange(ns)[None, :]

    def query_block(qb):
        q0 = qb * Q_BLOCK
        t = q0 + jnp.arange(Q_BLOCK)
        qq = lax.dynamic_slice_in_dim(q, q0, Q_BLOCK, axis=1).reshape(B, Q_BLOCK, G, R, dh)
        gg = lax.dynamic_slice_in_dim(gates, q0, Q_BLOCK, axis=1).reshape(B, Q_BLOCK, G, R, 3)

        d_c = t[:, None] - cmp_end[None, :]
        m_c = d_c >= 0
        l_c = (jnp.einsum('bqgrd,bcgd->bgrqc', qq, k_cmp).astype(jnp.float32) * scale
               + bias_grq[t5_bucket(d_c)].transpose(2, 3, 0, 1))
        p_c = jax.nn.softmax(jnp.where(m_c, l_c, NEG_INF), axis=-1) * m_c
        o_c = jnp.einsum('bgrqc,bcgd->bqgrd', p_c.astype(v_cmp.dtype), v_cmp)

        imp = jnp.einsum('bgrqc,cn->bgqn', p_c, overlap)
        cur = (t // SEL_BLOCK)[:, None]
        forced = (sel_ix == 0) | (sel_ix == cur) | (sel_ix == cur - 1)
        score = jnp.where(sel_start[None, :] <= t[:, None],
                          jnp.where(forced, FORCE_SCORE, imp), NEG_INF)
        _, top_idx = lax.top_k(score, n_top)
        k_s = ks_blk[b_ix, g_ix, top_idx].reshape(B, G, Q_BLOCK, n_top * SEL_BLOCK, dh)
        v_s = vs_blk[b_ix, g_ix, top_idx].reshape(B, G, Q_BLOCK, n_top * SEL_BLOCK, dh)
        s_pos = (top_idx[..., None] * SEL_BLOCK + blk_ix).reshape(B, G, Q_BLOCK, n_top * SEL_BLOCK)
        d_s = t[None, None, :, None] - s_pos
        m_s = (d_s >= 0)[:, :, None]
        l_s = (jnp.einsum('bqgrd,bgqkd->bgrqk', qq, k_s).astype(jnp.float32) * scale
               + bias_gbr[g_ix, t5_bucket(d_s)].transpose(0, 1, 4, 2, 3))
        p_s = jax.nn.softmax(jnp.where(m_s, l_s, NEG_INF), axis=-1)
        o_s = jnp.einsum('bgrqk,bgqkd->bqgrd', p_s.astype(v_s.dtype), v_s)

        k_w = lax.dynamic_slice_in_dim(kw_pad, q0, Q_BLOCK + WINDOW, axis=1)
        v_w = lax.dynamic_slice_in_dim(vw_pad, q0, Q_BLOCK + WINDOW, axis=1)
        s_w = q0 - WINDOW + win_ix
        d_w = t[:, None] - s_w[None, :]
        m_w = (d_w >= 0) & (d_w < WINDOW) & (s_w[None, :] >= 0)
        l_w = (jnp.einsum('bqgrd,bkgd->bgrqk', qq, k_w).astype(jnp.float32) * scale
               + bias_grq[t5_bucket(d_w)].transpose(2, 3, 0, 1))
        p_w = jax.nn.softmax(jnp.where(m_w, l_w, NEG_INF), axis=-1)
        o_w = jnp.einsum('bgrqk,bkgd->bqgrd', p_w.astype(v_w.dtype), v_w)

        o = gg[..., 0:1] * o_c + gg[..., 1:2] * o_s + gg[..., 2:3] * o_w
        return o.reshape(B, Q_BLOCK, D_NSA)

    out = lax.map(query_block, jnp.arange(T // Q_BLOCK))
    return out.transpose(1, 0, 2, 3).reshape(B, T, D_NSA)

def _wkv7_step(state, inp):
    r, w, k, v, a, b = inp
    sa = jnp.einsum('bhvk,bhk->bhv', state, a)
    state = state * w[:, :, None, :] + sa[..., None] * b[:, :, None, :] + v[..., None] * k[:, :, None, :]
    return state, jnp.einsum('bhvk,bhk->bhv', state, r)

def rwkv7_time_mix(feats, w0, w2, a0, a2, g2, k_k, k_a, r_k, ln_w, ln_b):
    B, T, _ = feats.shape
    H, N = RWKV_HEADS, HEAD_DIM
    r, k, v, xw, xa, xg = jnp.split(feats, np.cumsum(RWKV_SPLITS)[:-1].tolist(), axis=-1)
    w = -jax.nn.softplus(-(w0 + jnp.tanh(xw) @ w2)) - 0.5
    decay = jnp.exp(-jnp.exp(w.astype(jnp.float32)))
    a = jax.nn.sigmoid(a0 + xa @ a2)
    g = jax.nn.sigmoid(xg) @ g2

    def heads(z):
        return z.reshape(B, T, H, N).astype(jnp.float32)

    kk = heads(k * k_k)
    kk = kk / jnp.maximum(jnp.sqrt(jnp.sum(kk * kk, axis=-1, keepdims=True)), 1e-12)
    k = k * (1.0 + (a - 1.0) * k_a)
    rh, kh, vh, ah = heads(r), heads(k), heads(v), heads(a)
    xs = tuple(z.transpose(1, 0, 2, 3) for z in (rh, heads(decay), kh, vh, -kk, kk * ah))
    state0 = jnp.zeros((B, H, N, N), jnp.float32)
    _, y = lax.scan(_wkv7_step, state0, xs)
    y = y.transpose(1, 0, 2, 3)
    mu = jnp.mean(y, axis=-1, keepdims=True)
    var = jnp.mean(jnp.square(y - mu), axis=-1, keepdims=True)
    y = ((y - mu) * lax.rsqrt(var + GN_EPS_3)).reshape(B, T, D_RWKV) * ln_w + ln_b
    bonus = jnp.sum(rh * kh * r_k, axis=-1, keepdims=True) * vh
    y = (y + bonus.reshape(B, T, D_RWKV)) * g
    return y.astype(feats.dtype)

def third_inputs(seed: int = 0) -> dict:
    key = jax.random.key(seed)
    ks = list(jax.random.split(key, 32))
    L = DEPTH

    def nrm(shape, scale):
        return scale * jax.random.normal(ks.pop(), shape, jnp.float32)

    def unif(shape, lo, hi):
        return jax.random.uniform(ks.pop(), shape, jnp.float32, minval=lo, maxval=hi)

    return {
        'x': nrm((BATCH, SEQ, D_MODEL), 1.0),
        'norm1_g': 1.0 + nrm((L, D_MODEL), 0.02),
        'w_in': nrm((L, D_MODEL, D_IN), D_MODEL ** -0.5),
        'q_norm_g': 1.0 + nrm((L, HEAD_DIM), 0.02),
        'k_norm_g': 1.0 + nrm((L, 3, HEAD_DIM), 0.02),
        'cmp_pos': nrm((L, 2, CMP_BLOCK, HEAD_DIM), 0.02),
        'cmp_w1': nrm((L, 2, CMP_BLOCK * HEAD_DIM, CMP_HIDDEN), (CMP_BLOCK * HEAD_DIM) ** -0.5),
        'cmp_b1': nrm((L, 2, CMP_HIDDEN), 0.02),
        'cmp_w2': nrm((L, 2, CMP_HIDDEN, HEAD_DIM), CMP_HIDDEN ** -0.5),
        'cmp_b2': nrm((L, 2, HEAD_DIM), 0.02),
        'rel_bias': nrm((N_BUCKETS, NSA_HEADS), 0.5),
        'rwkv_mu': unif((L, D_RWKV_IN), 0.0, 1.0),
        'w0': unif((L, D_RWKV), -6.0, -1.0),
        'w2': nrm((L, LORA_W, D_RWKV), 0.1 * LORA_W ** -0.5),
        'a0': nrm((L, D_RWKV), 0.1),
        'a2': nrm((L, LORA_A, D_RWKV), 0.5 * LORA_A ** -0.5),
        'g2': nrm((L, LORA_G, D_RWKV), LORA_G ** -0.5),
        'k_k': 0.85 + nrm((L, D_RWKV), 0.02),
        'k_a': 1.0 + nrm((L, D_RWKV), 0.02),
        'r_k': nrm((L, RWKV_HEADS, HEAD_DIM), 0.1),
        'ln_x_w': 1.0 + nrm((L, D_RWKV), 0.02),
        'ln_x_b': nrm((L, D_RWKV), 0.02),
        'w_out': nrm((L, D_MIX, D_MODEL), D_MIX ** -0.5),
        'norm2_g': 1.0 + nrm((L, D_MODEL), 0.02),
        'ffn_up': nrm((L, D_MODEL, 2 * D_FF_3), D_MODEL ** -0.5),
        'conv_w': nrm((L, CONV_W, 2 * D_FF_3), CONV_W ** -0.5),
        'conv_b': nrm((L, 2 * D_FF_3), 0.02),
        'ffn_down': nrm((L, D_FF_3, D_MODEL), D_FF_3 ** -0.5),
    }

def third_block(x, norm1_g, w_in, q_norm_g, k_norm_g, cmp_pos, cmp_w1, cmp_b1, cmp_w2, cmp_b2,
              rel_bias, rwkv_mu, w0, w2, a0, a2, g2, k_k, k_a, r_k, ln_x_w, ln_x_b,
              w_out, norm2_g, ffn_up, conv_w, conv_b, ffn_down):
    B, T, _ = x.shape
    G, H, dh = NSA_KV_GROUPS, NSA_HEADS, HEAD_DIM
    nsa_cuts = np.cumsum(NSA_SPLITS)[:-1].tolist()

    def kv_heads(z):
        return z.reshape(B, T, G, dh)

    for l in range(DEPTH):
        h = rmsnorm_3(x, norm1_g[l])
        proj = h @ w_in[l]
        q, kc, vc, ksl, vsl, kwn, vwn, gl = jnp.split(proj[..., :D_NSA_IN], nsa_cuts, axis=-1)
        q = rmsnorm_3(q.reshape(B, T, H, dh), q_norm_g[l])
        k_cmp = rmsnorm_3(compress(kv_heads(kc), cmp_pos[l, 0], cmp_w1[l, 0], cmp_b1[l, 0],
                                 cmp_w2[l, 0], cmp_b2[l, 0]), k_norm_g[l, 0])
        v_cmp = compress(kv_heads(vc), cmp_pos[l, 1], cmp_w1[l, 1], cmp_b1[l, 1],
                         cmp_w2[l, 1], cmp_b2[l, 1])
        k_sel = rmsnorm_3(kv_heads(ksl), k_norm_g[l, 1])
        k_win = rmsnorm_3(kv_heads(kwn), k_norm_g[l, 2])
        gates = jax.nn.sigmoid(gl).reshape(B, T, H, 3)
        o_nsa = nsa_attention(q, k_cmp, v_cmp, k_sel, kv_heads(vsl), k_win, kv_heads(vwn),
                              gates, rel_bias)

        rw = proj[..., D_NSA_IN:]
        rw = rw + (token_shift(rw) - rw) * rwkv_mu[l]
        o_rwkv = rwkv7_time_mix(rw, w0[l], w2[l], a0[l], a2[l], g2[l], k_k[l], k_a[l],
                                r_k[l], ln_x_w[l], ln_x_b[l])
        x = x + jnp.concatenate([o_nsa, o_rwkv], axis=-1) @ w_out[l]

        h = rmsnorm_3(x, norm2_g[l])
        u = causal_dwconv_3(h @ ffn_up[l], conv_w[l], conv_b[l])
        u_val, u_gate = jnp.split(u, 2, axis=-1)
        x = x + (jax.nn.silu(u_gate) * u_val) @ ffn_down[l]
    return x


_first_inputs_3 = third_inputs


def third_inputs(seed=0):
    import zlib

    import numpy as np

    out = dict(_first_inputs_3(seed))
    spreads = {}
    factors = {'norm1_g': 3.5,
     'q_norm_g': 30.083,
     'k_norm_g': 33.869,
     'cmp_pos': 57.34,
     'cmp_b1': 55.935,
     'cmp_b2': 64.0,
     'w2': 52.336,
     'a0': 3.553,
     'k_k': 64.0,
     'k_a': 6.728,
     'ln_x_w': 56.096,
     'ln_x_b': 56.968,
     'norm2_g': 19.251,
     'conv_b': 18.351,
     'rel_bias': 8.0}
    for name, (base, spread) in spreads.items():
        noise = np.random.default_rng([zlib.crc32(name.encode()), seed]).standard_normal(out[name].shape)
        drawn = base * np.exp(spread * noise) if base else spread * noise
        out[name] = jnp.asarray(drawn.astype(out[name].dtype))
    for name, factor in factors.items():
        out[name] = (out[name] * factor).astype(out[name].dtype)
    return out


_narrow_inputs_3 = third_inputs


def third_inputs(seed=0):

    out = dict(_narrow_inputs_3(seed))
    wider = {'q_norm_g': 3.22, 'k_norm_g': 3.52, 'rel_bias': 9.36, 'k_k': 9.01}
    for name, times in wider.items():
        mean = out[name].mean()
        out[name] = (mean + times * (out[name] - mean)).astype(out[name].dtype)
    return out


def setup_inputs(seed=0):
    out = dict(first_inputs(seed))
    for name, value in second_inputs(seed + 1).items():
        if name != "x":
            out[name + "_2"] = value
    for name, value in third_inputs(seed + 2).items():
        if name != "x":
            out[name + "_3"] = value
    return out


def reference(
    x, meta_tokens, norm_ffn1, w_ffn1_in, w_ffn1_out, norm_mix, w_in, b_forget, b_gate,
    fox_q_norm, fox_k_norm, w_o_fox, ret_gn, w_o_ret, w_out, norm_ffn2, w_ffn2_in, w_ffn2_out,
    mix_norm_w_2, w_in_2, gate_bias_2, gmlp_ln_w_2, gmlp_ln_b_2, gmlp_ws_2, gmlp_bs_2,
    ssm_conv_w_2, ssm_conv_b_2, ssm_dt_bias_2, ssm_a_log_2, ssm_d_2, ssm_norm_w_2, w_proj_a_2,
    w_proj_b_2, w_out_2, ffn_norm_w_2, ffn_w_up_2, ffn_conv_w_2, ffn_conv_b_2, ffn_w_down_2,
    final_norm_w_2, norm1_g_3, w_in_3, q_norm_g_3, k_norm_g_3, cmp_pos_3, cmp_w1_3, cmp_b1_3,
    cmp_w2_3, cmp_b2_3, rel_bias_3, rwkv_mu_3, w0_3, w2_3, a0_3, a2_3, g2_3, k_k_3, k_a_3,
    r_k_3, ln_x_w_3, ln_x_b_3, w_out_3, norm2_g_3, ffn_up_3, conv_w_3, conv_b_3, ffn_down_3,
):
    x = first_block(
        x, meta_tokens, norm_ffn1, w_ffn1_in, w_ffn1_out, norm_mix, w_in, b_forget, b_gate,
        fox_q_norm, fox_k_norm, w_o_fox, ret_gn, w_o_ret, w_out, norm_ffn2, w_ffn2_in,
        w_ffn2_out,
    )
    x = second_block(
        x, mix_norm_w_2, w_in_2, gate_bias_2, gmlp_ln_w_2, gmlp_ln_b_2, gmlp_ws_2, gmlp_bs_2,
        ssm_conv_w_2, ssm_conv_b_2, ssm_dt_bias_2, ssm_a_log_2, ssm_d_2, ssm_norm_w_2,
        w_proj_a_2, w_proj_b_2, w_out_2, ffn_norm_w_2, ffn_w_up_2, ffn_conv_w_2, ffn_conv_b_2,
        ffn_w_down_2, final_norm_w_2,
    )
    return third_block(
        x, norm1_g_3, w_in_3, q_norm_g_3, k_norm_g_3, cmp_pos_3, cmp_w1_3, cmp_b1_3, cmp_w2_3,
        cmp_b2_3, rel_bias_3, rwkv_mu_3, w0_3, w2_3, a0_3, a2_3, g2_3, k_k_3, k_a_3, r_k_3,
        ln_x_w_3, ln_x_b_3, w_out_3, norm2_g_3, ffn_up_3, conv_w_3, conv_b_3, ffn_down_3,
    )


_drawn_inputs = setup_inputs


def setup_inputs(seed=0):
    import zlib

    import numpy as np

    out = dict(_drawn_inputs(seed))
    spreads = {}
    factors = {}
    for name, (base, spread) in spreads.items():
        noise = np.random.default_rng([zlib.crc32(name.encode()), seed]).standard_normal(out[name].shape)
        drawn = base * np.exp(spread * noise) if base else spread * noise
        out[name] = jnp.asarray(drawn.astype(out[name].dtype))
    for name, factor in factors.items():
        out[name] = (out[name] * factor).astype(out[name].dtype)
    return out
```

```python
from contextlib import ExitStack

import numpy as np

import concourse.bass as bass
from concourse import mybir

F32 = mybir.dt.float32
ALU = mybir.AluOpType
ACT = mybir.ActivationFunctionType
AX = mybir.AxisListType

P = 128
T = 512
META = 16
TM = T + META
NT = T // P
D = 1024
KD = D // P
FF = 2816
KF = FF // P
WEIGHT_SLOTS = 4
SLOT = 2048
CREDIT = 64
NEG = -1e30


def cols(buf, start, width, rows=P, row0=0):
    if isinstance(start, int):
        return buf[row0:row0 + rows, start:start + width]
    return buf[row0:row0 + rows, bass.ds(start, width)]


def steps(eng, n, unroll):
    rounds = n // unroll
    if rounds > 1:
        with eng.Fori(0, rounds) as i:
            for u in range(unroll):
                yield i, i * unroll + u, u
    elif rounds == 1:
        for u in range(unroll):
            yield 0, u, u
    for u in range(n % unroll):
        yield rounds, rounds * unroll + u, u


class Signal:

    def __init__(self, handle, start):
        self.h = handle
        self.start = start

    def __call__(self, n):
        return self.h, self.start + n


class Semaphores:

    def __init__(self, nc, ctx, count):
        self.free = [[ctx.enter_context(nc.semaphore(f"stage_signal_{i}")), CREDIT] for i in range(count)]
        self.all = [h for h, _ in self.free]

    def take(self, total):
        entry = self.free.pop(0)
        signal = Signal(entry[0], entry[1])
        self.free.append([entry[0], entry[1] + total])
        return signal


class Chain:

    def __init__(self, eng, signal, before=0):
        self.eng, self.sem, self.before, self.n = eng, signal, before, 0

    def __call__(self, instruction, wait=True):
        self.n += 1
        instruction.then_inc(self.sem.h, 1)
        if wait:
            self.eng.wait_ge(*self.sem(self.before + self.n))


class Product:

    def __init__(self, stream, weights, kt, slots, columns, width, ksplit=1):
        self.stream, self.kt, self.slots, self.columns, self.width, self.ksplit = stream, kt, slots, columns, width, ksplit
        self.view = weights.rearrange("(k p) n -> p k n", p=P)
        self.parts = len(columns(0))
        self.first = stream.slots_planned
        self.loads = list(stream.loads)
        self.groups = slots // ksplit
        stream.slots_planned += slots
        for k in range(slots):
            s = (self.first + k) % WEIGHT_SLOTS
            stream.loads[s] += 16 * self.parts
        self.sent = 0
        stream.plans.append(self)

    def slot_of(self, u):
        return (self.first + u) % WEIGHT_SLOTS

    def slot(self, u):
        s = self.slot_of(u)
        return self.stream.ring[:, s * SLOT:s * SLOT + self.kt * self.width].rearrange("p (k n) -> p k n", n=self.width)

    def send(self, eng, i, k, u):
        eng.wait_ge(self.stream.used, CREDIT + self.first + k - WEIGHT_SLOTS + 1)
        group = k if self.ksplit == 1 else i * (WEIGHT_SLOTS // self.ksplit) + u // self.ksplit
        k0 = (u % self.ksplit) * self.kt
        for c0, width, column in self.columns(group):
            n = slice(column, column + width) if isinstance(column, int) else bass.ds(column, width)
            eng.dma_start(self.slot(u)[:, :, c0:c0 + width], self.view[:, k0:k0 + self.kt, n])\
               .then_inc(self.stream.full[self.slot_of(u)], 16)

    def send_first(self, eng):
        for k in range(min(WEIGHT_SLOTS, self.slots)):
            self.send(eng, k // WEIGHT_SLOTS, k, k)
            self.sent += 1

    def send_rest(self, eng):
        rounds = self.slots // WEIGHT_SLOTS
        if rounds > 2:
            with eng.Fori(1, rounds) as i:
                for u in range(WEIGHT_SLOTS):
                    self.send(eng, i, i * WEIGHT_SLOTS + u, u)
        elif rounds == 2:
            for u in range(WEIGHT_SLOTS):
                self.send(eng, 1, WEIGHT_SLOTS + u, u)
        for k in range(max(rounds, 1) * WEIGHT_SLOTS, self.slots):
            self.send(eng, k // WEIGHT_SLOTS, k, k % WEIGHT_SLOTS)

    def wait_full(self, pe, i, u):
        s = self.slot_of(u)
        pe.wait_ge(self.stream.full[s], CREDIT + self.loads[s] + (i + 1) * 16 * self.parts)

    def done(self, group):
        return self.stream.used, CREDIT + self.first + (group + 1) * self.ksplit


class WeightStream:

    def __init__(self, nc, ctx):
        self.ring = ctx.enter_context(nc.sbuf_tensor("weight_ring", [P, WEIGHT_SLOTS * SLOT], F32))
        self.full = [ctx.enter_context(nc.semaphore(f"weight_slot_full_{s}")) for s in range(WEIGHT_SLOTS)]
        self.used = ctx.enter_context(nc.semaphore("weight_slots_used"))
        self.loads = [0] * WEIGHT_SLOTS
        self.slots_planned = 0
        self.plans = []
        self.at = 0

    def run(self, eng):
        plan = self.plans[self.at]
        if self.at == 0:
            plan.send_first(eng)
        plan.send_rest(eng)
        self.at += 1
        if self.at < len(self.plans):
            self.plans[self.at].send_first(eng)


class Kernel:

    def __init__(self, nc, ctx):
        self.nc = nc
        self.sems = Semaphores(nc, ctx, 40)
        self.stream = WeightStream(nc, ctx)
        self.ps = ctx.enter_context(nc.psum_tensor("psum", [P, 8 * T], F32))
        self.ctx = ctx

    def bank(self, b, width=T, rows=P, at=0):
        return self.ps[0:rows, b * T + at:b * T + at + width]

    def sb(self, ctx, name, width, rows=P):
        return ctx.enter_context(self.nc.sbuf_tensor(name, [rows, width], F32))


def product_t(K, plan, src, stride, col_tiles, evacuated, meta=False, rows=P, banks=0, meta_bank=4):
    def program(pe):
        per = WEIGHT_SLOTS // plan.ksplit
        for i, k, u in steps(pe, plan.slots, WEIGHT_SLOTS):
            part, pair = u % plan.ksplit, (u // plan.ksplit) % 2
            plan.wait_full(pe, i, u)
            if part == 0:
                for e in evacuated:
                    pe.wait_ge(*e(i * per + u // plan.ksplit - 1))
            for ct in range(col_tiles):
                for kt in range(plan.kt):
                    a = part * plan.kt + kt
                    flags = dict(start=a == 0, stop=a == plan.kt * plan.ksplit - 1)
                    w = plan.slot(u)[:, kt, ct * P:ct * P + rows]
                    last = pe.matmul(K.bank(banks + 2 * pair + ct, rows=rows), w, src[:, a * stride:a * stride + T], **flags)
                    if meta:
                        last = pe.matmul(K.bank(meta_bank + pair, META, rows, ct * META), w,
                                         src[:, a * stride + T:a * stride + TM], **flags)
            last.then_inc(K.stream.used, 1)
    return program


def product_n(K, plan, src, stride, width, evacuated, meta=False):
    def program(pe):
        for i, k, u in steps(pe, plan.slots, WEIGHT_SLOTS):
            pair = u % 2
            plan.wait_full(pe, i, u)
            for e in evacuated:
                pe.wait_ge(*e(k - 1))
            for t in range(NT):
                for kt in range(plan.kt):
                    last = pe.matmul(K.bank(2 * pair + t // 2, width, P, (t % 2) * 256),
                                     src[:, kt * stride + t * P:kt * stride + (t + 1) * P],
                                     plan.slot(u)[:, kt, 0:width], start=kt == 0, stop=kt == plan.kt - 1)
            if meta:
                for kt in range(plan.kt):
                    last = pe.matmul(K.bank(4 + pair, width, META), src[:, kt * stride + T:kt * stride + TM],
                                     plan.slot(u)[:, kt, 0:width], start=kt == 0, stop=kt == plan.kt - 1)
            last.then_inc(K.stream.used, 1)
    return program


def rmsnorm_t(K, x, out, stride, gain, eps, meta=False):
    nc = K.nc
    squared, summed, shifted, rooted = K.sems.take(KD), K.sems.take(1), K.sems.take(1), K.sems.take(1)
    own = K.sems.take(1)
    width = TM if meta else T
    with ExitStack() as ctx:
        r = K.sb(ctx, f"rms_scale_{nc.next_id()}", TM)
        block = ctx.enter_context(nc.Block())

        @block.scalar
        def _(act):
            for j in range(KD):
                c = slice(j * stride, j * stride + width)
                act.activation(out[:, c], x[:, c], ACT.Square).then_inc(squared.h, 1)
            act.wait_ge(*shifted(1))
            act.activation(r[:, 0:width], r[:, 0:width], ACT.Sqrt).then_inc(rooted.h, 1)

        @block.tensor
        def _(pe):
            for j in range(KD):
                pe.wait_ge(*squared(j + 1))
                last = pe.matmul(K.bank(0), K.ones[:, :], out[:, j * stride:j * stride + T], start=j == 0, stop=j == KD - 1)
                if meta:
                    last = pe.matmul(K.bank(1, META), K.ones[:, :], out[:, j * stride + T:j * stride + TM],
                                     start=j == 0, stop=j == KD - 1)
            last.then_inc(summed.h, 1)

        @block.vector
        def _(dve):
            dve.wait_ge(*summed(1))
            dve.tensor_scalar(r[:, 0:width], K.ps[:, 0:width], 1.0 / D, eps, ALU.mult, ALU.add).then_inc(shifted.h, 1)
            dve.wait_ge(*rooted(1))
            dve.reciprocal(r[:, 0:width], r[:, 0:width]).then_inc(own.h, 1)
            dve.wait_ge(*own(1))
            for j in range(KD):
                c = slice(j * stride, j * stride + width)
                dve.scalar_tensor_tensor(out=out[:, c], in0=x[:, c], scalar=gain(j), in1=r[:, 0:width],
                                         op0=ALU.mult, op1=ALU.mult)


def swiglu(K, u, stride, x, up, down, meta=False):
    nc = K.nc
    width = TM if meta else T
    silus, products = K.sems.take(up.groups), K.sems.take(up.groups)
    added = K.sems.take(down.groups)
    with ExitStack() as ctx:
        hidden = K.sb(ctx, f"ffn_hidden_{nc.next_id()}", KF * width)
        gated = K.sb(ctx, f"ffn_gate_{nc.next_id()}", 2 * width)
        block = ctx.enter_context(nc.Block())

        @block.sync
        def _(sync):
            K.stream.run(sync)
            K.stream.run(sync)

        @block.tensor
        def _(pe):
            product_t(K, up, u, stride, 2, [products], meta)(pe)
            pe.wait_ge(*products(up.groups))
            product_t(K, down, hidden, width, 1, [added], meta)(pe)

        @block.scalar
        def _(act):
            for i, k, s in steps(act, up.groups, WEIGHT_SLOTS):
                pair = s % 2
                act.wait_ge(*up.done(k))
                act.wait_ge(*products(k - 1))
                last = act.activation(gated[:, pair * width:pair * width + T], K.bank(2 * pair), ACT.Silu)
                if meta:
                    last = act.activation(gated[:, pair * width + T:pair * width + TM], K.bank(4 + pair, META), ACT.Silu)
                last.then_inc(silus.h, 1)

        @block.vector
        def _(dve):
            for i, k, s in steps(dve, up.groups, WEIGHT_SLOTS):
                pair = s % 2
                dve.wait_ge(*silus(k + 1))
                last = dve.tensor_tensor(cols(hidden, k * width, T), gated[:, pair * width:pair * width + T],
                                         K.bank(2 * pair + 1), ALU.mult)
                if meta:
                    last = dve.tensor_tensor(cols(hidden, k * width + T, META),
                                             gated[:, pair * width + T:pair * width + TM],
                                             K.bank(4 + pair, META, P, META), ALU.mult)
                last.then_inc(products.h, 1)
            for i, k, s in steps(dve, down.groups, WEIGHT_SLOTS):
                pair = s % 2
                dve.wait_ge(*down.done(k))
                x_k = cols(x, k * stride, T)
                last = dve.scalar_tensor_tensor(out=x_k, in0=K.bank(2 * pair), scalar=0.5, in1=x_k,
                                                op0=ALU.mult, op1=ALU.add)
                if meta:
                    x_k = cols(x, k * stride + T, META)
                    last = dve.scalar_tensor_tensor(out=x_k, in0=K.bank(4 + pair, META), scalar=0.5, in1=x_k,
                                                    op0=ALU.mult, op1=ALU.add)
                last.then_inc(added.h, 1)


def head_norm_t(K, buf, stride, tiles, gain, eps, meta_tiles=()):
    nc = K.nc
    n = len(tiles)
    squared, summed, shifted, rooted = (K.sems.take(n) for _ in range(4))
    own = K.sems.take(n)
    scaled = K.sems.take(n)
    with ExitStack() as ctx:
        sq = K.sb(ctx, f"head_squares_{nc.next_id()}", 2 * TM)
        r = K.sb(ctx, f"head_scale_{nc.next_id()}", 2 * TM)
        block = ctx.enter_context(nc.Block())
        width = [TM if t in meta_tiles else T for t in tiles]

        @block.scalar
        def _(act):
            def root(k):
                act.wait_ge(*shifted(k + 1))
                c = slice((k % 2) * TM, (k % 2) * TM + width[k])
                act.activation(r[:, c], r[:, c], ACT.Sqrt).then_inc(rooted.h, 1)
            for k, t in enumerate(tiles):
                if k >= 2:
                    act.wait_ge(*summed(k - 1))
                act.activation(sq[:, (k % 2) * TM:(k % 2) * TM + width[k]], buf[:, t * stride:t * stride + width[k]],
                               ACT.Square).then_inc(squared.h, 1)
                if k >= 1:
                    root(k - 1)
            root(n - 1)

        @block.tensor
        def _(pe):
            for k, t in enumerate(tiles):
                pe.wait_ge(*squared(k + 1))
                pe.wait_ge(*shifted(k - 1))
                last = pe.matmul(K.bank(4 * (k % 2)), K.head_ones[:, :], sq[:, (k % 2) * TM:(k % 2) * TM + T], start=True, stop=True)
                if width[k] == TM:
                    last = pe.matmul(K.bank(4 * (k % 2) + 1, META), K.head_ones[:, :],
                                     sq[:, (k % 2) * TM + T:(k % 2) * TM + TM], start=True, stop=True)
                last.then_inc(summed.h, 1)

        @block.vector
        def _(dve):
            def scale(k):
                t = tiles[k]
                dve.wait_ge(*rooted(k + 1))
                c = slice((k % 2) * TM, (k % 2) * TM + width[k])
                dve.reciprocal(r[:, c], r[:, c]).then_inc(own.h, 1)
                dve.wait_ge(*own(k + 1))
                b = buf[:, t * stride:t * stride + width[k]]
                dve.scalar_tensor_tensor(out=b, in0=b, scalar=gain(t), in1=r[:, c], op0=ALU.mult, op1=ALU.mult).then_inc(scaled.h, 1)
            for k, t in enumerate(tiles):
                if k >= 2:
                    dve.wait_ge(*scaled(k - 1))
                dve.wait_ge(*summed(k + 1))
                dve.tensor_scalar(r[:, (k % 2) * TM:(k % 2) * TM + width[k]],
                                  K.ps[:, 4 * (k % 2) * T:4 * (k % 2) * T + width[k]], 1.0 / 64, eps,
                                  ALU.mult, ALU.add).then_inc(shifted.h, 1)
                if k >= 1:
                    scale(k - 1)
            scale(n - 1)


def load_vectors(K, rows):
    nc = K.nc
    total = sum(n for _, _, n in rows)
    tiles = -(-total // P)
    K.vectors = K.sb(K.ctx, "vector_columns", tiles * P)
    K.column = {}
    pieces, at = [], 0
    for name, src, n in rows:
        K.column[name] = at
        done = 0
        while done < n:
            take = min(n - done, P - at % P)
            pieces.append((at // P, at % P, src[done:done + take, :], take))
            done += take
            at += take
    landed, cleared, turned = K.sems.take(16 * len(pieces)), K.sems.take(1), K.sems.take(1)
    with ExitStack() as ctx:
        rows_sb = K.sb(ctx, "vector_rows", tiles * P)
        block = ctx.enter_context(nc.Block())

        @block.sync
        def _(sync):
            sync.wait_ge(*cleared(1))
            for t, r, src, n in pieces:
                sync.dma_start(rows_sb[r:r + n, t * P:(t + 1) * P], src).then_inc(landed.h, 16)

        @block.tensor
        def _(pe):
            pe.wait_ge(*landed(16 * len(pieces)))
            for t in range(tiles):
                last = pe.transpose(K.bank(t // 4, P, P, (t % 4) * P), rows_sb[:, t * P:(t + 1) * P], K.ident[:, :])
            last.then_inc(turned.h, 1)

        @block.vector
        def _(dve):
            dve.memset(rows_sb[:, :], 0.0).then_inc(cleared.h, 1)
            dve.wait_ge(*turned(1))
            dve.tensor_copy(K.vectors[:, :], K.ps[:, 0:tiles * P])


def vector(K, name):
    return lambda j=0: cols(K.vectors, K.column[name] + j, 1)


def load_x(K, x, meta, buf, stride):
    nc = K.nc
    landed, turned, copied = K.sems.take(32), K.sems.take(KD), K.sems.take(KD)
    with ExitStack() as ctx:
        rows = K.sb(ctx, "x_rows", NT * D)
        meta_rows = K.sb(ctx, "meta_rows", D, META)
        block = ctx.enter_context(nc.Block())

        @block.sync
        def _(sync):
            sync.dma_start(rows[:, :].rearrange("p (t d) -> p t d", d=D), x.rearrange("(t p) d -> p t d", p=P))\
                .then_inc(landed.h, 16)
            sync.dma_start(meta_rows[:, :], meta).then_inc(landed.h, 16)

        @block.tensor
        def _(pe):
            pe.wait_ge(*landed(32))
            for j in range(KD):
                pe.wait_ge(*copied(j - 1))
                b = 2 * (j % 2)
                for t in range(NT):
                    pe.transpose(K.bank(b, P, P, t * P), rows[:, t * D + j * P:t * D + (j + 1) * P], K.ident[:, :])
                pe.transpose(K.bank(b + 1, META), meta_rows[:, j * P:(j + 1) * P], K.ident[0:META, 0:META])\
                    .then_inc(turned.h, 1)

        @block.vector
        def _(dve):
            for j in range(KD):
                dve.wait_ge(*turned(j + 1))
                dve.tensor_copy(buf[:, j * stride:j * stride + TM], K.ps[:, 2 * (j % 2) * T:2 * (j % 2) * T + TM])\
                   .then_inc(copied.h, 1)


def turn_tokens(K, src, dst, tiles):
    nc = K.nc
    turned, copied = K.sems.take(tiles), K.sems.take(tiles)
    with ExitStack() as ctx:
        block = ctx.enter_context(nc.Block())

        @block.tensor
        def _(pe):
            for j in range(tiles):
                pe.wait_ge(*copied(j - 1))
                for t in range(NT):
                    last = pe.transpose(K.bank(j % 2, P, P, t * P),
                                        src[:, t * tiles * P + j * P:t * tiles * P + (j + 1) * P], K.ident[:, :])
                last.then_inc(turned.h, 1)

        @block.vector
        def _(dve):
            for j in range(tiles):
                dve.wait_ge(*turned(j + 1))
                dve.tensor_copy(dst[:, j * T:(j + 1) * T], K.bank(j % 2)).then_inc(copied.h, 1)


def project_t(K, plan, src, stride, dst, dst_stride, meta=False, func=None, bias=None, rows=P, col_tiles=2):
    nc = K.nc
    read = K.sems.take(plan.groups)
    with ExitStack() as ctx:
        block = ctx.enter_context(nc.Block())

        @block.sync
        def _(sync):
            K.stream.run(sync)

        @block.tensor
        def _(pe):
            product_t(K, plan, src, stride, col_tiles, [read], meta, rows)(pe)

        @block.scalar
        def _(act):
            for i, k, u in steps(act, plan.groups, WEIGHT_SLOTS):
                pair = u % 2
                act.wait_ge(*plan.done(k))
                for ct in range(col_tiles):
                    t = k * col_tiles + ct
                    more = {} if bias is None else dict(bias=bias(t))
                    f = ACT.Copy if func is None else func
                    last = act.activation(cols(dst, t * dst_stride, T, rows), K.bank(2 * pair + ct, rows=rows), f, **more)
                    if meta:
                        last = act.activation(cols(dst, t * dst_stride + T, META, rows),
                                              K.bank(4 + pair, META, rows, ct * META), f, **more)
                last.then_inc(read.h, 1)


def project_n(K, plan, src, stride, dst, width, total, meta_dst=None, func=None):
    nc = K.nc
    read = K.sems.take(plan.groups)
    with ExitStack() as ctx:
        block = ctx.enter_context(nc.Block())

        @block.sync
        def _(sync):
            K.stream.run(sync)

        @block.tensor
        def _(pe):
            product_n(K, plan, src, stride, width, [read], meta_dst is not None)(pe)

        @block.scalar
        def _(act):
            for i, k, u in steps(act, plan.groups, WEIGHT_SLOTS):
                pair = u % 2
                act.wait_ge(*plan.done(k))
                for t in range(NT):
                    last = act.activation(cols(dst, k * width + t * total, width),
                                          K.bank(2 * pair + t // 2, width, P, (t % 2) * 256), func or ACT.Copy)
                if meta_dst is not None:
                    last = act.activation(cols(meta_dst, k * width, width, META), K.bank(4 + pair, width, META), ACT.Copy)
                last.then_inc(read.h, 1)


def add_product(K, plan, src, stride, x, x_stride):
    nc = K.nc
    added = K.sems.take(plan.groups)
    with ExitStack() as ctx:
        block = ctx.enter_context(nc.Block())

        @block.sync
        def _(sync):
            K.stream.run(sync)

        @block.tensor
        def _(pe):
            product_t(K, plan, src, stride, 2, [added])(pe)

        @block.vector
        def _(dve):
            for i, k, u in steps(dve, plan.groups, WEIGHT_SLOTS):
                dve.wait_ge(*plan.done(k))
                for ct in range(2):
                    x_t = cols(x, (k * 2 + ct) * x_stride, T)
                    last = dve.tensor_tensor(x_t, x_t, K.bank(2 * (u % 2) + ct), ALU.add)
                last.then_inc(added.h, 1)


def gated_sum(K, plan_a, src_a, plan_b, src_b, gate_a, gate_b):
    nc = K.nc
    first, weighed, summed = K.sems.take(plan_a.groups), K.sems.take(plan_b.groups), K.sems.take(plan_b.groups)
    with ExitStack() as ctx:
        block = ctx.enter_context(nc.Block())

        @block.sync
        def _(sync):
            K.stream.run(sync)
            K.stream.run(sync)

        @block.tensor
        def _(pe):
            product_t(K, plan_a, src_a, T, 2, [first])(pe)
            pe.wait_ge(*first(plan_a.groups))
            product_t(K, plan_b, src_b, T, 2, [weighed])(pe)

        @block.vector
        def _(dve):
            for i, k, u in steps(dve, plan_a.groups, WEIGHT_SLOTS):
                dve.wait_ge(*plan_a.done(k))
                for ct in range(2):
                    g = cols(gate_a, (k * 2 + ct) * T, T)
                    last = dve.tensor_tensor(g, g, K.bank(2 * (u % 2) + ct), ALU.mult)
                last.then_inc(first.h, 1)
            for i, k, u in steps(dve, plan_b.groups, WEIGHT_SLOTS):
                dve.wait_ge(*plan_b.done(k))
                for ct in range(2):
                    g = cols(gate_b, (k * 2 + ct) * T, T)
                    last = dve.tensor_tensor(g, g, K.bank(2 * (u % 2) + ct), ALU.mult)
                last.then_inc(weighed.h, 1)
                dve.wait_ge(*weighed(k + 1))
                dve.wait_ge(*first(plan_a.groups))
                for ct in range(2):
                    a, b = cols(gate_a, (k * 2 + ct) * T, T), cols(gate_b, (k * 2 + ct) * T, T)
                    last = dve.tensor_tensor(a, a, b, ALU.add)
                last.then_inc(summed.h, 1)


FOX_HEADS = 16
RET_HEADS = 4
RET_DK = 128
RET_DV = 256


def forget_sums(K, plan, u, bias, ncB):
    nc = K.nc
    own, act_own = K.sems.take(6), K.sems.take(2)
    picked, spread, copied = K.sems.take(FOX_HEADS), K.sems.take(FOX_HEADS), K.sems.take(FOX_HEADS)
    bias_landed = K.sems.take(16)
    H = FOX_HEADS
    with ExitStack() as ctx:
        z, m, a, sums, ones_row = (K.sb(ctx, f"forget_{n}", TM, H) for n in ("z", "max", "abs", "sums", "one"))
        b = K.sb(ctx, "forget_bias", 1, H)
        row = K.sb(ctx, "forget_row", 2 * TM, H)
        block = ctx.enter_context(nc.Block())

        @block.sync
        def _(sync):
            sync.dma_start(b[:, :], bias.rearrange("(h a) -> h a", a=1)).then_inc(bias_landed.h, 16)
            K.stream.run(sync)

        @block.tensor
        def _(pe):
            product_t(K, plan, u, TM, 1, [], True, H)(pe)
            for h in range(H):
                pe.wait_ge(*picked(h + 1))
                pe.wait_ge(*copied(h - 1))
                bank = 2 * (h % 2)
                pe.matmul(K.bank(bank), K.ones[0:H, :], row[:, (h % 2) * TM:(h % 2) * TM + T], start=True, stop=True)
                pe.matmul(K.bank(bank + 1, META), K.ones[0:H, :], row[:, (h % 2) * TM + T:(h % 2 + 1) * TM],
                          start=True, stop=True).then_inc(spread.h, 1)

        @block.vector
        def _(dve):
            chain = Chain(dve, own)
            dve.wait_ge(*plan.done(0))
            dve.wait_ge(*bias_landed(16))
            dve.tensor_scalar(z[:, META:TM], K.bank(0, rows=H), b[:, 0:1], -1.0, ALU.add, ALU.mult)
            chain(dve.tensor_scalar(z[:, 0:META], K.bank(4, META, H), b[:, 0:1], -1.0, ALU.add, ALU.mult))
            chain(dve.tensor_scalar(m[:, :], z[:, :], 0.0, None, ALU.max))
            chain(dve.memset(ones_row[:, :], 1.0))
            chain(dve.scalar_tensor_tensor(out=a[:, :], in0=m[:, :], scalar=-2.0, in1=z[:, :], op0=ALU.mult, op1=ALU.add))
            dve.wait_ge(*act_own(2))
            chain(dve.tensor_tensor(m[:, :], m[:, :], a[:, :], ALU.add))
            chain(dve.tensor_tensor_scan(sums[:, :], ones_row[:, :], m[:, :], 0.0, ALU.mult, ALU.add))
            for h in range(H):
                dve.wait_ge(*spread(h - 1))
                dve.tensor_scalar(row[:, (h % 2) * TM:(h % 2 + 1) * TM], sums[:, :], K.ident[0:H, h:h + 1], None, ALU.mult)\
                   .then_inc(picked.h, 1)

        @block.scalar
        def _(act):
            act.wait_ge(*own(4))
            act.activation(a[:, :], a[:, :], ACT.Exp).then_inc(act_own.h, 1)
            act.wait_ge(*act_own(1))
            act.activation(a[:, :], a[:, :], ACT.Ln, bias=1.0).then_inc(act_own.h, 1)
            for h in range(H):
                act.wait_ge(*spread(h + 1))
                b0 = 2 * (h % 2) * T
                act.activation(ncB[:, h * TM:(h + 1) * TM], K.ps[:, b0:b0 + TM], ACT.Copy).then_inc(copied.h, 1)


def fox_attention(K, q, k, v, v_meta, ncB, y):
    nc = K.nc
    PAIRS = FOX_HEADS // 2
    ROUND = 2
    rounds = PAIRS // ROUND
    S = [(a, h, i) for a in range(ROUND) for h in range(2) for i in range(NT)]
    n = len(S)
    q_staged, k_staged = K.sems.take(PAIRS), K.sems.take(PAIRS)
    scored, probs, turned, turned_copied, weighed, out = (K.sems.take(rounds * n) for _ in range(6))
    score_steps, recips = K.sems.take(rounds * n * 3), K.sems.take(rounds * n)
    with ExitStack() as ctx:
        qs = [K.sb(ctx, f"fox_q_{a}", T) for a in range(ROUND)]
        ks = [K.sb(ctx, f"fox_k_{a}", TM) for a in range(ROUND)]
        L = [K.sb(ctx, f"fox_scores_{a}", TM) for a in range(2)]
        pt = [K.sb(ctx, f"fox_probs_t_{a}", T) for a in range(2)]
        pt_meta = [K.sb(ctx, f"fox_probs_t_meta_{a}", P, META) for a in range(2)]
        stat = [K.sb(ctx, f"fox_stat_{a}", 4) for a in range(2)]
        block = ctx.enter_context(nc.Block())
        def score_at(b):
            return (2 * b + 1) * T - META

        @block.gpsimd
        def _(pool):
            with pool.Fori(0, rounds) as r:
                for a in range(ROUND):
                    pool.wait_ge(*scored(r * n - (ROUND - 1 - a) * (n // ROUND)))
                    pool.tensor_copy(ks[a][:, :], cols(k, (r * ROUND + a) * TM, TM)).then_inc(k_staged.h, 1)

        @block.tensor
        def _(pe):
            with pe.Fori(0, rounds) as r:
                for s in range(n + 2):
                    if s < n:
                        a, h, i = S[s]
                        b = s % 2
                        if h == 0 and i == 0:
                            pe.wait_ge(*q_staged(r * ROUND + a + 1))
                            pe.wait_ge(*k_staged(r * ROUND + a + 1))
                        pe.wait_ge(*score_steps((r * n + s - 2) * 3 + 1))
                        rows = slice(64 * h, 64 * h + 64)
                        lhs = qs[a][rows, i * P:(i + 1) * P]
                        pe.matmul(K.ps[:, score_at(b):score_at(b) + META], lhs, ks[a][rows, T:TM], start=True, stop=True)
                        pe.matmul(K.bank(2 * b + 1, (i + 1) * P), lhs, ks[a][rows, 0:(i + 1) * P], start=True, stop=True)\
                            .then_inc(scored.h, 1)
                    if 1 <= s <= n:
                        _, _, i = S[s - 1]
                        b = (s - 1) % 2
                        pe.wait_ge(*probs(r * n + s))
                        pe.wait_ge(*turned_copied(r * n + s - 2))
                        pe.wait_ge(*out(r * n + s - 2))
                        pe.transpose(K.bank(6 + b, P, META), L[b][:, 0:META], K.ident[:, :])
                        for t in range(i + 1):
                            last = pe.transpose(K.bank(4 + b, P, P, t * P), L[b][:, META + t * P:META + (t + 1) * P], K.ident[:, :])
                        last.then_inc(turned.h, 1)
                    if s >= 2:
                        a, h, i = S[s - 2]
                        b = (s - 2) % 2
                        head = ((r * ROUND + a) * 2 + h) * 64
                        pe.wait_ge(*turned_copied(r * n + s - 1))
                        o = K.bank(6 + b, 64, P, 128)
                        for t in range(i + 1):
                            pe.matmul(o, pt[b][:, t * P:(t + 1) * P], cols(v, head + t * D, 64), start=t == 0, stop=False)
                        pe.matmul(o, pt_meta[b][:, :], cols(v_meta, head, 64, META), start=False, stop=True)\
                            .then_inc(weighed.h, 1)

        @block.vector
        def _(dve):
            with dve.Fori(0, rounds) as r:
                for s in range(n + 2):
                    if s < n:
                        a, h, i = S[s]
                        b = s % 2
                        w = META + (i + 1) * P
                        head = (r * ROUND + a) * 2 + h
                        chain = Chain(dve, score_steps, (r * n + s) * 3)
                        dve.wait_ge(*scored(r * n + s + 1))
                        dve.wait_ge(*turned(r * n + s - 1))
                        chain(dve.scalar_tensor_tensor(out=L[b][:, 0:w], in0=K.ps[:, score_at(b):score_at(b) + w],
                                                       scalar=64 ** -0.5, in1=cols(ncB, head * TM, w), op0=ALU.mult, op1=ALU.add))
                        diag = L[b][:, w - P:w]
                        chain(dve.tensor_tensor(diag, diag, K.causal[:, :], ALU.add))
                        chain(dve.tensor_reduce(stat[b][:, 0:1], L[b][:, 0:w], AX.X, ALU.max, negate=True))
                    if s >= 2:
                        a, h, i = S[s - 2]
                        b = (s - 2) % 2
                        dve.wait_ge(*weighed(r * n + s - 1))
                        dve.reciprocal(stat[b][:, 2:3], stat[b][:, 1:2]).then_inc(recips.h, 1)
                        dve.wait_ge(*recips(r * n + s - 1))
                        dve.tensor_scalar(cols(y, ((r * ROUND + a) * 2 + h) * 64 + i * D, 64), K.bank(6 + b, 64, P, 128),
                                          stat[b][:, 2:3], None, ALU.mult).then_inc(out.h, 1)

        @block.scalar
        def _(act):
            with act.Fori(0, rounds) as r:
                for a in range(ROUND):
                    act.wait_ge(*scored(r * n - (ROUND - 1 - a) * (n // ROUND)))
                    act.activation(qs[a][:, :], cols(q, (r * ROUND + a) * T, T), ACT.Copy).then_inc(q_staged.h, 1)
                for s in range(n + 1):
                    if s < n:
                        _, _, i = S[s]
                        b = s % 2
                        w = META + (i + 1) * P
                        act.wait_ge(*score_steps((r * n + s) * 3 + 3))
                        act.wait_ge(*out(r * n + s - 1))
                        act.activation(L[b][:, 0:w], L[b][:, 0:w], ACT.Exp, bias=stat[b][:, 0:1],
                                       accum_out=stat[b][:, 1:2]).then_inc(probs.h, 1)
                    if s >= 1:
                        _, _, i = S[s - 1]
                        b = (s - 1) % 2
                        act.wait_ge(*turned(r * n + s))
                        act.wait_ge(*weighed(r * n + s - 2))
                        act.activation(pt_meta[b][:, :], K.bank(6 + b, P, META), ACT.Copy)
                        act.activation(pt[b][:, 0:(i + 1) * P], K.bank(4 + b, (i + 1) * P), ACT.Copy).then_inc(turned_copied.h, 1)


def retention(K, q, k, v, v_meta, rg, y, tables):
    nc = K.nc
    H = RET_HEADS
    swapped, rotated, turned, scaled = K.sems.take(H), K.sems.take(H), K.sems.take(H), K.sems.take(H)
    scored, decayed, states, stated, out, normed, turned_y = (K.sems.take(H) for _ in range(7))
    own_n = 20
    own, rooted, gated = K.sems.take(H * own_n), K.sems.take(H), K.sems.take(H)
    loaded = K.sems.take(16 * 7)
    with ExitStack() as ctx:
        cos, sin = K.sb(ctx, "rope_cos", TM), K.sb(ctx, "rope_sin", TM)
        swap = K.sb(ctx, "rope_swap", P)
        decay = K.sb(ctx, "ret_decay", H * P)
        xi = K.sb(ctx, "ret_xi", H * P)
        zeta = K.sb(ctx, "ret_zeta", 3 * H)
        qs, qx, t1 = K.sb(ctx, "ret_q", T), K.sb(ctx, "ret_q_xi", T), K.sb(ctx, "ret_tmp", TM)
        ks, kz = K.sb(ctx, "ret_k", TM), K.sb(ctx, "ret_k_zeta", T)
        kz_meta = K.sb(ctx, "ret_k_zeta_meta", P, META)
        st = K.sb(ctx, "ret_scores", T)
        R = K.sb(ctx, "ret_state", NT * RET_DV)
        yn = K.sb(ctx, "ret_normed", NT * RET_DV)
        stats, mv, rstd = K.sb(ctx, "ret_stats", 6 * NT + 2), K.sb(ctx, "ret_mean_var", 2 * NT), K.sb(ctx, "ret_rstd", NT)
        block = ctx.enter_context(nc.Block())

        @block.sync
        def _(sync):
            for dst, name in ((cos, "rope_cos"), (sin, "rope_sin"), (swap, "swap"), (decay, "decay"), (xi, "xi")):
                sync.dma_start(dst[:, :], tables[name]).then_inc(loaded.h, 16)
            sync.dma_start(zeta[:, 0:2 * H], tables["zeta"]).then_inc(loaded.h, 16)
            sync.dma_start(zeta[0:META, 2 * H:3 * H], tables["zeta_meta"]).then_inc(loaded.h, 16)

        @block.tensor
        def _(pe):
            pe.wait_ge(*loaded(16 * 7))
            with pe.Fori(0, H) as h:
                pe.wait_ge(*gated(h))
                pe.matmul(K.bank(0), swap[:, :], cols(q, h * T, T), start=True, stop=True)
                pe.matmul(K.bank(1), swap[:, :], cols(k, h * TM, T), start=True, stop=True)
                pe.matmul(K.bank(2, META), swap[:, :], cols(k, h * TM + T, META), start=True, stop=True)\
                    .then_inc(swapped.h, 1)
                pe.wait_ge(*rotated(h + 1))
                for c in range(NT):
                    pe.transpose(K.bank(3, P, P, c * P), ks[:, c * P:(c + 1) * P], K.ident[:, :])
                pe.transpose(K.bank(2, P, META, P), ks[:, T:TM], K.ident[:, :]).then_inc(turned.h, 1)
                for c in range(NT):
                    last = pe.matmul(K.bank(0, P, P, c * P), ks[:, c * P:(c + 1) * P], qs[:, c * P:(c + 1) * P],
                                     start=True, stop=True)
                last.then_inc(scored.h, 1)
                pe.wait_ge(*scaled(h + 1))
                for c in range(NT - 1):
                    pe.matmul(K.bank(4 + (c + 1) // 2, RET_DV, P, (c + 1) % 2 * RET_DV), kz[:, c * P:(c + 1) * P],
                              cols(v, c * D + h * RET_DV, RET_DV), start=True, stop=True)
                pe.matmul(K.bank(4, RET_DV), kz_meta[:, :], cols(v_meta, h * RET_DV, RET_DV, META), start=True, stop=True)\
                    .then_inc(states.h, 1)
                pe.wait_ge(*decayed(h + 1))
                pe.wait_ge(*stated(h + 1))
                for c in range(NT):
                    o = K.bank(6 + c // 2, RET_DV, P, c % 2 * RET_DV)
                    pe.matmul(o, st[:, c * P:(c + 1) * P], cols(v, c * D + h * RET_DV, RET_DV), start=True, stop=False)
                    last = pe.matmul(o, qx[:, c * P:(c + 1) * P], R[:, c * RET_DV:(c + 1) * RET_DV], start=False, stop=True)
                last.then_inc(out.h, 1)
                pe.wait_ge(*normed(h + 1))
                for e in range(2):
                    for c in range(NT):
                        last = pe.transpose(K.bank(e, P, P, c * P), yn[:, c * RET_DV + e * P:c * RET_DV + (e + 1) * P], K.ident[:, :])
                last.then_inc(turned_y.h, 1)

        @block.scalar
        def _(act):
            with act.Fori(0, H) as h:
                act.wait_ge(*turned(h + 1))
                act.wait_ge(*loaded(16 * 7))
                act.activation(kz[:, :], K.bank(3), ACT.Copy, scale=cols(zeta, h, 1))
                act.activation(kz_meta[:, :], K.bank(2, P, META, P), ACT.Copy, scale=cols(zeta, 2 * H + h, 1, META))\
                   .then_inc(scaled.h, 1)
                act.wait_ge(*own(h * own_n + 19))
                act.activation(rstd[:, :], rstd[:, :], ACT.Sqrt).then_inc(rooted.h, 1)

        @block.vector
        def _(dve):
            dve.wait_ge(*loaded(16 * 7))
            with dve.Fori(0, H) as h:
                chain = Chain(dve, own, h * own_n)
                dve.wait_ge(*swapped(h + 1))
                chain(dve.tensor_tensor(t1[:, 0:T], K.bank(0), sin[:, 0:T], ALU.mult))
                chain(dve.tensor_tensor(qs[:, :], cols(q, h * T, T), cos[:, 0:T], ALU.mult))
                chain(dve.tensor_tensor(qs[:, :], qs[:, :], t1[:, 0:T], ALU.add))
                chain(dve.tensor_tensor(t1[:, :], K.ps[:, T:2 * T + META], sin[:, :], ALU.mult))
                chain(dve.tensor_tensor(ks[:, :], cols(k, h * TM, TM), cos[:, :], ALU.mult))
                chain(dve.tensor_tensor(ks[:, :], ks[:, :], t1[:, :], ALU.add))
                chain(dve.tensor_scalar(ks[:, :], ks[:, :], RET_DK ** -0.5, None, ALU.mult))
                qx3 = qx[:, :].rearrange("p (c n) -> p c n", n=P)
                qs3 = qs[:, :].rearrange("p (c n) -> p c n", n=P)
                xi_h = cols(xi, h * P, P).unsqueeze(1).to_broadcast([P, NT, P])
                dve.tensor_tensor(qx3, qs3, xi_h, ALU.mult).then_inc(rotated.h, 1)
                dve.wait_ge(*scored(h + 1))
                decay_h = cols(decay, h * P, P).unsqueeze(1).to_broadcast([P, NT, P])
                dve.tensor_tensor(st[:, :].rearrange("p (c n) -> p c n", n=P),
                                  K.bank(0).rearrange("p (c n) -> p c n", n=P), decay_h, ALU.mult).then_inc(decayed.h, 1)
                dve.wait_ge(*states(h + 1))
                chain(dve.tensor_copy(R[:, 0:RET_DV], K.bank(4, RET_DV)))
                for c in range(1, NT):
                    ins = dve.scalar_tensor_tensor(out=R[:, c * RET_DV:(c + 1) * RET_DV], in0=R[:, (c - 1) * RET_DV:c * RET_DV],
                                                   scalar=cols(zeta, H + h, 1),
                                                   in1=K.bank(4 + c // 2, RET_DV, P, c % 2 * RET_DV), op0=ALU.mult, op1=ALU.add)
                    if c < NT - 1:
                        chain(ins)
                ins.then_inc(stated.h, 1)
                dve.wait_ge(*out(h + 1))
                for c in range(NT):
                    chain(dve.bn_stats(stats[:, 6 * c:6 * c + 6], K.bank(6 + c // 2, RET_DV, P, c % 2 * RET_DV)), c == NT - 1)
                dve.memset(stats[:, 6 * NT:6 * NT + 1], 0.0)
                for c in range(NT):
                    chain(dve.bn_aggr(mv[:, 2 * c:2 * c + 2], stats[:, 6 * c:6 * c + 6]), c == NT - 1)
                chain(dve.tensor_scalar(rstd[:, :], mv[:, 1:2 * NT:2], 1e-5, None, ALU.add))
                dve.wait_ge(*rooted(h + 1))
                chain(dve.reciprocal(rstd[:, :], rstd[:, :]))
                for c in range(NT):
                    ins = dve.tensor_scalar(yn[:, c * RET_DV:(c + 1) * RET_DV], K.bank(6 + c // 2, RET_DV, P, c % 2 * RET_DV),
                                            mv[:, 2 * c:2 * c + 1], rstd[:, c:c + 1], ALU.subtract, ALU.mult)
                ins.then_inc(normed.h, 1)
                dve.wait_ge(*turned_y(h + 1))
                for e in range(2):
                    g = cols(rg, (h * 2 + e) * T, T)
                    ins = dve.scalar_tensor_tensor(out=g, in0=K.bank(e), scalar=vector(K, "ret_gn")(h * 2 + e), in1=g,
                                                   op0=ALU.mult, op1=ALU.mult)
                ins.then_inc(gated.h, 1)


def convolve(dve, chain, acc, src, taps, bias):
    chain(dve.tensor_scalar(acc, src, taps[0], bias, ALU.mult, ALU.add))
    for s in range(1, len(taps)):
        chain(dve.scalar_tensor_tensor(out=acc[:, s:T], in0=src[:, 0:T - s], scalar=taps[s], in1=acc[:, s:T],
                                       op0=ALU.mult, op1=ALU.add))


def project_conv_t(K, plan, src, stride, dst, taps, name_w, name_b, tiles):
    nc = K.nc
    convolved, read = K.sems.take(plan.groups * 2 * taps), K.sems.take(plan.groups)
    per = 2 * taps
    with ExitStack() as ctx:
        acc = K.sb(ctx, f"conv_{nc.next_id()}", 4 * T)
        block_ = ctx.enter_context(nc.Block())

        @block_.sync
        def _(sync):
            K.stream.run(sync)

        @block_.tensor
        def _(pe):
            product_t(K, plan, src, stride, 2, [lambda k: convolved(k * per)])(pe)

        @block_.vector
        def _(dve):
            for i, k, u in steps(dve, plan.groups, WEIGHT_SLOTS):
                dve.wait_ge(*plan.done(k))
                dve.wait_ge(*read(k - 1))
                chain = Chain(dve, convolved, k * per)
                for ct in range(2):
                    t = 2 * k + ct
                    w = [vector(K, name_w)((taps - 1 - s) * tiles + t) for s in range(taps)]
                    a = (u % 2) * 2 + ct
                    convolve(dve, chain, acc[:, a * T:(a + 1) * T], K.bank(a), w, vector(K, name_b)(t))

        @block_.scalar
        def _(act):
            for i, k, u in steps(act, plan.groups, WEIGHT_SLOTS):
                act.wait_ge(*convolved((k + 1) * per))
                for ct in range(2):
                    a = (u % 2) * 2 + ct
                    last = act.activation(cols(dst, (2 * k + ct) * T, T), acc[:, a * T:(a + 1) * T], ACT.Silu)
                last.then_inc(read.h, 1)


def conv_swiglu(K, u, stride, x, up, down, name_w, name_b, gate_first):
    nc = K.nc
    taps, per = 3, 6
    convolved, silus = K.sems.take(up.groups * per), K.sems.take(up.groups)
    products, added = K.sems.take(up.groups), K.sems.take(down.groups)
    with ExitStack() as ctx:
        hidden = K.sb(ctx, f"ffn_hidden_{nc.next_id()}", KF * T)
        acc = K.sb(ctx, f"ffn_conv_{nc.next_id()}", 4 * T)
        block_ = ctx.enter_context(nc.Block())

        @block_.sync
        def _(sync):
            K.stream.run(sync)
            K.stream.run(sync)

        @block_.tensor
        def _(pe):
            product_t(K, up, u, stride, 2, [lambda k: convolved(k * per)])(pe)
            pe.wait_ge(*products(up.groups))
            product_t(K, down, hidden, T, 1, [added])(pe)

        @block_.vector
        def _(dve):
            def multiply(k, pair):
                dve.wait_ge(*silus(k + 1))
                dve.tensor_tensor(cols(hidden, k * T, T), acc[:, pair * 2 * T:(pair * 2 + 1) * T],
                                  acc[:, (pair * 2 + 1) * T:(pair * 2 + 2) * T], ALU.mult).then_inc(products.h, 1)
            for i, k, s in steps(dve, up.groups, WEIGHT_SLOTS):
                pair = s % 2
                dve.wait_ge(*up.done(k))
                dve.wait_ge(*products(k - 1))
                chain = Chain(dve, convolved, k * per)
                for ct in range(2):
                    t = k + ct * KF if gate_first else k + (1 - ct) * KF
                    w = [vector(K, name_w)((taps - 1 - n) * 2 * KF + t) for n in range(taps)]
                    a = pair * 2 + ct
                    convolve(dve, chain, acc[:, a * T:(a + 1) * T], K.bank(a), w, vector(K, name_b)(t))
                multiply(k, pair)
            for i, k, s in steps(dve, down.groups, WEIGHT_SLOTS):
                dve.wait_ge(*down.done(k))
                x_k = cols(x, k * stride, T)
                dve.tensor_tensor(x_k, x_k, K.bank(2 * (s % 2)), ALU.add).then_inc(added.h, 1)

        @block_.scalar
        def _(act):
            for i, k, s in steps(act, up.groups, WEIGHT_SLOTS):
                a = (s % 2) * 2
                act.wait_ge(*convolved((k + 1) * per))
                act.activation(acc[:, a * T:(a + 1) * T], acc[:, a * T:(a + 1) * T], ACT.Silu).then_inc(silus.h, 1)


def weigh(K, plan, src, gate, total=None):
    nc = K.nc
    weighed = K.sems.take(plan.groups)
    with ExitStack() as ctx:
        block_ = ctx.enter_context(nc.Block())

        @block_.sync
        def _(sync):
            K.stream.run(sync)

        @block_.tensor
        def _(pe):
            product_t(K, plan, src, T, 2, [weighed])(pe)

        @block_.vector
        def _(dve):
            for i, k, u in steps(dve, plan.groups, WEIGHT_SLOTS):
                dve.wait_ge(*plan.done(k))
                for ct in range(2):
                    g = cols(gate, (k * 2 + ct) * T, T)
                    last = dve.tensor_tensor(g, g, K.bank(2 * (u % 2) + ct), ALU.mult)
                last.then_inc(weighed.h, 1)
                if total is not None:
                    dve.wait_ge(*weighed(k + 1))
                    for ct in range(2):
                        a, b = cols(total, (k * 2 + ct) * T, T), cols(gate, (k * 2 + ct) * T, T)
                        dve.tensor_tensor(a, a, b, ALU.add)


GMLP_GROUPS = 8


def spatial_gate(K, v, gu, ws, ln_w, ln_b, bs):
    nc = K.nc
    G = GMLP_GROUPS
    loaded, turned_w, masked = K.sems.take(16 * 4), K.sems.take(1), K.sems.take(2)
    own_n = 13
    own, rooted, normed, mixed, gated = K.sems.take(G * own_n), K.sems.take(G), K.sems.take(G), K.sems.take(G), K.sems.take(G)
    with ExitStack() as ctx:
        w_rows, w_t = K.sb(ctx, "gmlp_w", G * P), K.sb(ctx, "gmlp_w_t", G * P)
        gain, bias, token_bias = (K.sb(ctx, f"gmlp_{n}", G * P) for n in ("gain", "bias", "token_bias"))
        vn = K.sb(ctx, "gmlp_normed", NT * P)
        stats, mv, rstd = K.sb(ctx, "gmlp_stats", 6 * NT + 2), K.sb(ctx, "gmlp_mean_var", 2 * NT), K.sb(ctx, "gmlp_rstd", NT)
        block_ = ctx.enter_context(nc.Block())

        @block_.sync
        def _(sync):
            sync.dma_start(w_rows[:, :].rearrange("t (g s) -> t g s", s=P), ws.rearrange("g t s -> t g s")).then_inc(loaded.h, 16)
            for dst, src in ((gain, ln_w), (bias, ln_b), (token_bias, bs)):
                sync.dma_start(dst[:, :], src.rearrange("g n -> (g n)").partition_broadcast(P)).then_inc(loaded.h, 16)

        @block_.tensor
        def _(pe):
            pe.wait_ge(*loaded(16 * 4))
            for g in range(G):
                last = pe.transpose(K.bank(g // 4, P, P, (g % 4) * P), w_rows[:, g * P:(g + 1) * P], K.ident[:, :])
            last.then_inc(turned_w.h, 1)
            pe.wait_ge(*masked(2))
            with pe.Fori(0, G) as g:
                pe.wait_ge(*normed(g + 1))
                pe.wait_ge(*gated(g))
                for t in range(NT):
                    last = pe.matmul(K.bank(2, P, P, t * P), vn[:, t * P:(t + 1) * P], cols(w_t, g * P, P), start=True, stop=True)
                last.then_inc(mixed.h, 1)

        @block_.scalar
        def _(act):
            with act.Fori(0, G) as g:
                act.wait_ge(*own(g * own_n + 9))
                act.activation(rstd[:, :], rstd[:, :], ACT.Sqrt).then_inc(rooted.h, 1)

        @block_.vector
        def _(dve):
            dve.wait_ge(*turned_w(1))
            dve.tensor_copy(w_t[:, :], K.ps[:, 0:G * P]).then_inc(masked.h, 1)
            dve.wait_ge(*masked(1))
            dve.memset(w_t[64:P, :].rearrange("s (g t) -> s g t", t=P)[:, :, 0:64], 0.0).then_inc(masked.h, 1)
            dve.wait_ge(*loaded(16 * 4))
            with dve.Fori(0, G) as g:
                chain = Chain(dve, own, g * own_n)
                for t in range(NT):
                    chain(dve.bn_stats(stats[:, 6 * t:6 * t + 6], cols(v, t * D + g * P, P)), t == NT - 1)
                dve.memset(stats[:, 6 * NT:6 * NT + 1], 0.0)
                for t in range(NT):
                    chain(dve.bn_aggr(mv[:, 2 * t:2 * t + 2], stats[:, 6 * t:6 * t + 6]), t == NT - 1)
                chain(dve.tensor_scalar(rstd[:, :], mv[:, 1:2 * NT:2], 1e-5, None, ALU.add), False)
                dve.wait_ge(*rooted(g + 1))
                chain(dve.reciprocal(rstd[:, :], rstd[:, :]))
                dve.wait_ge(*mixed(g))
                for t in range(NT):
                    ins = dve.tensor_scalar(vn[:, t * P:(t + 1) * P], cols(v, t * D + g * P, P), mv[:, 2 * t:2 * t + 1],
                                            rstd[:, t:t + 1], ALU.subtract, ALU.mult)
                chain(ins)
                vn3 = vn[:, :].rearrange("p (t n) -> p t n", n=P)
                chain(dve.tensor_tensor(vn3, vn3, cols(gain, g * P, P).unsqueeze(1).to_broadcast([P, NT, P]), ALU.mult))
                dve.tensor_tensor(vn3, vn3, cols(bias, g * P, P).unsqueeze(1).to_broadcast([P, NT, P]), ALU.add).then_inc(normed.h, 1)
                dve.wait_ge(*mixed(g + 1))
                chain(dve.tensor_tensor(vn3, K.bank(2).rearrange("p (t n) -> p t n", n=P),
                                        cols(token_bias, g * P, P).unsqueeze(1).to_broadcast([P, NT, P]), ALU.add))
                gu_g = cols(gu, g * T, T)
                dve.tensor_tensor(gu_g, gu_g, vn[:, :], ALU.mult).then_inc(gated.h, 1)


SSM_HEADS = 32
SSM_GROUPS = 4
SSM_PAIRS = SSM_HEADS // 2


def ssm_times(K, plan, u, dt_bias, a_log, acum, acum_n, dt_n, end_n, chunk_starts):
    nc = K.nc
    H = SSM_HEADS
    loaded, own, act_own, turned = K.sems.take(16 * 3), K.sems.take(12), K.sems.take(4), K.sems.take(1)
    with ExitStack() as ctx:
        z, m, dt, starts = (K.sb(ctx, f"ssm_{n}", T, H) for n in ("dt_raw", "dt_max", "dt", "starts"))
        small = K.sb(ctx, "ssm_head_values", 4, H)
        ends = K.sb(ctx, "ssm_chunk_ends", NT * P, H)
        block_ = ctx.enter_context(nc.Block())

        @block_.sync
        def _(sync):
            sync.dma_start(small[:, 0:1], dt_bias.rearrange("(h a) -> h a", a=1)).then_inc(loaded.h, 16)
            sync.dma_start(small[:, 1:2], a_log.rearrange("(h a) -> h a", a=1)).then_inc(loaded.h, 16)
            sync.dma_start(starts[:, :], chunk_starts[0:H, :]).then_inc(loaded.h, 16)
            K.stream.run(sync)

        @block_.tensor
        def _(pe):
            product_t(K, plan, u, TM, 1, [], False, H)(pe)
            pe.wait_ge(*own(10))
            for c in range(NT):
                tok = slice(c * P, (c + 1) * P)
                pe.transpose(K.bank(1, H, P, c * H), acum[:, tok], K.ident[0:H, 0:H])
                pe.transpose(K.bank(2, H, P, c * H), dt[:, tok], K.ident[0:H, 0:H])
                last = pe.matmul(K.bank(3, H, P, c * H), ends[:, tok], K.ident[0:H, 0:H], start=True, stop=True)
            last.then_inc(turned.h, 1)

        @block_.scalar
        def _(act):
            act.wait_ge(*loaded(16 * 3))
            act.activation(small[:, 2:3], small[:, 1:2], ACT.Exp).then_inc(act_own.h, 1)
            act.wait_ge(*own(3))
            act.activation(dt[:, :], dt[:, :], ACT.Exp).then_inc(act_own.h, 1)
            act.wait_ge(*act_own(2))
            act.activation(dt[:, :], dt[:, :], ACT.Ln, bias=1.0).then_inc(act_own.h, 1)
            act.wait_ge(*own(12))
            act.activation(end_n[:, :], end_n[:, :], ACT.Exp).then_inc(act_own.h, 1)

        @block_.vector
        def _(dve):
            chain = Chain(dve, own)
            dve.wait_ge(*loaded(16 * 3))
            dve.wait_ge(*plan.done(0))
            chain(dve.tensor_scalar(z[:, :], K.bank(0, rows=H), small[:, 0:1], None, ALU.add))
            chain(dve.tensor_scalar(m[:, :], z[:, :], 0.0, None, ALU.max))
            chain(dve.scalar_tensor_tensor(out=dt[:, :], in0=m[:, :], scalar=-2.0, in1=z[:, :], op0=ALU.mult, op1=ALU.add))
            dve.wait_ge(*act_own(3))
            chain(dve.tensor_tensor(dt[:, :], dt[:, :], m[:, :], ALU.add))
            chain(dve.tensor_scalar(z[:, :], dt[:, :], small[:, 2:3], -1.0, ALU.mult, ALU.mult))
            chain(dve.tensor_tensor_scan(acum[:, :], starts[:, :], z[:, :], 0.0, ALU.mult, ALU.add))
            for c in range(NT):
                chain(dve.tensor_scalar(ends[:, c * P:(c + 1) * P], K.ones[0:H, :], acum[:, (c + 1) * P - 1:(c + 1) * P],
                                        None, ALU.mult))
            dve.wait_ge(*turned(1))
            chain(dve.tensor_copy(acum_n[:, :], K.bank(1, NT * H)))
            dve.tensor_copy(dt_n[:, :], K.bank(2, NT * H))
            chain(dve.tensor_tensor(end_n[:, :], K.bank(3, NT * H), acum_n[:, :], ALU.subtract))
            dve.wait_ge(*act_own(4))
            dve.tensor_tensor(end_n[:, :], end_n[:, :], dt_n[:, :], ALU.mult)


def ssm_groups(K, bt, ct, bn, cbm, mask):
    nc = K.nc
    G = SSM_GROUPS
    turned, copied, masked, loaded = (K.sems.take(n) for n in (G, G, G, 16))
    with ExitStack() as ctx:
        m = K.sb(ctx, "ssm_causal", P)
        block_ = ctx.enter_context(nc.Block())

        @block_.sync
        def _(sync):
            sync.dma_start(m[:, :], mask).then_inc(loaded.h, 16)

        @block_.tensor
        def _(pe):
            for g in range(G):
                pe.wait_ge(*copied(g - 1))
                pe.wait_ge(*masked(g - 1))
                for c in range(NT):
                    tok = slice(g * T + c * P, g * T + (c + 1) * P)
                    pe.matmul(K.bank(2 + g % 2, P, P, c * P), bt[:, tok], ct[:, tok], start=True, stop=True)
                    last = pe.transpose(K.bank(g % 2, P, P, c * P), bt[:, tok], K.ident[:, :])
                last.then_inc(turned.h, 1)

        @block_.scalar
        def _(act):
            for g in range(G):
                act.wait_ge(*turned(g + 1))
                act.activation(bn[:, g * T:(g + 1) * T], K.bank(g % 2), ACT.Copy).then_inc(copied.h, 1)

        @block_.vector
        def _(dve):
            dve.wait_ge(*loaded(16))
            for g in range(G):
                dve.wait_ge(*turned(g + 1))
                dve.tensor_tensor(cbm[:, g * T:(g + 1) * T].rearrange("p (c n) -> p c n", n=P),
                                  K.bank(2 + g % 2).rearrange("p (c n) -> p c n", n=P),
                                  m[:, :].unsqueeze(1).to_broadcast([P, NT, P]), ALU.mult).then_inc(masked.h, 1)


def ssm_scan(K, xs, z, bn, cbm, ct, acum, acum_n, dt_n, end_n, d_skip):
    nc = K.nc
    H, NP = SSM_HEADS, SSM_PAIRS
    own_n = 20
    own = K.sems.take(NP * own_n)
    staged, b_staged, picked, spread, turned, states, out, done = (K.sems.take(n) for n in (NP, NP, NP, NP, NP, NP, NP, NP))
    exps, decays = K.sems.take(NP), K.sems.take(NP)
    loaded = K.sems.take(16)
    with ExitStack() as ctx:
        x = K.sb(ctx, "ssm_x_pair", T)
        b = K.sb(ctx, "ssm_b_group", T)
        row = K.sb(ctx, "ssm_sum_rows", 2 * T, H)
        xd, xe = K.sb(ctx, "ssm_x_dt", T), K.sb(ctx, "ssm_x_end", T)
        seg, E, ce = K.sb(ctx, "ssm_decay", 2 * T), K.sb(ctx, "ssm_exp_sum", 2 * T), K.sb(ctx, "ssm_c_decay", 2 * T)
        R = K.sb(ctx, "ssm_state", (NT - 1) * P)
        d, d_heads = K.sb(ctx, "ssm_skip", NP), K.sb(ctx, "ssm_skip_heads", H)
        y = K.sb(ctx, "ssm_y_pair", T)
        block_ = ctx.enter_context(nc.Block())

        @block_.sync
        def _(sync):
            sync.dma_start(d_heads[:, :], d_skip.partition_broadcast(P)).then_inc(loaded.h, 16)

        @block_.gpsimd
        def _(pool):
            with pool.Fori(0, SSM_GROUPS) as g:
                with pool.Fori(0, 4) as jj:
                    j = g * 4 + jj
                    pool.wait_ge(*states(j))
                    pool.tensor_copy(b[:, :], cols(bn, g * T, T)).then_inc(b_staged.h, 1)

        @block_.tensor
        def _(pe):
            with pe.Fori(0, NP) as j:
                pe.wait_ge(*picked(j + 1))
                pe.wait_ge(*exps(j))
                for h in range(2):
                    last = pe.matmul(K.bank(h), K.ones[0:H, :], row[:, h * T:(h + 1) * T], start=True, stop=True)
                last.then_inc(spread.h, 1)
                pe.wait_ge(*staged(j + 1))
                for c in range(NT):
                    last = pe.transpose(K.bank(2, P, P, c * P), x[:, c * P:(c + 1) * P], K.ident[:, :])
                last.then_inc(turned.h, 1)
                pe.wait_ge(*own(j * own_n + 2))
                pe.wait_ge(*b_staged(j + 1))
                for c in range(NT - 1):
                    last = pe.matmul(K.bank(3, P, P, c * P), b[:, c * P:(c + 1) * P], xe[:, c * P:(c + 1) * P], start=True, stop=True)
                last.then_inc(states.h, 1)
                pe.wait_ge(*done(j))
                pe.wait_ge(*own(j * own_n + 19))
                for h in range(2):
                    rows = slice(64 * h, 64 * h + 64)
                    for c in range(NT):
                        o = K.ps[rows, 4 * T + c * P:4 * T + (c + 1) * P]
                        last = pe.matmul(o, xd[:, c * P + 64 * h:c * P + 64 * h + 64], seg[:, h * T + c * P:h * T + (c + 1) * P],
                                         start=True, stop=c == 0)
                        if c:
                            last = pe.matmul(o, R[:, (c - 1) * P + 64 * h:(c - 1) * P + 64 * h + 64],
                                             ce[:, h * T + c * P:h * T + (c + 1) * P], start=False, stop=True)
                last.then_inc(out.h, 1)

        @block_.scalar
        def _(act):
            with act.Fori(0, NP) as j:
                act.wait_ge(*out(j))
                act.wait_ge(*done(j))
                act.activation(x[:, :], cols(xs, j * T, T), ACT.Copy).then_inc(staged.h, 1)
                act.wait_ge(*spread(j + 1))
                act.activation(E[:, :], K.ps[:, 0:2 * T], ACT.Exp).then_inc(exps.h, 1)
                act.wait_ge(*own(j * own_n + 10))
                act.activation(seg[:, :], seg[:, :], ACT.Exp).then_inc(decays.h, 1)

        @block_.vector
        def _(dve):
            dve.wait_ge(*loaded(16))
            for a in range(2):
                dve.tensor_copy(d[64 * a:64 * a + 64, :], d_heads[64 * a:64 * a + 64, a:H:2])
            with dve.Fori(0, SSM_GROUPS) as g:
                with dve.Fori(0, 4) as jj:
                    j = g * 4 + jj
                    chain = Chain(dve, own, j * own_n)
                    dve.wait_ge(*out(j))
                    for h in range(2):
                        last = dve.tensor_scalar(row[:, h * T:(h + 1) * T], acum[:, :], cols(K.ident, j * 2 + h, 1, H), None, ALU.mult)
                    last.then_inc(picked.h, 1)
                    dve.wait_ge(*turned(j + 1))
                    for dst, src in ((xd, dt_n), (xe, end_n)):
                        by_head = src[:, :].rearrange("p (c h) -> p c h", h=H)[:, :, bass.ds(j * 2, 2)].unsqueeze(3).to_broadcast([P, NT, 2, 64])
                        chain(dve.tensor_tensor(dst[:, :].rearrange("p (c h n) -> p c h n", h=2, n=64),
                                                K.bank(2).rearrange("p (c h n) -> p c h n", h=2, n=64), by_head, ALU.mult), False)
                    dve.wait_ge(*exps(j + 1))
                    for h in range(2):
                        for c in range(NT):
                            chain(dve.tensor_scalar(seg[:, h * T + c * P:h * T + (c + 1) * P], K.bank(h, P, P, c * P),
                                                    cols(acum_n, c * H + j * 2 + h, 1), 0.0, ALU.subtract, ALU.min), False)
                    for h in range(2):
                        chain(dve.tensor_tensor(ce[:, h * T:(h + 1) * T], E[:, h * T:(h + 1) * T], cols(ct, g * T, T), ALU.mult), False)
                    dve.wait_ge(*states(j + 1))
                    chain(dve.tensor_copy(R[:, 0:P], K.bank(3, P)))
                    for c in range(1, NT - 1):
                        for h in range(2):
                            a, b_ = c * P + 64 * h, (c - 1) * P + 64 * h
                            chain(dve.scalar_tensor_tensor(out=R[:, a:a + 64], in0=R[:, b_:b_ + 64],
                                                           scalar=E[:, h * T + (c + 1) * P - 1:h * T + (c + 1) * P],
                                                           in1=K.bank(3, 64, P, a), op0=ALU.mult, op1=ALU.add), h == 1)
                    dve.wait_ge(*decays(j + 1))
                    for h in range(2):
                        chain(dve.tensor_tensor(seg[:, h * T:(h + 1) * T], seg[:, h * T:(h + 1) * T], cols(cbm, g * T, T), ALU.mult), False)
                    dve.wait_ge(*out(j + 1))
                    chain(dve.scalar_tensor_tensor(out=y[:, :], in0=x[:, :], scalar=cols(d, j, 1), in1=K.bank(4), op0=ALU.mult, op1=ALU.add))
                    z_j = cols(z, j * T, T)
                    dve.tensor_tensor(z_j, z_j, y[:, :], ALU.mult).then_inc(done.h, 1)


def group_norm_t(K, buf, groups, tiles, gain, eps):
    nc = K.nc
    n = groups * tiles
    squared, shifted, rooted = K.sems.take(n), K.sems.take(groups), K.sems.take(groups)
    own = K.sems.take(groups)
    with ExitStack() as ctx:
        sq = K.sb(ctx, f"group_squares_{nc.next_id()}", 2 * T)
        r = K.sb(ctx, f"group_scale_{nc.next_id()}", groups * T)
        block_ = ctx.enter_context(nc.Block())
        added = K.sems.take(n)

        @block_.scalar
        def _(act):
            for t in range(n):
                act.wait_ge(*added(t - 1))
                act.activation(sq[:, (t % 2) * T:(t % 2 + 1) * T], buf[:, t * T:(t + 1) * T], ACT.Square).then_inc(squared.h, 1)
            for g in range(groups):
                act.wait_ge(*shifted(g + 1))
                act.activation(r[:, g * T:(g + 1) * T], r[:, g * T:(g + 1) * T], ACT.Sqrt).then_inc(rooted.h, 1)

        @block_.tensor
        def _(pe):
            for t in range(n):
                g = t // tiles
                pe.wait_ge(*squared(t + 1))
                if t % tiles == 0:
                    pe.wait_ge(*shifted(g - 1))
                pe.matmul(K.bank(g % 2), K.ones[:, :], sq[:, (t % 2) * T:(t % 2 + 1) * T], start=t % tiles == 0,
                          stop=t % tiles == tiles - 1).then_inc(added.h, 1)

        @block_.vector
        def _(dve):
            for g in range(groups):
                dve.wait_ge(*added((g + 1) * tiles))
                dve.tensor_scalar(r[:, g * T:(g + 1) * T], K.bank(g % 2), 1.0 / (tiles * P), eps, ALU.mult, ALU.add)\
                   .then_inc(shifted.h, 1)
            for g in range(groups):
                dve.wait_ge(*rooted(g + 1))
                dve.reciprocal(r[:, g * T:(g + 1) * T], r[:, g * T:(g + 1) * T]).then_inc(own.h, 1)
                dve.wait_ge(*own(g + 1))
                for t in range(g * tiles, (g + 1) * tiles):
                    b = buf[:, t * T:(t + 1) * T]
                    dve.scalar_tensor_tensor(out=b, in0=b, scalar=gain(t), in1=r[:, g * T:(g + 1) * T], op0=ALU.mult, op1=ALU.mult)


def second_block(K, d, tables, X, U, plans):
    V = lambda name: vector(K, name)
    H = SSM_HEADS
    rmsnorm_t(K, X, U, TM, V("mix_norm_w_2"), 1e-5)
    with ExitStack() as mix:
        merged = K.sb(mix, "merged", KD * T)
        project_t(K, plans["gate_a2"], U, TM, merged, T, func=ACT.Sigmoid, bias=V("gate_bias_2"))
        with ExitStack() as gmlp:
            gu, gv = K.sb(gmlp, "gmlp_u", KD * T), K.sb(gmlp, "gmlp_v", NT * D)
            project_t(K, plans["gmlp_u"], U, TM, gu, T, func=ACT.Gelu_apprx_tanh)
            project_n(K, plans["gmlp_v"], U, TM, gv, 256, D, func=ACT.Gelu_apprx_tanh)
            spatial_gate(K, gv, gu, d["gmlp_ws_2"][0], d["gmlp_ln_w_2"][0], d["gmlp_ln_b_2"][0], d["gmlp_bs_2"][0])
            weigh(K, plans["w_proj_a"], gu, merged)
        z = K.sb(mix, "ssm_z", 2 * KD * T)
        with ExitStack() as ssm:
            xbc = K.sb(ssm, "ssm_xbc", 3 * KD * T)
            acum = K.sb(ssm, "ssm_sums", T, H)
            acum_n, dt_n, end_n = (K.sb(ssm, f"ssm_{n}_n", NT * H) for n in ("sums", "dt", "end"))
            project_conv_t(K, plans["xbc"], U, TM, xbc, 4, "ssm_conv_w_2", "ssm_conv_b_2", 3 * KD)
            ssm_times(K, plans["dt"], U, d["ssm_dt_bias_2"][0], d["ssm_a_log_2"][0], acum, acum_n, dt_n, end_n, tables["starts"])
            project_t(K, plans["ssm_z"], U, TM, z, T, func=ACT.Silu)
            bt, ct = xbc[:, 16 * T:20 * T], xbc[:, 20 * T:24 * T]
            cbm = K.sb(ssm, "ssm_cb", 4 * T)
            bn = bt
            ssm_groups(K, bt, ct, bn, cbm, tables["causal01"])
            ssm_scan(K, xbc, z, bn, cbm, ct, acum, acum_n, dt_n, end_n, d["ssm_d_2"][0])
        group_norm_t(K, z, SSM_GROUPS, 4, V("ssm_norm_w_2"), 1e-5)
        gate_b = K.sb(mix, "gate_b2", KD * T)
        project_t(K, plans["gate_b2"], U, TM, gate_b, T, func=ACT.Sigmoid, bias=lambda t: V("gate_bias_2")(t + KD))
        weigh_wide(K, plans["w_proj_b"], z, gate_b, merged)
        add_product(K, plans["w_out2"], merged, T, X, TM)
    rmsnorm_t(K, X, U, TM, V("ffn_norm_w_2"), 1e-5)
    conv_swiglu(K, U, TM, X, plans["ffn_up2"], plans["ffn_down2"], "ffn_conv_w_2", "ffn_conv_b_2", True)
    rmsnorm_t(K, X, U, TM, V("final_norm_w_2"), 1e-5)


def weigh_wide(K, plan, src, gate, total):
    nc = K.nc
    weighed = K.sems.take(plan.groups)
    with ExitStack() as ctx:
        block_ = ctx.enter_context(nc.Block())

        @block_.sync
        def _(sync):
            K.stream.run(sync)

        @block_.tensor
        def _(pe):
            product_t(K, plan, src, T, 2, [weighed])(pe)

        @block_.vector
        def _(dve):
            for g in range(plan.groups):
                dve.wait_ge(*plan.done(g))
                a = slice(2 * g * T, 2 * (g + 1) * T)
                dve.tensor_tensor(gate[:, a], gate[:, a], K.ps[:, 2 * (g % 2) * T:2 * (g % 2 + 1) * T], ALU.mult).then_inc(weighed.h, 1)
                dve.wait_ge(*weighed(g + 1))
                dve.tensor_tensor(total[:, a], total[:, a], gate[:, a], ALU.add)


NSA_HEADS = 8
NSA_GROUPS = 2
CMP_BLOCK = 32
CMP_STRIDE = 16
CMP = (T - CMP_BLOCK) // CMP_STRIDE + 1
BUCKETS = 32
BIAS_W = 3 * P + T
HEAD = 64


def distance_bias(K, rel_bias, onehot, flip, scratch, table):
    nc = K.nc
    H, L = NSA_HEADS, 2 * T
    N = H * BIAS_W // T
    filled, loaded, made, copied, stored, landed, flipped, placed = (K.sems.take(n) for n in (1, 48, 1, 1, 16, 16, N, N))
    with ExitStack() as ctx:
        b = K.sb(ctx, "nsa_bucket_bias", H, BUCKETS + 1)
        hot = K.sb(ctx, "nsa_onehot", L, BUCKETS + 1)
        line = K.sb(ctx, "nsa_distance_bias", L, H)
        reverse, order = K.sb(ctx, "nsa_bias_reversed", H * BIAS_W), K.sb(ctx, "partition_flip", P)
        block_ = ctx.enter_context(nc.Block())

        @block_.sync
        def _(sync):
            sync.wait_ge(*filled(1))
            sync.dma_start(b[0:BUCKETS, :], rel_bias).then_inc(loaded.h, 16)
            sync.dma_start(hot[:, :], onehot).then_inc(loaded.h, 16)
            sync.dma_start(order[:, :], flip).then_inc(loaded.h, 16)
            sync.wait_ge(*copied(1))
            sync.dma_start(scratch, line[:, :]).then_inc(stored.h, 16)
            sync.wait_ge(*stored(16))
            sync.dma_start(reverse[:, :].rearrange("p (h m) -> p h m", m=BIAS_W),
                           bass.AP(scratch.tensor, 0, [[1, P], [L, H], [1, BIAS_W]])).then_inc(landed.h, 16)

        @block_.tensor
        def _(pe):
            pe.wait_ge(*loaded(48))
            for half in range(2):
                last = pe.matmul(K.bank(half, rows=H), b[:, :], hot[:, half * T:(half + 1) * T], start=True, stop=True)
            last.then_inc(made.h, 1)
            pe.wait_ge(*landed(16))
            for n in range(N):
                pe.wait_ge(*placed(n - 1))
                pe.matmul(K.bank(2 + n % 2), order[:, :], reverse[:, n * T:(n + 1) * T], start=True, stop=True).then_inc(flipped.h, 1)

        @block_.vector
        def _(dve):
            dve.memset(b[:, :], NEG).then_inc(filled.h, 1)
            dve.wait_ge(*made(1))
            dve.tensor_copy(line[:, :], K.ps[0:H, 0:L]).then_inc(copied.h, 1)
            for n in range(N):
                dve.wait_ge(*flipped(n + 1))
                dve.tensor_copy(table[:, n * T:(n + 1) * T], K.bank(2 + n % 2)).then_inc(placed.h, 1)


def compress(K, kv, kc, vc, pos, w1, w2, b2, eps, gain):
    nc = K.nc
    G = NSA_GROUPS
    M = P
    loaded = K.sems.take(16 * 12)
    turned, placed, posted, hidden, active, second, biased, squared, summed, rooted = (
        K.sems.take(n) for n in (1, 1, 2, 2, 2, 1, 1, 1, 1, 1))
    own = K.sems.take(2)
    with ExitStack() as ctx:
        w1s = K.sb(ctx, "cmp_w1", 2 * CMP_BLOCK * M)
        w2s = K.sb(ctx, "cmp_w2", 2 * P)
        rows, post = K.sb(ctx, "cmp_pos_rows", 2 * P, CMP_BLOCK), K.sb(ctx, "cmp_pos", 2 * CMP_BLOCK)
        blk = K.sb(ctx, "cmp_blocks", 2 * CMP_BLOCK * CMP)
        hid = K.sb(ctx, "cmp_hidden", 4 * CMP)
        bv = K.sb(ctx, "cmp_bias_v", HEAD, CMP)
        sq, r = K.sb(ctx, "cmp_squares", G * CMP), K.sb(ctx, "cmp_scale", G * CMP)
        block_ = ctx.enter_context(nc.Block())

        @block_.sync
        def _(sync):
            for i in range(2):
                w = w1[i].rearrange("(j d) m -> d j m", d=HEAD)
                for half in range(2):
                    sync.dma_start(w1s[64 * half:64 * half + 64, i * CMP_BLOCK * M:(i + 1) * CMP_BLOCK * M]
                                   .rearrange("d (j m) -> d j m", m=M), w).then_inc(loaded.h, 16)
            for i in range(2):
                for half in range(2):
                    sync.dma_start(rows[:, i * P + half * HEAD:i * P + (half + 1) * HEAD], pos[i]).then_inc(loaded.h, 16)
            for half in range(2):
                sync.dma_start(w2s[:, half * HEAD:(half + 1) * HEAD], w2[0]).then_inc(loaded.h, 16)
            sync.dma_start(w2s[:, P:P + HEAD], w2[1]).then_inc(loaded.h, 16)
            sync.dma_start(bv[:, :], b2[1, 0:HEAD].partition_broadcast(CMP)).then_inc(loaded.h, 16)

        @block_.tensor
        def _(pe):
            pe.wait_ge(*loaded(16 * 12))
            for i in range(2):
                last = pe.transpose(K.bank(0, CMP_BLOCK, P, i * CMP_BLOCK), rows[:, i * P:(i + 1) * P], K.ident[0:CMP_BLOCK, 0:CMP_BLOCK])
            last.then_inc(turned.h, 1)
            for i in range(2):
                pe.wait_ge(*posted(i + 1))
                for g in range(G):
                    part = slice(64 * g, 64 * g + 64)
                    for j in range(CMP_BLOCK):
                        c = i * CMP_BLOCK + j
                        last = pe.matmul(K.bank(1 + i + 4 * g, CMP), w1s[part, c * M:(c + 1) * M],
                                         blk[part, c * CMP:(c + 1) * CMP], start=j == 0, stop=j == CMP_BLOCK - 1)
                last.then_inc(hidden.h, 1)
            pe.wait_ge(*active(2))
            for g in range(G):
                pe.matmul(K.bank(3, CMP, P, g * CMP), w2s[:, 0:P], hid[:, g * CMP:(g + 1) * CMP], start=True, stop=True)
                last = pe.matmul(K.bank(4, HEAD, CMP, g * HEAD), hid[:, (2 + g) * CMP:(3 + g) * CMP], w2s[:, P:P + HEAD],
                                 start=True, stop=True)
            last.then_inc(second.h, 1)
            pe.wait_ge(*squared(1))
            pe.matmul(K.bank(7, G * CMP), K.head_ones[:, :], sq[:, :], start=True, stop=True).then_inc(summed.h, 1)

        @block_.scalar
        def _(act):
            for i in range(2):
                act.wait_ge(*hidden(i + 1))
                for g in range(G):
                    last = act.activation(hid[:, (2 * i + g) * CMP:(2 * i + g + 1) * CMP], K.bank(1 + i + 4 * g, CMP),
                                          ACT.Gelu_apprx_tanh, bias=vector(K, "cmp_b1_3")(i))
                last.then_inc(active.h, 1)
            act.wait_ge(*own(1))
            act.activation(sq[:, :], kc[:, :], ACT.Square).then_inc(squared.h, 1)
            act.wait_ge(*biased(1))
            act.activation(r[:, :], r[:, :], ACT.Sqrt).then_inc(rooted.h, 1)

        @block_.vector
        def _(dve):
            dve.wait_ge(*turned(1))
            dve.tensor_copy(post[:, :], K.bank(0, 2 * CMP_BLOCK)).then_inc(placed.h, 1)
            dve.wait_ge(*placed(1))
            for i in range(2):
                by_stride = kv[:, i * T:(i + 1) * T].rearrange("p (c b) -> p b c", b=CMP_STRIDE)
                for a in range(CMP_BLOCK // CMP_STRIDE):
                    j0 = i * CMP_BLOCK + a * CMP_STRIDE
                    last = dve.tensor_tensor(
                        blk[:, j0 * CMP:(j0 + CMP_STRIDE) * CMP].rearrange("p (b c) -> p b c", c=CMP), by_stride[:, :, a:a + CMP],
                        post[:, j0:j0 + CMP_STRIDE].unsqueeze(2).to_broadcast([P, CMP_STRIDE, CMP]), ALU.add)
                last.then_inc(posted.h, 1)
            dve.wait_ge(*second(1))
            dve.tensor_scalar(kc[:, :], K.bank(3, G * CMP), vector(K, "cmp_b2_3")(0), None, ALU.add).then_inc(own.h, 1)
            for g in range(G):
                dve.tensor_tensor(vc[:, g * HEAD:(g + 1) * HEAD], K.bank(4, HEAD, CMP, g * HEAD), bv[:, :], ALU.add)
            dve.wait_ge(*summed(1))
            dve.tensor_scalar(r[:, :], K.bank(7, G * CMP), 1.0 / HEAD, eps, ALU.mult, ALU.add).then_inc(biased.h, 1)
            dve.wait_ge(*rooted(1))
            dve.reciprocal(r[:, :], r[:, :]).then_inc(own.h, 1)
            dve.wait_ge(*own(2))
            dve.scalar_tensor_tensor(out=kc[:, :], in0=kc[:, :], scalar=gain, in1=r[:, :], op0=ALU.mult, op1=ALU.mult)


def nsa_attention(K, q, k, v, kc, vc, gates, bias, y):
    nc = K.nc
    PAIRS = NSA_HEADS // 2
    S = [(h, i, br) for h in range(2) for i in range(NT) for br in range(3)]
    n = len(S)
    q_staged, k_staged = K.sems.take(PAIRS), K.sems.take(PAIRS)
    scored, probs, turned, turned_copied, weighed = (K.sems.take(PAIRS * n) for _ in range(5))
    score_steps, out_steps = K.sems.take(PAIRS * n * 2), K.sems.take(PAIRS * n * 3)
    with ExitStack() as ctx:
        qs = K.sb(ctx, "nsa_q_pair", T)
        ks = [K.sb(ctx, "nsa_k_selected", T), K.sb(ctx, "nsa_k_window", T)]
        kcs, vcs = K.sb(ctx, "nsa_k_group_cmp", CMP), K.sb(ctx, "nsa_v_group_cmp", HEAD, CMP)
        L = [K.sb(ctx, f"nsa_scores_{a}", T) for a in range(2)]
        pt = [K.sb(ctx, f"nsa_probs_t_{a}", T) for a in range(2)]
        stat = [K.sb(ctx, f"nsa_stat_{a}", 4) for a in range(2)]
        acc = K.sb(ctx, "nsa_out_sum", HEAD)
        block_ = ctx.enter_context(nc.Block())
        def width(s):
            _, i, br = S[s]
            return (i + 1) * P if br else CMP

        @block_.gpsimd
        def _(pool):
            with pool.Fori(0, NSA_GROUPS) as g:
                with pool.Fori(0, 2) as jj:
                    j = g * 2 + jj
                    pool.wait_ge(*weighed(j * n))
                    pool.tensor_copy(ks[0][:, :], cols(k, g * T, T))
                    pool.tensor_copy(ks[1][:, :], cols(k, g * T + 2 * T, T))
                    pool.tensor_copy(kcs[:, :], cols(kc, g * CMP, CMP))
                    pool.tensor_copy(vcs[:, :], cols(vc, g * HEAD, HEAD, CMP)).then_inc(k_staged.h, 1)

        @block_.tensor
        def _(pe):
            with pe.Fori(0, NSA_GROUPS) as g:
                with pe.Fori(0, 2) as jj:
                    j = g * 2 + jj
                    pe.wait_ge(*q_staged(j + 1))
                    pe.wait_ge(*k_staged(j + 1))
                    for s in range(n + 2):
                        if s < n:
                            h, i, br = S[s]
                            pe.wait_ge(*score_steps((j * n + s - 2) * 2 + 1))
                            rows = slice(64 * h, 64 * h + 64)
                            keys = ks[br - 1][rows, 0:width(s)] if br else kcs[rows, :]
                            pe.matmul(K.bank(s % 2, width(s)), qs[rows, i * P:(i + 1) * P], keys, start=True, stop=True)\
                                .then_inc(scored.h, 1)
                        if 1 <= s <= n:
                            _, i, br = S[s - 1]
                            b = (s - 1) % 2
                            pe.wait_ge(*probs(j * n + s))
                            pe.wait_ge(*turned_copied(j * n + s - 2))
                            if br:
                                for t in range(i + 1):
                                    last = pe.transpose(K.bank(2 + b, P, P, t * P), L[b][:, t * P:(t + 1) * P], K.ident[:, :])
                            else:
                                last = pe.transpose(K.bank(2 + b, P, CMP), L[b][:, 0:CMP], K.ident[:, :])
                            last.then_inc(turned.h, 1)
                        if s >= 2:
                            h, i, br = S[s - 2]
                            b = (s - 2) % 2
                            pe.wait_ge(*turned_copied(j * n + s - 1))
                            pe.wait_ge(*out_steps((j * n + s - 3) * 3))
                            o = K.bank(4 + b, HEAD)
                            if br:
                                for t in range(i + 1):
                                    last = pe.matmul(o, pt[b][:, t * P:(t + 1) * P],
                                                     cols(v, t * 2 * P + (br - 1) * P + g * HEAD, HEAD), start=t == 0, stop=t == i)
                            else:
                                last = pe.matmul(o, pt[b][0:CMP, 0:P], vcs[:, :], start=True, stop=True)
                            last.then_inc(weighed.h, 1)

        @block_.vector
        def _(dve):
            with dve.Fori(0, PAIRS) as j:
                for s in range(n + 2):
                    if s < n:
                        h, i, br = S[s]
                        b, w = s % 2, width(s)
                        at = (j * 2 + h) * BIAS_W
                        if br:
                            near = cols(bias, at + 3 * P - i * P, w)
                        else:
                            first = at + 3 * P - i * P + CMP_BLOCK - 1
                            near = bias[:, bass.ds(first, CMP, step=CMP_STRIDE)]
                        chain = Chain(dve, score_steps, (j * n + s) * 2)
                        dve.wait_ge(*scored(j * n + s + 1))
                        dve.wait_ge(*turned(j * n + s - 1))
                        chain(dve.scalar_tensor_tensor(out=L[b][:, 0:w], in0=K.bank(s % 2, w), scalar=HEAD ** -0.5, in1=near,
                                                       op0=ALU.mult, op1=ALU.add))
                        chain(dve.tensor_reduce(stat[b][:, 0:1], L[b][:, 0:w], AX.X, ALU.max, negate=True), False)
                    if s >= 2:
                        h, i, br = S[s - 2]
                        b = (s - 2) % 2
                        chain = Chain(dve, out_steps, (j * n + s - 2) * 3)
                        dve.wait_ge(*weighed(j * n + s - 1))
                        chain(dve.reciprocal(stat[b][:, 2:3], stat[b][:, 1:2]))
                        gate = cols(gates, i * 3 * NSA_HEADS + (j * 2 + h) * 3 + br, 1)
                        chain(dve.tensor_tensor(stat[b][:, 3:4], stat[b][:, 2:3], gate, ALU.mult))
                        o, scale = K.bank(4 + b, HEAD), stat[b][:, 3:4]
                        if br == 0:
                            chain(dve.tensor_scalar(acc[:, :], o, scale, None, ALU.mult))
                        else:
                            dst = acc[:, :] if br == 1 else cols(y, i * T + (j * 2 + h) * HEAD, HEAD)
                            chain(dve.scalar_tensor_tensor(out=dst, in0=o, scalar=scale, in1=acc[:, :], op0=ALU.mult, op1=ALU.add))

        @block_.scalar
        def _(act):
            with act.Fori(0, PAIRS) as j:
                act.wait_ge(*scored(j * n))
                act.activation(qs[:, :], cols(q, j * T, T), ACT.Copy).then_inc(q_staged.h, 1)
                for s in range(n + 1):
                    if s < n:
                        b, w = s % 2, width(s)
                        act.wait_ge(*score_steps((j * n + s) * 2 + 2))
                        act.wait_ge(*out_steps((j * n + s - 1) * 3))
                        act.activation(L[b][:, 0:w], L[b][:, 0:w], ACT.Exp, bias=stat[b][:, 0:1],
                                       accum_out=stat[b][:, 1:2]).then_inc(probs.h, 1)
                    if s >= 1:
                        b, (_, i, br) = (s - 1) % 2, S[s - 1]
                        act.wait_ge(*turned(j * n + s))
                        act.wait_ge(*weighed(j * n + s - 2))
                        if br:
                            last = act.activation(pt[b][:, 0:(i + 1) * P], K.bank(2 + b, (i + 1) * P), ACT.Copy)
                        else:
                            last = act.activation(pt[b][0:CMP, 0:P], K.bank(2 + b, P, CMP), ACT.Copy)
                        last.then_inc(turned_copied.h, 1)


RWKV_TILES = 4
CHUNK = 64
E_HALF = float(np.exp(-0.5))


def rwkv_features(K, d, starts64, rw, A, R, B, C, ends, gate, bonus):
    nc = K.nc
    N = RWKV_TILES
    loaded = K.sems.take(16 * 4)
    lora, mixed, acts, own = K.sems.take(2), K.sems.take(3 * N), K.sems.take(7 * N), K.sems.take(17 * N)
    pe_sums = K.sems.take(2 * N)
    V = lambda name: vector(K, name)
    with ExitStack() as ctx:
        w2a2 = K.sb(ctx, "rwkv_lora_w", N * P)
        g2 = K.sb(ctx, "rwkv_lora_g", N * P)
        starts = K.sb(ctx, "rwkv_chunk_starts", T)
        lw, cl, a, kk, sq, t1, k2 = (K.sb(ctx, f"rwkv_{n}", T) for n in ("log_w", "log_sum", "a", "kk", "squares", "tmp", "k2"))
        e_pos, e_neg, e_ex = (K.sb(ctx, f"rwkv_{n}", T) for n in ("w_run", "w_inv", "w_before"))
        low, glow = rw[:, 12 * T:13 * T], rw[:, 13 * T:14 * T]
        block_ = ctx.enter_context(nc.Block())

        @block_.sync
        def _(sync):
            sync.dma_start(w2a2[0:64, :], d["w2_3"][0]).then_inc(loaded.h, 16)
            sync.dma_start(w2a2[64:P, :], d["a2_3"][0]).then_inc(loaded.h, 16)
            sync.dma_start(g2[:, :], d["g2_3"][0]).then_inc(loaded.h, 16)
            sync.dma_start(starts[:, :], starts64).then_inc(loaded.h, 16)

        @block_.tensor
        def _(pe):
            pe.wait_ge(*loaded(16 * 4))
            pe.wait_ge(*lora(2))
            for t in range(N):
                f = slice(t * P, (t + 1) * P)
                b = 3 * (t % 2)
                pe.wait_ge(*acts((t - 1) * 7))
                pe.matmul(K.bank(b), w2a2[0:64, f], low[0:64, :], start=True, stop=True).then_inc(mixed.h, 1)
                pe.matmul(K.bank(b + 1), w2a2[64:P, f], low[64:P, :], start=True, stop=True).then_inc(mixed.h, 1)
                pe.matmul(K.bank(b + 2), g2[:, f], glow, start=True, stop=True).then_inc(mixed.h, 1)
                pe.wait_ge(*acts(t * 7 + 4))
                pe.matmul(K.bank(6), K.head_ones[:, :], sq[:, :], start=True, stop=True).then_inc(pe_sums.h, 1)
                pe.wait_ge(*own(t * 17 + 11))
                pe.matmul(K.bank(7), K.head_ones[:, :], t1[:, :], start=True, stop=True).then_inc(pe_sums.h, 1)

        @block_.scalar
        def _(act):
            act.activation(low[0:64, :], low[0:64, :], ACT.Tanh).then_inc(lora.h, 1)
            act.activation(glow, glow, ACT.Sigmoid).then_inc(lora.h, 1)
            for t in range(N):
                b = 3 * (t % 2)
                act.wait_ge(*mixed(t * 3 + 3))
                act.wait_ge(*own(t * 17))
                act.wait_ge(*pe_sums(t * 2))
                act.activation(lw[:, :], K.bank(b), ACT.Sigmoid, bias=V("w0_3")(t)).then_inc(acts.h, 1)
                act.activation(a[:, :], K.bank(b + 1), ACT.Sigmoid, bias=V("a0_3")(t)).then_inc(acts.h, 1)
                act.activation(gate[:, t * T:(t + 1) * T], K.bank(b + 2), ACT.Copy).then_inc(acts.h, 1)
                act.wait_ge(*own(t * 17 + 1))
                act.activation(sq[:, :], kk[:, :], ACT.Square).then_inc(acts.h, 1)
                act.wait_ge(*own(t * 17 + 4))
                act.activation(e_pos[:, :], cl[:, :], ACT.Exp)
                act.activation(e_neg[:, :], cl[:, :], ACT.Exp, scale=-1.0)
                act.activation(e_ex[:, :], lw[:, :], ACT.Exp).then_inc(acts.h, 1)
                act.wait_ge(*pe_sums(t * 2 + 1))
                act.activation(sq[:, :], K.bank(6), ACT.Sqrt).then_inc(acts.h, 1)
                act.wait_ge(*pe_sums(t * 2 + 2))
                act.activation(lw[:, :], K.bank(7), ACT.Copy).then_inc(acts.h, 1)

        @block_.vector
        def _(dve):
            dve.wait_ge(*loaded(16 * 4))
            for t in range(N):
                f = slice(t * T, (t + 1) * T)
                r, k, v = (rw[:, (i * N + t) * T:(i * N + t + 1) * T] for i in range(3))
                chain = Chain(dve, own, t * 17)
                chain(dve.tensor_scalar(kk[:, :], k, V("k_k_3")(t), None, ALU.mult))
                dve.wait_ge(*acts(t * 7 + 1))
                chain(dve.tensor_scalar(lw[:, :], lw[:, :], -E_HALF, None, ALU.mult))
                chain(dve.tensor_tensor_scan(cl[:, :], starts[:, :], lw[:, :], 0.0, ALU.mult, ALU.add))
                chain(dve.tensor_tensor(lw[:, :], cl[:, :], lw[:, :], ALU.subtract))
                dve.wait_ge(*acts(t * 7 + 2))
                chain(dve.tensor_scalar(k2[:, :], a[:, :], -1.0, V("k_a_3")(t), ALU.add, ALU.mult))
                chain(dve.scalar_tensor_tensor(out=k2[:, :], in0=k2[:, :], scalar=1.0, in1=k, op0=ALU.add, op1=ALU.mult))
                dve.wait_ge(*acts(t * 7 + 6))
                chain(dve.tensor_scalar(sq[:, :], sq[:, :], 1e-12, None, ALU.max))
                chain(dve.reciprocal(sq[:, :], sq[:, :]))
                chain(dve.tensor_tensor(kk[:, :], kk[:, :], sq[:, :], ALU.mult))
                chain(dve.tensor_tensor(a[:, :], a[:, :], kk[:, :], ALU.mult))
                chain(dve.scalar_tensor_tensor(out=t1[:, :], in0=r, scalar=V("r_k_3")(t), in1=k2[:, :], op0=ALU.mult, op1=ALU.mult), False)
                chain(dve.scalar_tensor_tensor(out=A[:, f], in0=kk[:, :], scalar=-1.0, in1=e_ex[:, :], op0=ALU.mult, op1=ALU.mult), False)
                chain(dve.tensor_tensor(B[:, f], a[:, :], e_neg[:, :], ALU.mult), False)
                chain(dve.tensor_tensor(C[:, f], k2[:, :], e_neg[:, :], ALU.mult), False)
                chain(dve.tensor_tensor(R[:, f], r, e_pos[:, :], ALU.mult), False)
                chain(dve.tensor_copy(ends[:, t * 8:(t + 1) * 8], e_pos[:, CHUNK - 1:T:CHUNK]), False)
                dve.wait_ge(*acts(t * 7 + 7))
                chain(dve.tensor_tensor(bonus[:, f], lw[:, :], v, ALU.mult))


def rwkv_scan(K, A, R, B, C, v, ends, masks, y):
    nc = K.nc
    N = RWKV_TILES
    W = 2 * NT * P
    LEVELS = 3
    PE_N, DVE_N, ACT_N = 14, 25, 5
    mm, own, acted = K.sems.take(N * PE_N), K.sems.take(N * DVE_N), K.sems.take(N * ACT_N)
    staged, done = K.sems.take(N), K.sems.take(N)
    chunk_mm, chunk_own = K.sems.take(N * 8 * 3), K.sems.take(N * 8 * 4)
    loaded = K.sems.take(16)

    def blk(buf, h, c):
        return buf[:, (h * NT + c) * P:(h * NT + c + 1) * P]

    with ExitStack() as ctx:
        m = K.sb(ctx, "rwkv_masks", 6 * P)
        ar = K.sb(ctx, "rwkv_a_r", 2 * T)
        b, c_, vs = K.sb(ctx, "rwkv_b_pair", T), K.sb(ctx, "rwkv_c_pair", T), K.sb(ctx, "rwkv_v_pair", T)
        bn, cn, vn = K.sb(ctx, "rwkv_b_n", T), K.sb(ctx, "rwkv_c_n", T), K.sb(ctx, "rwkv_v_n", T)
        ba, ca = K.sb(ctx, "rwkv_ba_br", 2 * W), K.sb(ctx, "rwkv_ca_cr", 2 * W)
        bat = K.sb(ctx, "rwkv_ba_t", W)
        p1, p1t, p2, p2t, inv, invt = (K.sb(ctx, f"rwkv_{n}", W) for n in ("p1", "p1t", "p2", "p2t", "inv", "inv_t"))
        S, aged = K.sb(ctx, "rwkv_state", P), K.sb(ctx, "rwkv_state_aged", P)
        wsb, usb = K.sb(ctx, "rwkv_w_chunk", P), K.sb(ctx, "rwkv_u_chunk", P)
        block_ = ctx.enter_context(nc.Block())

        def wide(buf, n=P):
            return buf.rearrange("p (x n) -> p x n", n=n)

        def spread(tiles, i, n=1):
            return tiles[:, i * P:(i + n) * P].unsqueeze(1).to_broadcast([P, 2 * NT, n * P])

        def banks(i, n=2):
            return K.ps[:, i * T:(i + n) * T]

        @block_.sync
        def _(sync):
            sync.dma_start(m[:, :], masks).then_inc(loaded.h, 16)

        @block_.gpsimd
        def _(pool):
            with pool.Fori(0, N) as j:
                pool.wait_ge(*done(j))
                for i, src in enumerate((A, R)):
                    pool.tensor_copy(ar[:, :].rearrange("p (c i n) -> p c i n", i=2, n=P)[:, :, i, :],
                                     cols(src, j * T, T).rearrange("p (c n) -> p c n", n=P))
                pool.tensor_copy(b[:, :], cols(B, j * T, T))
                pool.tensor_copy(c_[:, :], cols(C, j * T, T))
                pool.tensor_copy(vs[:, :], cols(v, j * T, T)).then_inc(staged.h, 1)

        @block_.tensor
        def _(pe):
            def each(bank, left, right, width=P):
                for h in range(2):
                    for c in range(NT):
                        x = bank * T + (h * NT + c) * width
                        last = pe.matmul(K.ps[:, x:x + width], left(h, c), right(h, c), start=True, stop=True)
                return last

            def whole(buf):
                return lambda h, c: blk(buf, h, c)

            def half(buf, stride=P, width=P):
                return lambda h, c: buf[64 * h:64 * h + 64, c * stride:c * stride + width]

            with pe.Fori(0, N) as j:
                at = j * DVE_N
                pe.wait_ge(*staged(j + 1))
                pe.wait_ge(*done(j))
                each(0, half(b), half(ar, 2 * P, 2 * P), 2 * P).then_inc(mm.h, 1)
                each(4, half(ar, 2 * P), half(b)).then_inc(mm.h, 1)
                pe.wait_ge(*own(at + 1))
                each(0, half(c_), half(ar, 2 * P, 2 * P), 2 * P).then_inc(mm.h, 1)
                pe.wait_ge(*own(at + 2))
                for i, src in enumerate((b, c_, vs)):
                    for c in range(NT):
                        last = pe.transpose(K.bank(4 + i, P, P, c * P), src[:, c * P:(c + 1) * P], K.ident[:, :])
                last.then_inc(mm.h, 1)
                pe.wait_ge(*acted(j * ACT_N + 1))
                q, qt, s, st = p1, p1t, p2, p2t
                for lev in range(LEVELS):
                    pe.wait_ge(*own(at + 7 + 3 * lev))
                    each(0, whole(qt), whole(q))
                    each(2, whole(q), whole(qt)).then_inc(mm.h, 1)
                    pe.wait_ge(*own(at + 8 + 3 * lev))
                    pe.wait_ge(*acted(j * ACT_N + 2 + lev))
                    each(4, whole(st), whole(inv))
                    each(6, whole(s), whole(invt)).then_inc(mm.h, 1)
                    q, qt, s, st = s, st, q, qt
                pe.wait_ge(*own(at + 18))
                each(0, whole(qt), whole(inv))
                each(2, whole(q), whole(invt)).then_inc(mm.h, 1)
                pe.wait_ge(*own(at + 19))
                pe.wait_ge(*acted(j * ACT_N + 5))
                each(4, whole(invt), whole(s))
                each(6, whole(inv), whole(st)).then_inc(mm.h, 1)
                pe.wait_ge(*own(at + 22))
                each(0, whole(qt), whole(inv)).then_inc(mm.h, 1)
                pe.wait_ge(*own(at + 23))
                each(4, whole(invt), whole(s)).then_inc(mm.h, 1)

                for n in range(T // CHUNK):
                    c, o = n // 2, CHUNK * (n % 2)
                    tok, at_n = slice(o, o + CHUNK), j * 32 + 4 * n
                    if n == 0:
                        pe.wait_ge(*own(at + 25))
                    else:
                        pe.wait_ge(*chunk_own(at_n))
                    pe.matmul(K.ps[tok, 0:P], ar[:, c * 2 * P + o:c * 2 * P + o + CHUNK], S[:, :], start=True, stop=False,
                              skip_group_check=True)
                    for h in range(2):
                        x = (h * NT + c) * 2 * P
                        last = pe.matmul(K.ps[tok, 64 * h:64 * h + 64], ca[:, x + o:x + o + CHUNK],
                                         vn[:, c * P + 64 * h:c * P + 64 * h + 64], start=False, stop=h == 1, skip_group_check=True)
                    last.then_inc(chunk_mm.h, 1)
                    pe.wait_ge(*chunk_own(at_n + 2))
                    for h in range(2):
                        last = pe.matmul(K.ps[tok, T + 64 * h:T + 64 * h + 64], blk(inv, h, c)[:, tok],
                                         wsb[:, 64 * h:64 * h + 64], start=True, stop=True)
                    last.then_inc(chunk_mm.h, 1)
                    pe.wait_ge(*chunk_own(at_n + 3))
                    grown = K.bank(3, P)
                    pe.matmul(grown, bn[tok, c * P:(c + 1) * P], usb[tok, :], start=True, stop=False)
                    pe.matmul(grown, cn[tok, c * P:(c + 1) * P], vn[tok, c * P:(c + 1) * P], start=False, stop=True)
                    y_at = 2 * T + n * CHUNK
                    pe.matmul(K.ps[:, y_at:y_at + CHUNK], S[:, :], ar[:, (c * 2 + 1) * P + o:(c * 2 + 1) * P + o + CHUNK],
                              start=True, stop=False, skip_group_check=True)
                    for h in range(2):
                        x = (h * NT + c) * 2 * P + P + o
                        out = K.ps[64 * h:64 * h + 64, y_at:y_at + CHUNK]
                        pe.matmul(out, usb[:, 64 * h:64 * h + 64], ba[:, x:x + CHUNK], start=False, stop=False, skip_group_check=True)
                        last = pe.matmul(out, vn[:, c * P + 64 * h:c * P + 64 * h + 64], ca[:, x:x + CHUNK], start=False,
                                         stop=h == 1, skip_group_check=True)
                    last.then_inc(chunk_mm.h, 1)

        @block_.scalar
        def _(act):
            with act.Fori(0, N) as j:
                def copy(n, dst, src):
                    act.wait_ge(*mm(j * PE_N + n))
                    act.activation(dst, src, ACT.Copy).then_inc(acted.h, 1)
                act.wait_ge(*mm(j * PE_N + 4))
                act.activation(bn[:, :], K.bank(4), ACT.Copy)
                act.activation(cn[:, :], K.bank(5), ACT.Copy)
                act.activation(vn[:, :], K.bank(6), ACT.Copy).then_inc(acted.h, 1)
                for lev in range(LEVELS):
                    copy(5 + 2 * lev, (p2t if lev % 2 == 0 else p1t)[:, :], banks(2))
                copy(11, p1t[:, :], banks(2))

        @block_.vector
        def _(dve):
            dve.wait_ge(*loaded(16))
            with dve.Fori(0, N) as j:
                chain = Chain(dve, own, j * DVE_N)

                def after(n):
                    dve.wait_ge(*mm(j * PE_N + n))

                def masked(dst, src, i):
                    return dve.tensor_tensor(wide(dst[:, :]), src, spread(m, i), ALU.mult)

                def grow(buf, bank):
                    return dve.tensor_tensor(buf[:, :], buf[:, :], banks(bank), ALU.add)
                ba_part = wide(ba[:, :], 2 * P)[:, :, 0:P]
                after(1)
                chain(dve.tensor_tensor(wide(ba[:, :], 2 * P), wide(banks(0, 4), 2 * P), spread(m, 0, 2), ALU.mult))
                after(2)
                chain(masked(bat, wide(banks(4)), 2))
                after(3)
                chain(dve.tensor_tensor(wide(ca[:, :], 2 * P), wide(banks(0, 4), 2 * P), spread(m, 0, 2), ALU.mult), False)
                chain(masked(p1, ba_part, 3))
                chain(masked(p1t, wide(bat[:, :]), 3))
                chain(dve.tensor_tensor(wide(inv[:, :]), wide(p1[:, :]), spread(K.ident, 0), ALU.add), False)
                chain(dve.tensor_tensor(wide(invt[:, :]), wide(p1t[:, :]), spread(K.ident, 0), ALU.add), False)
                for lev in range(LEVELS):
                    after(5 + 2 * lev)
                    chain(dve.tensor_copy((p2 if lev % 2 == 0 else p1)[:, :], banks(0)), False)
                    after(6 + 2 * lev)
                    chain(grow(inv, 4))
                    chain(grow(invt, 6))
                chain(masked(p2, ba_part, 4), False)
                chain(masked(p2t, wide(bat[:, :]), 4), False)
                after(11)
                chain(dve.tensor_copy(p1[:, :], banks(0)), False)
                after(12)
                chain(grow(inv, 4), False)
                chain(grow(invt, 6), False)
                chain(masked(p2t, wide(bat[:, :]), 5))
                after(13)
                chain(dve.tensor_copy(p1[:, :], banks(0)), False)
                after(14)
                chain(grow(inv, 4), False)
                dve.memset(wsb[:, :], 0.0)
                dve.memset(usb[:, :], 0.0)
                chain(dve.memset(S[:, :], 0.0))
                for n in range(T // CHUNK):
                    o = CHUNK * (n % 2)
                    tok = slice(o, o + CHUNK)
                    chunk = Chain(dve, chunk_own, j * 32 + 4 * n)
                    chunk(dve.tensor_scalar(aged[:, :], S[:, :], cols(ends, j * 8 + n, 1), None, ALU.mult), False)
                    dve.wait_ge(*chunk_mm(j * 24 + 3 * n + 1))
                    chunk(dve.tensor_copy(wsb[tok, :], K.ps[tok, 0:P]), False)
                    dve.wait_ge(*chunk_mm(j * 24 + 3 * n + 2))
                    chunk(dve.tensor_copy(usb[tok, :], K.ps[tok, T:T + P]))
                    dve.wait_ge(*chunk_mm(j * 24 + 3 * n + 3))
                    for h in range(2):
                        feat = slice(64 * h, 64 * h + 64)
                        last = dve.scalar_tensor_tensor(out=S[feat, feat], in0=K.ps[feat, 3 * T + 64 * h:3 * T + 64 * h + 64],
                                                        scalar=cols(ends, j * 8 + n, 1, 64, 64 * h), in1=aged[feat, feat],
                                                        op0=ALU.mult, op1=ALU.add)
                    chunk(last)
                dve.tensor_copy(cols(y, j * T, T), K.bank(2)).then_inc(done.h, 1)


def rwkv_output(K, y, bonus, gate, dst):
    nc = K.nc
    N = RWKV_TILES
    summed, own, acts = K.sems.take(2 * N), K.sems.take(8 * N), K.sems.take(2 * N)
    V = lambda name: vector(K, name)
    with ExitStack() as ctx:
        sq, r = K.sb(ctx, "rwkv_y_squares", T), K.sb(ctx, "rwkv_y_scale", T)
        block_ = ctx.enter_context(nc.Block())

        @block_.tensor
        def _(pe):
            for t in range(N):
                if t:
                    pe.wait_ge(*own(t * 8))
                pe.matmul(K.bank(0), K.head_ones[:, :], y[:, t * T:(t + 1) * T], start=True, stop=True).then_inc(summed.h, 1)
                pe.wait_ge(*acts(2 * t + 1))
                pe.matmul(K.bank(1), K.head_ones[:, :], sq[:, :], start=True, stop=True).then_inc(summed.h, 1)

        @block_.scalar
        def _(act):
            for t in range(N):
                act.wait_ge(*own(t * 8 + 1))
                act.activation(sq[:, :], y[:, t * T:(t + 1) * T], ACT.Square).then_inc(acts.h, 1)
                act.wait_ge(*own(t * 8 + 2))
                act.activation(r[:, :], r[:, :], ACT.Sqrt).then_inc(acts.h, 1)

        @block_.vector
        def _(dve):
            for t in range(N):
                f = slice(t * T, (t + 1) * T)
                chain = Chain(dve, own, t * 8)
                dve.wait_ge(*summed(2 * t + 1))
                chain(dve.scalar_tensor_tensor(out=y[:, f], in0=K.bank(0), scalar=-1.0 / HEAD, in1=y[:, f], op0=ALU.mult, op1=ALU.add))
                dve.wait_ge(*summed(2 * t + 2))
                chain(dve.tensor_scalar(r[:, :], K.bank(1), 1.0 / HEAD, 64e-5, ALU.mult, ALU.add))
                dve.wait_ge(*acts(2 * t + 2))
                chain(dve.reciprocal(r[:, :], r[:, :]))
                chain(dve.tensor_tensor(y[:, f], y[:, f], r[:, :], ALU.mult))
                chain(dve.tensor_scalar(y[:, f], y[:, f], V("ln_x_w_3")(t), V("ln_x_b_3")(t), ALU.mult, ALU.add))
                chain(dve.tensor_tensor(y[:, f], y[:, f], bonus[:, f], ALU.add))
                chain(dve.tensor_tensor(dst[:, f], y[:, f], gate[:, f], ALU.mult))
                chain(dve.memset(r[:, 0:1], 0.0), False)


def third_block(K, d, tables, X, U, plans, scratch):
    V = lambda name: vector(K, name)
    rmsnorm_t(K, X, U, TM, V("norm1_g_3"), 1e-6)
    with ExitStack() as mix:
        mixed = K.sb(mix, "mixer_out", KD * T)
        with ExitStack() as nsa:
            qkv = K.sb(nsa, "nsa_q_cmp", 6 * T)
            k = K.sb(nsa, "nsa_k", 4 * T)
            v = K.sb(nsa, "nsa_v", NT * 2 * P)
            gates = K.sb(nsa, "nsa_gates", NT * 3 * NSA_HEADS)
            kc, vc = K.sb(nsa, "nsa_k_cmp", NSA_GROUPS * CMP), K.sb(nsa, "nsa_v_cmp", NSA_GROUPS * HEAD, CMP)
            project_t(K, plans["nsa_q"], U, TM, qkv, T)
            project_t(K, plans["nsa_k"], U, TM, k, T)
            project_n(K, plans["nsa_v"], U, TM, v, 2 * P, 2 * P)
            project_n(K, plans["nsa_gates"], U, TM, gates, 3 * NSA_HEADS, 3 * NSA_HEADS, func=ACT.Sigmoid)
            head_norm_t(K, qkv, T, range(4), lambda t: V("q_norm_g_3")(0), 1e-6)
            head_norm_t(K, k, T, range(4), lambda t: V("k_norm_g_3")(1 + t // 2), 1e-6)
            compress(K, qkv[:, 4 * T:6 * T], kc, vc, d["cmp_pos_3"][0], d["cmp_w1_3"][0], d["cmp_w2_3"][0],
                     d["cmp_b2_3"][0], 1e-6, V("k_norm_g_3")(0))
            bias = K.sb(nsa, "nsa_bias", NSA_HEADS * BIAS_W)
            distance_bias(K, d["rel_bias_3"], tables["bucket_onehot"], tables["flip"], scratch, bias)
            hide_uncompressed(K, gates, tables["cmp_seen"])
            y = K.sb(nsa, "nsa_y", NT * T)
            nsa_attention(K, qkv, k, v, kc, vc, gates, bias, y)
            turn_tokens(K, y, mixed, NT)
        with ExitStack() as rwkv:
            bonus, gate = K.sb(rwkv, "rwkv_bonus", NT * T), K.sb(rwkv, "rwkv_gate", NT * T)
            ends = K.sb(rwkv, "rwkv_w_ends", RWKV_TILES * 8)
            rw = K.sb(rwkv, "rwkv_in", 14 * T)
            project_shift_t(K, plans["rwkv_in"], U, TM, rw)
            A, B = U[:, 0:4 * T], U[:, 4 * T:8 * T]
            R, C = rw[:, 0:4 * T], rw[:, 4 * T:8 * T]
            rwkv_features(K, d, tables["starts64"], rw, A, R, B, C, ends, gate, bonus)
            y = mixed[:, 4 * T:8 * T]
            rwkv_scan(K, A, R, B, C, rw[:, 8 * T:12 * T], ends, tables["chunk_masks"], y)
            rwkv_output(K, y, bonus, gate, y)
        add_product(K, plans["w_out3"], mixed, T, X, TM)
    rmsnorm_t(K, X, U, TM, V("norm2_g_3"), 1e-6)
    conv_swiglu(K, U, TM, X, plans["ffn_up3"], plans["ffn_down3"], "conv_w_3", "conv_b_3", False)


def hide_uncompressed(K, gates, seen):
    nc = K.nc
    loaded = K.sems.take(16)
    with ExitStack() as ctx:
        mask = K.sb(ctx, "cmp_seen", 1)
        block_ = ctx.enter_context(nc.Block())

        @block_.sync
        def _(sync):
            sync.dma_start(mask[:, :], seen).then_inc(loaded.h, 16)

        @block_.vector
        def _(dve):
            dve.wait_ge(*loaded(16))
            g = gates[:, 0:3 * NSA_HEADS:3]
            dve.tensor_scalar(g, g, mask[:, 0:1], None, ALU.mult)


def project_shift_t(K, plan, src, stride, dst):
    nc = K.nc
    taps, tiles = 2, 14
    per = 2 * taps
    shifted = K.sems.take(plan.groups * per)
    mixed = K.sems.take(1)
    with ExitStack() as ctx:
        block_ = ctx.enter_context(nc.Block())

        @block_.sync
        def _(sync):
            K.stream.run(sync)

        @block_.tensor
        def _(pe):
            product_t(K, plan, src, stride, 2, [lambda k: shifted(k * per)])(pe)

        @block_.vector
        def _(dve):
            c = K.column["rwkv_mix"]
            dve.tensor_scalar(K.vectors[:, c + tiles:c + 2 * tiles], K.vectors[:, c:c + tiles], -1.0, 1.0, ALU.mult, ALU.add)\
               .then_inc(mixed.h, 1)
            dve.wait_ge(*mixed(1))
            for i, k, u in steps(dve, plan.groups, WEIGHT_SLOTS):
                dve.wait_ge(*plan.done(k))
                chain = Chain(dve, shifted, k * per)
                for ct in range(2):
                    t = 2 * k + ct
                    w = [vector(K, "rwkv_mix")(tiles + t), vector(K, "rwkv_mix")(t)]
                    dst_t = cols(dst, t * T, T)
                    bank = K.bank((u % 2) * 2 + ct)
                    chain(dve.tensor_scalar(dst_t, bank, w[0], None, ALU.mult))
                    dst_s = cols(dst, t * T + 1, T - 1)
                    chain(dve.scalar_tensor_tensor(out=dst_s, in0=bank[:, 0:T - 1], scalar=w[1], in1=dst_s, op0=ALU.mult, op1=ALU.add))


def rows_of(ap, n=None):
    return ap.rearrange("(r p) -> r p", p=P)


def twice(ap):
    return ap.rearrange("(a n) -> a n", a=1)


def first_block(K, d, tables, X, U, plans):
    nc = K.nc
    V = lambda name: vector(K, name)
    rmsnorm_t(K, X, U, TM, V("norm_ffn1"), 1e-6, meta=True)
    swiglu(K, U, TM, X, plans["ffn1_up"], plans["ffn1_down"], meta=True)
    rmsnorm_t(K, X, U, TM, V("norm_mix"), 1e-6, meta=True)
    with ExitStack() as mix:
        ya = K.sb(mix, "fox_y_t", KD * T)
        with ExitStack() as fox:
            v = K.sb(fox, "fox_v", NT * D)
            v_meta = K.sb(fox, "fox_v_meta", D, META)
            y = K.sb(fox, "fox_y", NT * D)
            with ExitStack() as qk:
                q, k = K.sb(qk, "fox_q", KD * T), K.sb(qk, "fox_k", KD * TM)
                ncB = K.sb(qk, "fox_forget", FOX_HEADS * TM)
                project_t(K, plans["fox_q"], U, TM, q, T)
                project_t(K, plans["fox_k"], U, TM, k, TM, meta=True)
                project_n(K, plans["fox_v"], U, TM, v, 256, D, v_meta)
                forget_sums(K, plans["fox_f"], U, d["b_forget"][0], ncB)
                head_norm_t(K, q, T, range(KD), lambda t: V("fox_q_norm")(0), 1e-6)
                head_norm_t(K, k, TM, range(KD), lambda t: V("fox_k_norm")(0), 1e-6, range(KD))
                fox_attention(K, q, k, v, v_meta, ncB, y)
            turn_tokens(K, y, ya, KD)
        yb = K.sb(mix, "ret_y_t", KD * T)
        with ExitStack() as ret:
            q, k = K.sb(ret, "ret_q_t", RET_HEADS * T), K.sb(ret, "ret_k_t", RET_HEADS * TM)
            v, v_meta = K.sb(ret, "ret_v", NT * D), K.sb(ret, "ret_v_meta", D, META)
            project_t(K, plans["ret_q"], U, TM, q, T)
            project_t(K, plans["ret_k"], U, TM, k, TM, meta=True)
            project_n(K, plans["ret_v"], U, TM, v, 256, D, v_meta)
            project_t(K, plans["ret_g"], U, TM, yb, T, func=ACT.Silu)
            retention(K, q, k, v, v_meta, yb, yb, tables)
        gates = K.sb(mix, "mix_gates", 2 * KD * T)
        project_t(K, plans["gates1"], U, TM, gates, T, func=ACT.Sigmoid, bias=V("b_gate"))
        gated_sum(K, plans["w_o_fox"], ya, plans["w_o_ret"], yb, gates[:, 0:KD * T], gates[:, KD * T:2 * KD * T])
        add_product(K, plans["w_out1"], gates, T, X, TM)
    rmsnorm_t(K, X, U, TM, V("norm_ffn2"), 1e-6)
    swiglu(K, U, TM, X, plans["ffn2_up"], plans["ffn2_down"])


def block(start, step=256, width=256):
    return lambda k: [(0, width, k * step + start)]


def pair(second):
    return lambda k: [(0, P, k * P), (P, P, k * P + second)]


def plan_weights(K, d):
    S, plans = K.stream, {}

    def add(name, weights, kt, slots, columns, width=256, ksplit=1):
        plans[name] = Product(S, weights, kt, slots, columns, width, ksplit)

    w = d["w_in"][0]
    add("ffn1_up", d["w_ffn1_in"][0], KD, KF, pair(FF))
    add("ffn1_down", d["w_ffn1_out"][0], KF // 2, 2 * KD, block(0, P, P), P, 2)
    add("fox_q", w, KD, 4, block(0))
    add("fox_k", w, KD, 4, block(1024))
    add("fox_v", w, KD, 4, block(2048))
    add("fox_f", w, KD, 1, block(3072, 0, FOX_HEADS), FOX_HEADS)
    add("ret_q", w, KD, 2, block(3088))
    add("ret_k", w, KD, 2, block(3600))
    add("ret_v", w, KD, 4, block(4112))
    add("ret_g", w, KD, 4, block(5136))
    add("gates1", w, KD, 8, block(6160))
    add("w_o_fox", d["w_o_fox"][0], KD, 4, block(0))
    add("w_o_ret", d["w_o_ret"][0], KD, 4, block(0))
    add("w_out1", d["w_out"][0], KD, 4, block(0))
    add("ffn2_up", d["w_ffn2_in"][0], KD, KF, pair(FF))
    add("ffn2_down", d["w_ffn2_out"][0], KF // 2, 2 * KD, block(0, P, P), P, 2)
    w = d["w_in_2"][0]
    add("gate_a2", w, KD, 4, block(0))
    add("gmlp_u", w, KD, 4, block(2048))
    add("gmlp_v", w, KD, 4, block(3072))
    add("w_proj_a", d["w_proj_a_2"][0], KD, 4, block(0))
    add("xbc", w, KD, 12, block(6144))
    add("dt", w, KD, 1, block(9216, 0, SSM_HEADS), SSM_HEADS)
    add("ssm_z", w, KD, 8, block(4096))
    add("gate_b2", w, KD, 4, block(1024))
    add("w_proj_b", d["w_proj_b_2"][0], KD, 8, block(0), 256, 2)
    add("w_out2", d["w_out_2"][0], KD, 4, block(0))
    add("ffn_up2", d["ffn_w_up_2"][0], KD, KF, pair(FF))
    add("ffn_down2", d["ffn_w_down_2"][0], KF // 2, 2 * KD, block(0, P, P), P, 2)
    w = d["w_in_3"][0]
    add("nsa_q", w, KD, 3, block(0))
    add("nsa_k", w, KD, 2, lambda k: [(HEAD * i, HEAD, 768 + 256 * k + HEAD * (i // 2)) for i in range(4)])
    add("nsa_v", w, KD, 1, lambda k: [(0, P, 896), (P, P, 1152)])
    add("nsa_gates", w, KD, 1, block(1280, 0, 3 * NSA_HEADS), 3 * NSA_HEADS)
    add("rwkv_in", w, KD, 7, block(1304))
    add("w_out3", d["w_out_3"][0], KD, 4, block(0))
    add("ffn_up3", d["ffn_up_3"][0], KD, KF, lambda k: [(0, P, k * P + FF), (P, P, k * P)])
    add("ffn_down3", d["ffn_down_3"][0], KF // 2, 2 * KD, block(0, P, P), P, 2)
    return plans


def write_t(K, buf, stride, out):
    nc = K.nc
    turned, copied, written = K.sems.take(KD), K.sems.take(KD), K.sems.take(16 * NT)
    with ExitStack() as ctx:
        rows = K.sb(ctx, f"out_rows_{nc.next_id()}", NT * D)
        blk = ctx.enter_context(nc.Block())

        @blk.tensor
        def _(pe):
            for n in range(2 * NT):
                t, half = n // 2, n % 2
                pe.wait_ge(*copied(n - 1))
                for j in range(4):
                    f = half * 4 + j
                    last = pe.transpose(K.bank(n % 2, P, P, j * P), buf[:, f * stride + t * P:f * stride + (t + 1) * P], K.ident[:, :])
                last.then_inc(turned.h, 1)

        @blk.vector
        def _(dve):
            for n in range(2 * NT):
                dve.wait_ge(*turned(n + 1))
                dve.tensor_copy(rows[:, n * T:(n + 1) * T], K.bank(n % 2)).then_inc(copied.h, 1)

        @blk.sync
        def _(sync):
            for t in range(NT):
                sync.wait_ge(*copied(2 * t + 2))
                sync.dma_start(out[t * P:(t + 1) * P, :], rows[:, t * D:(t + 1) * D]).then_inc(written.h, 16)
            sync.wait_ge(*written(16 * NT))


def setup(K, tables):
    nc = K.nc
    K.ident = K.sb(K.ctx, "identity", P)
    K.ones = K.sb(K.ctx, "ones", P)
    K.head_ones = K.sb(K.ctx, "head_ones", P)
    K.causal = K.sb(K.ctx, "causal_mask", P)
    with ExitStack() as ctx:
        block_ = ctx.enter_context(nc.Block())

        @block_.vector
        def _(dve):
            dve.memset(K.ones[:, :], 1.0)

        @block_.gpsimd
        def _(pool):
            for h in K.sems.all + K.stream.full + [K.stream.used]:
                pool.sem_inc(h, CREDIT)
    landed = K.sems.take(16 * 3)
    with ExitStack() as ctx:
        block_ = ctx.enter_context(nc.Block())

        @block_.sync
        def _(sync):
            for dst, name in ((K.ident, "ident"), (K.head_ones, "head_ones"), (K.causal, "causal")):
                sync.dma_start(dst[:, :], tables[name]).then_inc(landed.h, 16)
            sync.wait_ge(*landed(16 * 3))


def three_blocks_kernel(nc, d, tables, scratch, out):
    with ExitStack() as ctx:
        K = Kernel(nc, ctx)
        setup(K, tables)
        plans = plan_weights(K, d)
        vec = []

        def add(name, ap, n, doubled=False):
            vec.append((name, ap, n))
        for name in ("norm_ffn1", "norm_mix", "norm_ffn2", "ret_gn"):
            add(name, rows_of(d[name][0]), KD)
        add("b_gate", rows_of(d["b_gate"][0]), 2 * KD)
        add("fox_q_norm", d["fox_q_norm"], 1)
        add("fox_k_norm", d["fox_k_norm"], 1)
        for name, n in (("mix_norm_w_2", KD), ("gate_bias_2", 2 * KD), ("ssm_conv_b_2", 3 * KD), ("ssm_norm_w_2", 2 * KD),
                        ("ffn_norm_w_2", KD), ("ffn_conv_b_2", 2 * KF)):
            ap = d[name][0]
            add(name, ap.rearrange("a (r p) -> (a r) p", p=P) if name == "gate_bias_2" else rows_of(ap), n)
        add("final_norm_w_2", rows_of(d["final_norm_w_2"]), KD)
        add("ssm_conv_w_2", d["ssm_conv_w_2"][0].rearrange("k (r p) -> (k r) p", p=P), 4 * 3 * KD)
        add("ffn_conv_w_2", d["ffn_conv_w_2"][0].rearrange("k (r p) -> (k r) p", p=P), 3 * 2 * KF)
        for name, n in (("norm1_g_3", KD), ("norm2_g_3", KD), ("conv_b_3", 2 * KF), ("w0_3", 4), ("a0_3", 4), ("k_k_3", 4),
                        ("k_a_3", 4), ("ln_x_w_3", 4), ("ln_x_b_3", 4)):
            add(name, rows_of(d[name][0]), n)
        add("r_k_3", d["r_k_3"][0].rearrange("(t h) n -> t (h n)", h=2), 4)
        add("rwkv_mix", rows_of(d["rwkv_mu_3"][0]), 14)
        add("rwkv_mix_rest", rows_of(d["rwkv_mu_3"][0]), 14)
        add("cmp_b1_3", d["cmp_b1_3"][0], 2)
        add("cmp_b2_3", d["cmp_b2_3"][0], 2)
        add("q_norm_g_3", d["q_norm_g_3"], 1)
        add("k_norm_g_3", d["k_norm_g_3"][0], 3)
        add("conv_w_3", d["conv_w_3"][0].rearrange("k (r p) -> (k r) p", p=P), 3 * 2 * KF)
        load_vectors(K, vec)
        X = K.sb(ctx, "residual", KD * TM)
        U = K.sb(ctx, "normalized", KD * TM)
        load_x(K, d["x"][0], d["meta_tokens"], X, TM)
        first_block(K, d, tables, X, U, plans)
        second_block(K, d, tables, X, U, plans)
        third_block(K, d, tables, U, X, plans, scratch)
        write_t(K, U, TM, out[0])


def shape_tables():
    f = np.float32
    t = {"ident": np.eye(P, dtype=f), "head_ones": np.kron(np.eye(2, dtype=f), np.ones((64, 64), f))}
    a = np.arange(P)
    t["causal"] = np.where(a[None, :] <= a[:, None], 0, NEG).astype(f)
    t["causal01"] = (a[None, :] >= a[:, None]).astype(f)
    t["starts"] = np.broadcast_to(np.arange(T) % P != 0, (P, T)).astype(f)
    d_ = 511 - np.arange(2 * T)
    n = np.maximum(d_, 0)
    large = 16 + (np.log(np.maximum(n, 1).astype(f) / f(16)) / f(np.log(128 / 16)) * f(16)).astype(np.int32)
    bucket = np.where(d_ < 0, BUCKETS, np.where(n < 16, n, np.minimum(large, BUCKETS - 1)))
    t["bucket_onehot"] = (np.arange(BUCKETS + 1)[:, None] == bucket[None, :]).astype(f)
    t["cmp_seen"] = (a[:, None] >= CMP_BLOCK - 1).astype(f)
    to, fr = a[None, :], a[:, None]
    near = [fr // w == to // w for w in (16, 32, 64)]
    t["chunk_masks"] = np.concatenate([near[2] & (fr < to), near[2] & (fr <= to), near[2] & (fr > to), near[0],
                                       near[1] & ~near[0], near[2] & ~near[1]], axis=1).astype(f)
    t["starts64"] = np.broadcast_to(np.arange(T) % CHUNK != 0, (P, T)).astype(f)
    t["flip"] = np.ascontiguousarray(np.eye(P, dtype=f)[::-1])
    t["swap"] = np.roll(np.eye(P, dtype=f), P // 2, axis=0)
    pos = np.concatenate([META + np.arange(T), np.arange(META)]).astype(f)
    half = P // 2
    inv = (f(10000.0) ** (-np.arange(half, dtype=f) / f(half))).astype(f)
    ang = (inv[:, None] * pos[None, :]).astype(f).astype(np.float64)
    t["rope_cos"] = np.concatenate([np.cos(ang), np.cos(ang)]).astype(f)
    t["rope_sin"] = np.concatenate([-np.sin(ang), np.sin(ang)]).astype(f)
    lg = np.log1p(-np.exp2(-5.0 - np.arange(4)))
    gap = a[None, :] - a[:, None]
    t["decay"] = np.concatenate([np.where(gap >= 0, np.exp(g * np.maximum(gap, 0)), 0) for g in lg], axis=1).astype(f)
    t["xi"] = np.concatenate([np.broadcast_to(np.exp(g * (a + 1.0)), (P, P)) for g in lg], axis=1).astype(f)
    t["zeta"] = np.concatenate([np.stack([np.exp(g * (P - 1 - a)) for g in lg], 1),
                                np.broadcast_to(np.exp(lg * P), (P, 4))], axis=1).astype(f)
    t["zeta_meta"] = np.stack([np.exp(g * (META - 1 - np.arange(META))) for g in lg], 1).astype(f)
    return t


def kernel(**inputs):
    import concourse.bacc as bacc
    from concourse.bass_utils import run_bass_kernel_spmd

    nc = bacc.Bacc("TRN2", target_bir_lowering=False, num_devices=1)
    arrays = {f"in_{name}": np.ascontiguousarray(a) for name, a in inputs.items()}
    for name in ("fox_q_norm", "fox_k_norm", "q_norm_g_3", "k_norm_g_3", "cmp_b2_3"):
        a = arrays[f"in_{name}"]
        arrays[f"in_{name}"] = np.ascontiguousarray(np.concatenate([a, a], axis=-1))
    tables = {f"table_{name}": np.ascontiguousarray(a) for name, a in shape_tables().items()}

    def declare(name, a):
        return nc.dram_tensor(name, a.shape, mybir.dt.from_np(a.dtype), kind="ExternalInput").ap()
    d = {name[3:]: declare(name, a) for name, a in arrays.items()}
    tb = {name[6:]: declare(name, a) for name, a in tables.items()}
    out = nc.dram_tensor("out", (1, T, D), F32, kind="ExternalOutput").ap()
    scratch = nc.dram_tensor("distance_bias_line", (NSA_HEADS, 2 * T), F32, kind="Internal").ap()
    three_blocks_kernel(nc, d, tb, scratch, out)
    r = run_bass_kernel_spmd(nc, [{**arrays, **tables}], core_ids=[0])
    return r.results[0]["out"]
```

```python
from contextlib import ExitStack

import numpy as np

import concourse.bass as bass
from concourse import mybir

F32 = mybir.dt.float32
ALU = mybir.AluOpType
ACT = mybir.ActivationFunctionType
AX = mybir.AxisListType

P = 128
T = 512
META = 16
TM = T + META
HEAD_ROWS = 32
HALF = TM // 2
NT = T // P
D = 1024
KD = D // P
FF = 2816
KF = FF // P
WEIGHT_SLOTS = 4
SLOT = 2048
CREDIT = 64
NEG = -1e30


def cols(buf, start, width, rows=P, row0=0):
    if isinstance(start, int):
        return buf[row0:row0 + rows, start:start + width]
    return buf[row0:row0 + rows, bass.ds(start, width)]


def steps(eng, n, unroll):
    rounds = n // unroll
    if rounds > 1:
        with eng.Fori(0, rounds) as i:
            for u in range(unroll):
                yield i, i * unroll + u, u
    elif rounds == 1:
        for u in range(unroll):
            yield 0, u, u
    for u in range(n % unroll):
        yield rounds, rounds * unroll + u, u


class Signal:

    def __init__(self, handle, start):
        self.h = handle
        self.start = start

    def __call__(self, n):
        return self.h, self.start + n


class Semaphores:

    def __init__(self, nc, ctx, count):
        self.free = [[ctx.enter_context(nc.semaphore(f"stage_signal_{i}")), CREDIT] for i in range(count)]
        self.all = [h for h, _ in self.free]

    def take(self, total):
        entry = self.free.pop(0)
        signal = Signal(entry[0], entry[1])
        self.free.append([entry[0], entry[1] + total])
        return signal


class Chain:

    def __init__(self, eng, signal, before=0):
        self.eng, self.sem, self.before, self.n = eng, signal, before, 0

    def __call__(self, instruction, wait=True):
        self.n += 1
        instruction.then_inc(self.sem.h, 1)
        if wait:
            self.eng.wait_ge(*self.sem(self.before + self.n))


class Product:

    def __init__(self, stream, weights, kt, slots, columns, width, ksplit=1):
        self.stream, self.kt, self.slots, self.columns, self.width, self.ksplit = stream, kt, slots, columns, width, ksplit
        self.view = weights.rearrange("(k p) n -> p k n", p=P)
        self.parts = len(columns(0))
        self.first = stream.slots_planned
        self.loads = list(stream.loads)
        self.groups = slots // ksplit
        stream.slots_planned += slots
        for k in range(slots):
            s = (self.first + k) % WEIGHT_SLOTS
            stream.loads[s] += 16 * self.parts
        self.sent = 0
        stream.plans.append(self)

    def slot_of(self, u):
        return (self.first + u) % WEIGHT_SLOTS

    def slot(self, u):
        s = self.slot_of(u)
        return self.stream.ring[:, s * SLOT:s * SLOT + self.kt * self.width].rearrange("p (k n) -> p k n", n=self.width)

    def send(self, eng, i, k, u):
        eng.wait_ge(self.stream.used, CREDIT + self.first + k - WEIGHT_SLOTS + 1)
        group = k if self.ksplit == 1 else i * (WEIGHT_SLOTS // self.ksplit) + u // self.ksplit
        k0 = (u % self.ksplit) * self.kt
        for c0, width, column in self.columns(group):
            n = slice(column, column + width) if isinstance(column, int) else bass.ds(column, width)
            eng.dma_start(self.slot(u)[:, :, c0:c0 + width], self.view[:, k0:k0 + self.kt, n])\
               .then_inc(self.stream.full[self.slot_of(u)], 16)

    def send_first(self, eng):
        for k in range(min(WEIGHT_SLOTS, self.slots)):
            self.send(eng, k // WEIGHT_SLOTS, k, k)
            self.sent += 1

    def send_rest(self, eng):
        rounds = self.slots // WEIGHT_SLOTS
        if rounds > 2:
            with eng.Fori(1, rounds) as i:
                for u in range(WEIGHT_SLOTS):
                    self.send(eng, i, i * WEIGHT_SLOTS + u, u)
        elif rounds == 2:
            for u in range(WEIGHT_SLOTS):
                self.send(eng, 1, WEIGHT_SLOTS + u, u)
        for k in range(max(rounds, 1) * WEIGHT_SLOTS, self.slots):
            self.send(eng, k // WEIGHT_SLOTS, k, k % WEIGHT_SLOTS)

    def wait_full(self, pe, i, u):
        s = self.slot_of(u)
        pe.wait_ge(self.stream.full[s], CREDIT + self.loads[s] + (i + 1) * 16 * self.parts)

    def done(self, group):
        return self.stream.used, CREDIT + self.first + (group + 1) * self.ksplit


class WeightStream:

    def __init__(self, nc, ctx):
        self.ring = ctx.enter_context(nc.sbuf_tensor("weight_ring", [P, WEIGHT_SLOTS * SLOT], F32))
        self.full = [ctx.enter_context(nc.semaphore(f"weight_slot_full_{s}")) for s in range(WEIGHT_SLOTS)]
        self.used = ctx.enter_context(nc.semaphore("weight_slots_used"))
        self.loads = [0] * WEIGHT_SLOTS
        self.slots_planned = 0
        self.plans = []
        self.at = 0

    def run(self, eng, ahead=True):
        plan = self.plans[self.at]
        if self.at == 0:
            plan.send_first(eng)
        plan.send_rest(eng)
        self.at += 1
        if ahead:
            self.ahead(eng)

    def ahead(self, eng):
        if self.at < len(self.plans):
            self.plans[self.at].send_first(eng)


class Kernel:

    def __init__(self, nc, ctx):
        self.nc = nc
        self.sems = Semaphores(nc, ctx, 40)
        self.stream = WeightStream(nc, ctx)
        self.ps = ctx.enter_context(nc.psum_tensor("psum", [P, 8 * T], F32))
        self.ctx = ctx

    def bank(self, b, width=T, rows=P, at=0):
        return self.ps[0:rows, b * T + at:b * T + at + width]

    def sb(self, ctx, name, width, rows=P):
        return ctx.enter_context(self.nc.sbuf_tensor(name, [rows, width], F32))


def halves(K, pair, ct, rows=P):
    b = 4 * pair + 2 * ct
    return K.ps[0:rows, b * T:(b + 2) * T].rearrange("p (h n) -> p h n", n=T)[:, :, 0:HALF]


def split(ap):
    return ap.rearrange("p (h n) -> p h n", n=HALF)


def product_t(K, plan, src, stride, col_tiles, evacuated, meta=False, rows=P, banks=0, norm=None):
    def program(pe):
        per = WEIGHT_SLOTS // plan.ksplit
        for i, k, u in steps(pe, plan.slots, WEIGHT_SLOTS):
            part, pair = u % plan.ksplit, (u // plan.ksplit) % 2
            plan.wait_full(pe, i, u)
            if part == 0:
                for e in evacuated:
                    pe.wait_ge(*e(i * per + u // plan.ksplit - 1))
            for ct in range(col_tiles):
                for kt in range(plan.kt):
                    a = part * plan.kt + kt
                    if norm and u == 0 and ct == 0:
                        pe.wait_ge(*norm.scaled(kt + 1))
                    flags = dict(start=a == 0, stop=a == plan.kt * plan.ksplit - 1)
                    w = plan.slot(u)[:, kt, ct * P:ct * P + rows]
                    if meta:
                        for half in range(2):
                            at = a * stride + half * HALF
                            last = pe.matmul(K.bank(4 * pair + 2 * ct + half, HALF, rows), w, src[:, at:at + HALF], **flags)
                    else:
                        last = pe.matmul(K.bank(banks + 2 * pair + ct, rows=rows), w, src[:, a * stride:a * stride + T], **flags)
            last.then_inc(K.stream.used, 1)
    return program


def product_n(K, plan, src, stride, width, evacuated, meta=False):
    def program(pe):
        for i, k, u in steps(pe, plan.slots, WEIGHT_SLOTS):
            pair = u % 2
            plan.wait_full(pe, i, u)
            for e in evacuated:
                pe.wait_ge(*e(k - 1))
            for t in range(NT):
                for kt in range(plan.kt):
                    last = pe.matmul(K.bank(2 * pair + t // 2, width, P, (t % 2) * 256),
                                     src[:, kt * stride + t * P:kt * stride + (t + 1) * P],
                                     plan.slot(u)[:, kt, 0:width], start=kt == 0, stop=kt == plan.kt - 1)
            if meta:
                for kt in range(plan.kt):
                    last = pe.matmul(K.bank(4 + pair, width, META), src[:, kt * stride + T:kt * stride + TM],
                                     plan.slot(u)[:, kt, 0:width], start=kt == 0, stop=kt == plan.kt - 1)
            last.then_inc(K.stream.used, 1)
    return program


class RmsNorm:

    def __init__(self, K, x, out, stride, gain, eps, meta=False):
        self.K, self.x, self.out, self.stride, self.gain, self.eps = K, x, out, stride, gain, eps
        self.meta, self.width = meta, TM if meta else T

    def open(self, ctx):
        K = self.K
        self.squared = [K.sems.take(KD // 2), K.sems.take(KD // 2)]
        self.summed, self.shifted, self.rooted, self.inverted = (K.sems.take(1) for _ in range(4))
        self.scaled = K.sems.take(KD)
        self.r = K.sb(ctx, f"rms_scale_{K.nc.next_id()}", TM)

    def tile(self, buf, j):
        return buf[:, j * self.stride:j * self.stride + self.width]

    def scalar(self, act):
        act.activation(self.r[:, 0:1], self.K.ones[:, 0:1], ACT.Sqrt)
        for j in range(0, KD, 2):
            act.activation(self.tile(self.out, j), self.tile(self.x, j), ACT.Square).then_inc(self.squared[0].h, 1)
        act.wait_ge(*self.shifted(1))
        act.activation(self.r[:, 0:self.width], self.r[:, 0:self.width], ACT.Sqrt).then_inc(self.rooted.h, 1)

    def tensor(self, pe):
        K = self.K
        for j in range(KD):
            pe.wait_ge(*self.squared[j % 2](j // 2 + 1))
            square = self.tile(self.out, j)
            last = pe.matmul(K.bank(6), K.ones[:, :], square[:, 0:T], start=j == 0, stop=j == KD - 1)
            if self.meta:
                last = pe.matmul(K.bank(7, META), K.ones[:, :], square[:, T:TM], start=j == 0, stop=j == KD - 1)
        last.then_inc(self.summed.h, 1)

    def vector(self, dve):
        r = self.r[:, 0:self.width]
        for j in range(1, KD, 2):
            dve.tensor_tensor(self.tile(self.out, j), self.tile(self.x, j), self.tile(self.x, j), ALU.mult)\
               .then_inc(self.squared[1].h, 1)
        dve.wait_ge(*self.summed(1))
        dve.tensor_scalar(r, self.K.ps[:, 6 * T:6 * T + self.width], 1.0 / D, self.eps, ALU.mult, ALU.add).then_inc(self.shifted.h, 1)
        dve.wait_ge(*self.rooted(1))
        dve.reciprocal(r, r).then_inc(self.inverted.h, 1)
        dve.wait_ge(*self.inverted(1))
        for j in range(KD):
            dve.scalar_tensor_tensor(out=self.tile(self.out, j), in0=self.tile(self.x, j), scalar=self.gain(j), in1=r,
                                     op0=ALU.mult, op1=ALU.mult).then_inc(self.scaled.h, 1)


def rmsnorm_t(K, *args, **more):
    norm = RmsNorm(K, *args, **more)
    with ExitStack() as ctx:
        norm.open(ctx)
        block = ctx.enter_context(K.nc.Block())
        block.scalar(norm.scalar)
        block.tensor(norm.tensor)
        block.vector(norm.vector)


def swiglu(K, norm, u, stride, x, up, down, meta=False):
    nc = K.nc
    width = TM if meta else T
    silus, products = K.sems.take(up.groups), K.sems.take(up.groups)
    added = K.sems.take(down.groups)
    with ExitStack() as ctx:
        hidden = K.sb(ctx, f"ffn_hidden_{nc.next_id()}", KF * width)
        gated = K.sb(ctx, f"ffn_gate_{nc.next_id()}", 2 * width)
        norm.open(ctx)
        block = ctx.enter_context(nc.Block())

        @block.sync
        def _(sync):
            K.stream.run(sync)
            K.stream.run(sync)

        @block.tensor
        def _(pe):
            norm.tensor(pe)
            product_t(K, up, u, stride, 2, [products], meta, norm=norm)(pe)
            pe.wait_ge(*products(up.groups))
            product_t(K, down, hidden, width, 1, [added], meta)(pe)

        @block.scalar
        def _(act):
            norm.scalar(act)
            for i, k, s in steps(act, up.groups, WEIGHT_SLOTS):
                pair = s % 2
                act.wait_ge(*up.done(k))
                act.wait_ge(*products(k - 1))
                gate = gated[:, pair * width:(pair + 1) * width]
                if meta:
                    act.activation(split(gate), halves(K, pair, 0), ACT.Silu).then_inc(silus.h, 1)
                else:
                    act.activation(gate, K.bank(2 * pair), ACT.Silu).then_inc(silus.h, 1)

        @block.vector
        def _(dve):
            norm.vector(dve)
            for i, k, s in steps(dve, up.groups, WEIGHT_SLOTS):
                pair = s % 2
                dve.wait_ge(*silus(k + 1))
                gate, hidden_k = gated[:, pair * width:(pair + 1) * width], cols(hidden, k * width, width)
                if meta:
                    last = dve.tensor_tensor(split(hidden_k), split(gate), halves(K, pair, 1), ALU.mult)
                else:
                    last = dve.tensor_tensor(hidden_k, gate, K.bank(2 * pair + 1), ALU.mult)
                last.then_inc(products.h, 1)
            for i, k, s in steps(dve, down.groups, WEIGHT_SLOTS):
                pair = s % 2
                dve.wait_ge(*down.done(k))
                x_k = cols(x, k * stride, width)
                new = K.bank(2 * pair)
                if meta:
                    x_k, new = split(x_k), halves(K, pair, 0)
                dve.scalar_tensor_tensor(out=x_k, in0=new, scalar=0.5, in1=x_k, op0=ALU.mult, op1=ALU.add).then_inc(added.h, 1)


def head_norm_t(K, tiles, tables, eps):
    nc = K.nc
    n = len(tiles)
    metas = [k for k in range(n) if tiles[k][2]]
    full = TM if metas else T
    PLACES, BANK_SETS = 4, 3
    squared, summed, shifted, rooted = [K.sems.take(-(-n // 2)), K.sems.take(n // 2)], K.sems.take(n), K.sems.take(1), K.sems.take(1)
    inverse, spread, scaled, landed = K.sems.take(1), K.sems.take(n), K.sems.take(n), K.sems.take(32)
    with ExitStack() as ctx:
        sq = K.sb(ctx, f"head_squares_{nc.next_id()}", PLACES * TM)
        r = K.sb(ctx, f"head_scale_{nc.next_id()}", TM, HEAD_ROWS)
        gather = K.sb(ctx, f"head_gather_{nc.next_id()}", 2 * HEAD_ROWS - 2)
        scatter = K.sb(ctx, f"head_scatter_{nc.next_id()}", HEAD_ROWS // 2 * P, HEAD_ROWS)
        block = ctx.enter_context(nc.Block())

        def square_of(k):
            return sq[:, (k % PLACES) * TM:(k % PLACES) * TM + (TM if tiles[k][2] else T)]

        @block.sync
        def _(sync):
            sync.dma_start(gather[:, :], tables["head_gather"]).then_inc(landed.h, 16)
            sync.dma_start(scatter[:, :], tables["head_scatter"]).then_inc(landed.h, 16)

        @block.scalar
        def _(act):
            for k in range(0, n, 2):
                if k >= PLACES:
                    act.wait_ge(*summed(k - PLACES + 1))
                act.activation(square_of(k), tiles[k][0], ACT.Square).then_inc(squared[0].h, 1)
            act.wait_ge(*shifted(1))
            act.activation(r[:, 0:full], r[:, 0:full], ACT.Sqrt).then_inc(rooted.h, 1)

        @block.tensor
        def _(pe):
            pe.wait_ge(*landed(32))
            for k in range(n):
                pe.wait_ge(*squared[k % 2](k // 2 + 1))
                rows = gather[:, HEAD_ROWS - 2 - 2 * k:2 * HEAD_ROWS - 2 - 2 * k]
                square = square_of(k)
                last = pe.matmul(K.bank(0, T, HEAD_ROWS), rows, square[:, 0:T], start=k == 0, stop=k == n - 1)
                if k in metas:
                    last = pe.matmul(K.bank(1, META, HEAD_ROWS), rows, square[:, T:TM], start=k == metas[0], stop=k == metas[-1])
                last.then_inc(summed.h, 1)
            pe.wait_ge(*inverse(1))
            for k in range(n):
                bank = 2 + 2 * (k % BANK_SETS)
                if k >= BANK_SETS:
                    pe.wait_ge(*scaled(k - BANK_SETS + 1))
                w = scatter[:, k * P:(k + 1) * P]
                if k in metas:
                    for half in range(2):
                        last = pe.matmul(K.bank(bank + half, HALF), w, r[:, half * HALF:(half + 1) * HALF], start=True, stop=True)
                else:
                    last = pe.matmul(K.bank(bank), w, r[:, 0:T], start=True, stop=True)
                last.then_inc(spread.h, 1)

        @block.vector
        def _(dve):
            for k in range(1, n, 2):
                if k >= PLACES:
                    dve.wait_ge(*summed(k - PLACES + 1))
                dve.tensor_tensor(square_of(k), tiles[k][0], tiles[k][0], ALU.mult).then_inc(squared[1].h, 1)
            dve.wait_ge(*summed(n))
            dve.tensor_scalar(r[:, 0:full], K.ps[0:HEAD_ROWS, 0:full], 1.0 / 64, eps, ALU.mult, ALU.add).then_inc(shifted.h, 1)
            dve.wait_ge(*rooted(1))
            dve.reciprocal(r[:, 0:full], r[:, 0:full]).then_inc(inverse.h, 1)
            for k, (buf, gain, meta) in enumerate(tiles):
                dve.wait_ge(*spread(k + 1))
                bank = 2 + 2 * (k % BANK_SETS)
                scale = K.bank(bank)
                if meta:
                    scale = K.ps[:, bank * T:(bank + 2) * T].rearrange("p (h n) -> p h n", n=T)[:, :, 0:HALF]
                    buf = split(buf)
                dve.scalar_tensor_tensor(out=buf, in0=buf, scalar=gain, in1=scale, op0=ALU.mult, op1=ALU.mult).then_inc(scaled.h, 1)


def load_vectors(K, rows):
    nc = K.nc
    total = sum(n for _, _, n in rows)
    tiles = -(-total // P)
    K.vectors = K.sb(K.ctx, "vector_columns", tiles * P)
    K.column = {}
    pieces, at = [], 0
    for name, src, n in rows:
        K.column[name] = at
        done = 0
        while done < n:
            take = min(n - done, P - at % P)
            pieces.append((at // P, at % P, src[done:done + take, :], take))
            done += take
            at += take
    landed, cleared, turned = K.sems.take(16 * len(pieces)), K.sems.take(1), K.sems.take(1)
    with ExitStack() as ctx:
        rows_sb = K.sb(ctx, "vector_rows", tiles * P)
        block = ctx.enter_context(nc.Block())

        @block.sync
        def _(sync):
            sync.wait_ge(*cleared(1))
            for t, r, src, n in pieces:
                sync.dma_start(rows_sb[r:r + n, t * P:(t + 1) * P], src).then_inc(landed.h, 16)

        @block.tensor
        def _(pe):
            pe.wait_ge(*landed(16 * len(pieces)))
            for t in range(tiles):
                last = pe.transpose(K.bank(t // 4, P, P, (t % 4) * P), rows_sb[:, t * P:(t + 1) * P], K.ident[:, :])
            last.then_inc(turned.h, 1)

        @block.vector
        def _(dve):
            dve.memset(rows_sb[:, :], 0.0).then_inc(cleared.h, 1)
            dve.wait_ge(*turned(1))
            dve.tensor_copy(K.vectors[:, :], K.ps[:, 0:tiles * P])


def vector(K, name):
    return lambda j=0: cols(K.vectors, K.column[name] + j, 1)


def load_x(K, x, meta, buf, stride):
    nc = K.nc
    landed, turned, copied = K.sems.take(32), K.sems.take(KD), K.sems.take(KD)
    with ExitStack() as ctx:
        rows = K.sb(ctx, "x_rows", NT * D)
        meta_rows = K.sb(ctx, "meta_rows", D, META)
        block = ctx.enter_context(nc.Block())

        @block.sync
        def _(sync):
            sync.dma_start(rows[:, :].rearrange("p (t d) -> p t d", d=D), x.rearrange("(t p) d -> p t d", p=P))\
                .then_inc(landed.h, 16)
            sync.dma_start(meta_rows[:, :], meta).then_inc(landed.h, 16)

        @block.tensor
        def _(pe):
            pe.wait_ge(*landed(32))
            for j in range(KD):
                pe.wait_ge(*copied(j - 1))
                b = 2 * (j % 2)
                for t in range(NT):
                    pe.transpose(K.bank(b, P, P, t * P), rows[:, t * D + j * P:t * D + (j + 1) * P], K.ident[:, :])
                pe.transpose(K.bank(b + 1, META), meta_rows[:, j * P:(j + 1) * P], K.ident[0:META, 0:META])\
                    .then_inc(turned.h, 1)

        @block.vector
        def _(dve):
            for j in range(KD):
                dve.wait_ge(*turned(j + 1))
                dve.tensor_copy(buf[:, j * stride:j * stride + TM], K.ps[:, 2 * (j % 2) * T:2 * (j % 2) * T + TM])\
                   .then_inc(copied.h, 1)


def turn_tokens(K, src, dst, tiles, place=None):
    place = place or (lambda t, j: (t * tiles + j) * P)
    nc = K.nc
    turned, copied = K.sems.take(tiles), K.sems.take(tiles)
    with ExitStack() as ctx:
        block = ctx.enter_context(nc.Block())

        @block.tensor
        def _(pe):
            for j in range(tiles):
                pe.wait_ge(*copied(j - 1))
                for t in range(NT):
                    last = pe.transpose(K.bank(j % 2, P, P, t * P),
                                        src[:, place(t, j):place(t, j) + P], K.ident[:, :])
                last.then_inc(turned.h, 1)

        @block.vector
        def _(dve):
            for j in range(tiles):
                dve.wait_ge(*turned(j + 1))
                dve.tensor_copy(dst[:, j * T:(j + 1) * T], K.bank(j % 2)).then_inc(copied.h, 1)


def project_t(K, plan, src, stride, dst, dst_stride, meta=False, func=None, bias=None, rows=P, col_tiles=2,
              ring_follows=True, norm=None):
    nc = K.nc
    read = K.sems.take(plan.groups)
    with ExitStack() as ctx:
        if norm:
            norm.open(ctx)
        block = ctx.enter_context(nc.Block())

        @block.sync
        def _(sync):
            K.stream.run(sync, ring_follows)

        @block.tensor
        def _(pe):
            if norm:
                norm.tensor(pe)
            product_t(K, plan, src, stride, col_tiles, [read], meta, rows, norm=norm)(pe)

        if norm:
            block.vector(norm.vector)

        @block.scalar
        def _(act):
            if norm:
                norm.scalar(act)
            for i, k, u in steps(act, plan.groups, WEIGHT_SLOTS):
                pair = u % 2
                act.wait_ge(*plan.done(k))
                for ct in range(col_tiles):
                    t = k * col_tiles + ct
                    more = {} if bias is None else dict(bias=bias(t))
                    f = ACT.Copy if func is None else func
                    if meta:
                        last = act.activation(split(cols(dst, t * dst_stride, TM, rows)), halves(K, pair, ct, rows), f, **more)
                    else:
                        last = act.activation(cols(dst, t * dst_stride, T, rows), K.bank(2 * pair + ct, rows=rows), f, **more)
                last.then_inc(read.h, 1)


def project_n(K, plan, src, stride, dst, width, total, meta_dst=None, func=None):
    nc = K.nc
    read = K.sems.take(plan.groups)
    with ExitStack() as ctx:
        block = ctx.enter_context(nc.Block())

        @block.sync
        def _(sync):
            K.stream.run(sync)

        @block.tensor
        def _(pe):
            product_n(K, plan, src, stride, width, [read], meta_dst is not None)(pe)

        @block.scalar
        def _(act):
            for i, k, u in steps(act, plan.groups, WEIGHT_SLOTS):
                pair = u % 2
                act.wait_ge(*plan.done(k))
                for t in range(NT):
                    last = act.activation(cols(dst, k * width + t * total, width),
                                          K.bank(2 * pair + t // 2, width, P, (t % 2) * 256), func or ACT.Copy)
                if meta_dst is not None:
                    last = act.activation(cols(meta_dst, k * width, width, META), K.bank(4 + pair, width, META), ACT.Copy)
                last.then_inc(read.h, 1)


def add_product(K, plan, src, stride, x, x_stride):
    nc = K.nc
    added = K.sems.take(plan.groups)
    with ExitStack() as ctx:
        block = ctx.enter_context(nc.Block())

        @block.sync
        def _(sync):
            K.stream.run(sync)

        @block.tensor
        def _(pe):
            product_t(K, plan, src, stride, 2, [added])(pe)

        @block.vector
        def _(dve):
            for i, k, u in steps(dve, plan.groups, WEIGHT_SLOTS):
                dve.wait_ge(*plan.done(k))
                for ct in range(2):
                    x_t = cols(x, (k * 2 + ct) * x_stride, T)
                    last = dve.tensor_tensor(x_t, x_t, K.bank(2 * (u % 2) + ct), ALU.add)
                last.then_inc(added.h, 1)


def gated_sum(K, plan_a, src_a, plan_b, src_b, gates, bias):
    nc = K.nc
    gate_a, gate_b = gates[:, 0:KD * T], gates[:, KD * T:2 * KD * T]
    opened = K.sems.take(2 * KD)
    first, weighed, summed = K.sems.take(plan_a.groups), K.sems.take(plan_b.groups), K.sems.take(plan_b.groups)
    with ExitStack() as ctx:
        block = ctx.enter_context(nc.Block())

        @block.sync
        def _(sync):
            K.stream.run(sync)
            K.stream.run(sync)

        @block.tensor
        def _(pe):
            product_t(K, plan_a, src_a, T, 2, [first])(pe)
            pe.wait_ge(*first(plan_a.groups))
            product_t(K, plan_b, src_b, T, 2, [weighed])(pe)

        @block.scalar
        def _(act):
            for t in range(2 * KD):
                g = gates[:, t * T:(t + 1) * T]
                act.activation(g, g, ACT.Sigmoid, bias=bias(t)).then_inc(opened.h, 1)

        @block.vector
        def _(dve):
            for i, k, u in steps(dve, plan_a.groups, WEIGHT_SLOTS):
                dve.wait_ge(*plan_a.done(k))
                dve.wait_ge(*opened(2 * k + 2))
                for ct in range(2):
                    g = cols(gate_a, (k * 2 + ct) * T, T)
                    last = dve.tensor_tensor(g, g, K.bank(2 * (u % 2) + ct), ALU.mult)
                last.then_inc(first.h, 1)
            for i, k, u in steps(dve, plan_b.groups, WEIGHT_SLOTS):
                dve.wait_ge(*plan_b.done(k))
                dve.wait_ge(*opened(KD + 2 * k + 2))
                for ct in range(2):
                    g = cols(gate_b, (k * 2 + ct) * T, T)
                    last = dve.tensor_tensor(g, g, K.bank(2 * (u % 2) + ct), ALU.mult)
                last.then_inc(weighed.h, 1)
                dve.wait_ge(*weighed(k + 1))
                dve.wait_ge(*first(plan_a.groups))
                for ct in range(2):
                    a, b = cols(gate_a, (k * 2 + ct) * T, T), cols(gate_b, (k * 2 + ct) * T, T)
                    last = dve.tensor_tensor(a, a, b, ALU.add)
                last.then_inc(summed.h, 1)


FOX_HEADS = 16
RET_HEADS = 4
RET_DK = 128
RET_DV = 256


def forget_sums(K, plan, u, bias, ncB):
    nc = K.nc
    own, act_own = K.sems.take(6), K.sems.take(2)
    picked, spread, copied = K.sems.take(FOX_HEADS), K.sems.take(FOX_HEADS), K.sems.take(FOX_HEADS)
    bias_landed = K.sems.take(16)
    H = FOX_HEADS
    with ExitStack() as ctx:
        z, m, a, sums, ones_row = (K.sb(ctx, f"forget_{n}", TM, H) for n in ("z", "max", "abs", "sums", "one"))
        b = K.sb(ctx, "forget_bias", 1, H)
        row = K.sb(ctx, "forget_row", 2 * TM, H)
        block = ctx.enter_context(nc.Block())

        @block.sync
        def _(sync):
            sync.dma_start(b[:, :], bias.rearrange("(h a) -> h a", a=1)).then_inc(bias_landed.h, 16)
            K.stream.run(sync)

        @block.tensor
        def _(pe):
            product_t(K, plan, u, TM, 1, [], True, H)(pe)
            for h in range(H):
                pe.wait_ge(*picked(h + 1))
                pe.wait_ge(*copied(h - 1))
                bank = 2 * (h % 2)
                pe.matmul(K.bank(bank), K.ones[0:H, :], row[:, (h % 2) * TM:(h % 2) * TM + T], start=True, stop=True)
                pe.matmul(K.bank(bank + 1, META), K.ones[0:H, :], row[:, (h % 2) * TM + T:(h % 2 + 1) * TM],
                          start=True, stop=True).then_inc(spread.h, 1)

        @block.vector
        def _(dve):
            chain = Chain(dve, own)
            dve.wait_ge(*plan.done(0))
            dve.wait_ge(*bias_landed(16))
            dve.tensor_scalar(z[:, META:META + HALF], K.bank(0, HALF, H), b[:, 0:1], -1.0, ALU.add, ALU.mult)
            dve.tensor_scalar(z[:, META + HALF:TM], K.bank(1, HALF - META, H), b[:, 0:1], -1.0, ALU.add, ALU.mult)
            chain(dve.tensor_scalar(z[:, 0:META], K.bank(1, META, H, HALF - META), b[:, 0:1], -1.0, ALU.add, ALU.mult))
            chain(dve.tensor_scalar(m[:, :], z[:, :], 0.0, None, ALU.max))
            chain(dve.memset(ones_row[:, :], 1.0))
            chain(dve.scalar_tensor_tensor(out=a[:, :], in0=m[:, :], scalar=-2.0, in1=z[:, :], op0=ALU.mult, op1=ALU.add))
            dve.wait_ge(*act_own(2))
            chain(dve.tensor_tensor(m[:, :], m[:, :], a[:, :], ALU.add))
            chain(dve.tensor_tensor_scan(sums[:, :], ones_row[:, :], m[:, :], 0.0, ALU.mult, ALU.add))
            for h in range(H):
                dve.wait_ge(*spread(h - 1))
                dve.tensor_scalar(row[:, (h % 2) * TM:(h % 2 + 1) * TM], sums[:, :], K.ident[0:H, h:h + 1], None, ALU.mult)\
                   .then_inc(picked.h, 1)

        @block.scalar
        def _(act):
            act.wait_ge(*own(4))
            act.activation(a[:, :], a[:, :], ACT.Exp).then_inc(act_own.h, 1)
            act.wait_ge(*act_own(1))
            act.activation(a[:, :], a[:, :], ACT.Ln, bias=1.0).then_inc(act_own.h, 1)
            for h in range(H):
                act.wait_ge(*spread(h + 1))
                b0 = 2 * (h % 2) * T
                act.activation(ncB[:, h * TM:(h + 1) * TM], K.ps[:, b0:b0 + TM], ACT.Copy).then_inc(copied.h, 1)


def fox_attention(K, q, k, v, v_meta, ncB, side, side_src, side_dst):
    nc = K.nc
    PAIRS = FOX_HEADS // 2
    ROUND, QK_PLACES = 4, 2
    rounds = PAIRS // ROUND
    S = [(a, h, i) for a in range(ROUND) for h in range(2) for i in range(NT)]
    n = len(S)
    PAIR_STEPS, SIDE_STEPS = n // ROUND, n // WEIGHT_SLOTS
    HALF_SLOT = SIDE_STEPS // 2
    SIDE_SHARES = [range(0, 3), range(3, 6), range(6, KD), ()]
    assert side.slots == rounds * WEIGHT_SLOTS and HALF_SLOT == len(SIDE_SHARES)
    side_first, side_read = K.sems.take(side.slots), K.sems.take(2 * side.slots)
    q_staged, k_staged = K.sems.take(PAIRS), K.sems.take(PAIRS)
    scored, probs, turned, turned_copied, weighed, out = (K.sems.take(rounds * n) for _ in range(6))
    score_steps, recips = K.sems.take(rounds * n * 3), K.sems.take(rounds * n)
    with ExitStack() as ctx:
        qs = [K.sb(ctx, f"fox_q_{a}", T) for a in range(QK_PLACES)]
        ks = [K.sb(ctx, f"fox_k_{a}", TM) for a in range(QK_PLACES)]
        L = [K.sb(ctx, f"fox_scores_{a}", TM) for a in range(3)]
        pt = [K.sb(ctx, f"fox_probs_t_{a}", T) for a in range(2)]
        pt_meta = [K.sb(ctx, f"fox_probs_t_meta_{a}", P, META) for a in range(2)]
        stat = [K.sb(ctx, f"fox_stat_{a}", 4) for a in range(4)]
        block = ctx.enter_context(nc.Block())
        def score_at(b):
            return (2 * b + 1) * T - META

        @block.sync
        def _(sync):
            K.stream.run(sync)

        @block.gpsimd
        def _(pool):
            with pool.Fori(0, rounds) as r:
                for a in range(ROUND):
                    pair = r * ROUND + a
                    pool.wait_ge(*scored((pair - 1) * PAIR_STEPS))
                    pool.tensor_copy(ks[a % QK_PLACES][:, :], cols(k, pair * TM, TM)).then_inc(k_staged.h, 1)

        @block.tensor
        def _(pe):
            def side_step(r, s):
                f, ct, part = s // SIDE_STEPS, s % SIDE_STEPS // HALF_SLOT, s % HALF_SLOT
                if s % SIDE_STEPS == 0:
                    side.wait_full(pe, r, f)
                if part == 0:
                    pe.wait_ge(*side_read(r * 2 * WEIGHT_SLOTS + s // HALF_SLOT))
                for kt in SIDE_SHARES[part]:
                    last = pe.matmul(K.bank(7), side.slot(f)[:, kt, ct * P:(ct + 1) * P], side_src[:, kt * TM:kt * TM + T],
                                     start=kt == 0, stop=kt == KD - 1)
                    if kt == KD - 1:
                        last.then_inc(*((K.stream.used, 1) if ct else (side_first.h, 1)))

            with pe.Fori(0, rounds) as r:
                for s in range(n + 3):
                    if s < n:
                        a, h, i = S[s]
                        b = s % 2
                        q_a, k_a = qs[a % QK_PLACES], ks[a % QK_PLACES]
                        if h == 0 and i == 0:
                            pe.wait_ge(*q_staged(r * ROUND + a + 1))
                            pe.wait_ge(*k_staged(r * ROUND + a + 1))
                        pe.wait_ge(*score_steps((r * n + s - 2) * 3 + 1))
                        rows = slice(64 * h, 64 * h + 64)
                        lhs = q_a[rows, i * P:(i + 1) * P]
                        pe.matmul(K.ps[:, score_at(b):score_at(b) + META], lhs, k_a[rows, T:TM], start=True, stop=True)
                        pe.matmul(K.bank(2 * b + 1, (i + 1) * P), lhs, k_a[rows, 0:(i + 1) * P], start=True, stop=True)\
                            .then_inc(scored.h, 1)
                        side_step(r, s)
                    if 2 <= s < n + 2:
                        done = s - 2
                        _, _, i = S[done]
                        Ls = L[done % 3]
                        pe.wait_ge(*probs(r * n + done + 1))
                        pe.wait_ge(*turned_copied(r * n + done))
                        pe.transpose(K.bank(5, P, META), Ls[:, 0:META], K.ident[:, :])
                        for t in range(i + 1):
                            last = pe.transpose(K.bank(4, P, P, t * P), Ls[:, META + t * P:META + (t + 1) * P], K.ident[:, :])
                        last.then_inc(turned.h, 1)
                    if s >= 3:
                        a, h, i = S[s - 3]
                        b = (s - 3) % 2
                        head = ((r * ROUND + a) * 2 + h) * 64
                        pe.wait_ge(*turned_copied(r * n + s - 2))
                        pe.wait_ge(*out(r * n + s - 3))
                        o = K.bank(6, 64)
                        for t in range(i + 1):
                            pe.matmul(o, pt[b][:, t * P:(t + 1) * P], cols(v, head + t * D, 64), start=t == 0, stop=False)
                        pe.matmul(o, pt_meta[b][:, :], cols(v_meta, head, 64, META), start=False, stop=True)\
                            .then_inc(weighed.h, 1)

        @block.vector
        def _(dve):
            with dve.Fori(0, rounds) as r:
                for s in range(n + 3):
                    if s < n:
                        a, h, i = S[s]
                        b, Ls, st = s % 2, L[s % 3], stat[s % 4]
                        w = META + (i + 1) * P
                        head = (r * ROUND + a) * 2 + h
                        chain = Chain(dve, score_steps, (r * n + s) * 3)
                        dve.wait_ge(*scored(r * n + s + 1))
                        dve.wait_ge(*turned(r * n + s - 2))
                        chain(dve.scalar_tensor_tensor(out=Ls[:, 0:w], in0=K.ps[:, score_at(b):score_at(b) + w],
                                                       scalar=64 ** -0.5, in1=cols(ncB, head * TM, w), op0=ALU.mult, op1=ALU.add))
                        diag = Ls[:, w - P:w]
                        chain(dve.tensor_tensor(diag, diag, K.causal[:, :], ALU.add))
                        chain(dve.tensor_reduce(st[:, 0:1], Ls[:, 0:w], AX.X, ALU.max, negate=True))
                    if s >= 3:
                        a, h, i = S[s - 3]
                        b, st = (s - 3) % 2, stat[(s - 3) % 4]
                        dve.wait_ge(*weighed(r * n + s - 2))
                        dve.reciprocal(st[:, 2:3], st[:, 1:2]).then_inc(recips.h, 1)
                        dve.wait_ge(*recips(r * n + s - 2))
                        dve.tensor_scalar(cols(q, (r * ROUND + a) * T + (i * P + h * 64), 64), K.bank(6, 64),
                                          st[:, 2:3], None, ALU.mult).then_inc(out.h, 1)

        @block.scalar
        def _(act):
            with act.Fori(0, rounds) as r:
                def stage_q(a):
                    pair = r * ROUND + a
                    act.wait_ge(*scored((pair - 1) * PAIR_STEPS))
                    act.activation(qs[a % QK_PLACES][:, :], cols(q, pair * T, T), ACT.Copy).then_inc(q_staged.h, 1)

                def read_side(e):
                    f, ct = e // 2, e % 2
                    if ct:
                        act.wait_ge(*side.done(r * WEIGHT_SLOTS + f))
                    else:
                        act.wait_ge(*side_first(r * WEIGHT_SLOTS + f + 1))
                    act.activation(cols(side_dst, (r * 2 * WEIGHT_SLOTS + e) * T, T), K.bank(7), ACT.Copy).then_inc(side_read.h, 1)

                stage_q(0)
                for s in range(n + 2):
                    if s >= 2:
                        _, _, i = S[s - 2]
                        b = (s - 2) % 2
                        act.wait_ge(*turned(r * n + s - 1))
                        act.wait_ge(*weighed(r * n + s - 3))
                        act.activation(pt_meta[b][:, :], K.bank(5, P, META), ACT.Copy)
                        act.activation(pt[b][:, 0:(i + 1) * P], K.bank(4, (i + 1) * P), ACT.Copy).then_inc(turned_copied.h, 1)
                    if s < n and s % HALF_SLOT == HALF_SLOT - 1:
                        read_side(s // HALF_SLOT)
                    if s < n:
                        if s % PAIR_STEPS == 2 and s // PAIR_STEPS + 1 < ROUND:
                            stage_q(s // PAIR_STEPS + 1)
                        Ls, w, st = L[s % 3], META + (S[s][2] + 1) * P, stat[s % 4]
                        act.wait_ge(*score_steps((r * n + s) * 3 + 3))
                        act.activation(Ls[:, 0:w], Ls[:, 0:w], ACT.Exp, bias=st[:, 0:1], accum_out=st[:, 1:2]).then_inc(probs.h, 1)


def retention(K, q, k, v, v_meta, y, tables, gate, gate_src):
    nc = K.nc
    H = RET_HEADS
    swapped, rotated, turned, scaled = K.sems.take(H), K.sems.take(H), K.sems.take(H), K.sems.take(H)
    scored, decayed, states, stated, out, normed, turned_y = (K.sems.take(H) for _ in range(7))
    own_n = 20
    own, rooted, gated = K.sems.take(H * own_n), K.sems.take(H), K.sems.take(H)
    loaded, gate_first, opened = K.sems.take(16 * 7), K.sems.take(H), K.sems.take(H)
    with ExitStack() as ctx:
        cos, sin = K.sb(ctx, "rope_cos", TM), K.sb(ctx, "rope_sin", TM)
        swap = K.sb(ctx, "rope_swap", P)
        decay = K.sb(ctx, "ret_decay", H * P)
        xi = K.sb(ctx, "ret_xi", H * P)
        zeta = K.sb(ctx, "ret_zeta", 3 * H)
        qs, qx, t1 = K.sb(ctx, "ret_q", T), K.sb(ctx, "ret_q_xi", T), K.sb(ctx, "ret_tmp", TM)
        ks, kz = K.sb(ctx, "ret_k", TM), K.sb(ctx, "ret_k_zeta", T)
        kz_meta = K.sb(ctx, "ret_k_zeta_meta", P, META)
        st = K.sb(ctx, "ret_scores", T)
        R = K.sb(ctx, "ret_state", NT * RET_DV)
        yn = K.sb(ctx, "ret_normed", NT * RET_DV)
        stats, mv, rstd = K.sb(ctx, "ret_stats", 6 * NT + 2), K.sb(ctx, "ret_mean_var", 2 * NT), K.sb(ctx, "ret_rstd", NT)
        block = ctx.enter_context(nc.Block())

        @block.sync
        def _(sync):
            for dst, name in ((cos, "rope_cos"), (sin, "rope_sin"), (swap, "swap"), (decay, "decay"), (xi, "xi")):
                sync.dma_start(dst[:, :], tables[name]).then_inc(loaded.h, 16)
            sync.dma_start(zeta[:, 0:2 * H], tables["zeta"]).then_inc(loaded.h, 16)
            sync.dma_start(zeta[0:META, 2 * H:3 * H], tables["zeta_meta"]).then_inc(loaded.h, 16)
            K.stream.run(sync)

        @block.tensor
        def _(pe):
            pe.wait_ge(*loaded(16 * 7))
            def gate_tile(h, ct):
                for kt in range(KD):
                    last = pe.matmul(K.bank(3 - ct), gate.slot(h)[:, kt, ct * P:(ct + 1) * P],
                                     gate_src[:, kt * TM:kt * TM + T], start=kt == 0, stop=kt == KD - 1)
                last.then_inc(*((K.stream.used, 1) if ct else (gate_first.h, 1)))

            for h in range(H):
                pe.wait_ge(*gated(h))
                pe.matmul(K.bank(0), swap[:, :], cols(q, h * T, T), start=True, stop=True)
                pe.matmul(K.bank(1), swap[:, :], cols(k, h * TM, T), start=True, stop=True)
                pe.matmul(K.bank(2, META), swap[:, :], cols(k, h * TM + T, META), start=True, stop=True)\
                    .then_inc(swapped.h, 1)
                pe.wait_ge(*rotated(h + 1))
                for c in range(NT):
                    pe.transpose(K.bank(3, P, P, c * P), ks[:, c * P:(c + 1) * P], K.ident[:, :])
                pe.transpose(K.bank(2, P, META, P), ks[:, T:TM], K.ident[:, :]).then_inc(turned.h, 1)
                for c in range(NT):
                    last = pe.matmul(K.bank(0, P, P, c * P), ks[:, c * P:(c + 1) * P], qs[:, c * P:(c + 1) * P],
                                     start=True, stop=True)
                last.then_inc(scored.h, 1)
                pe.wait_ge(*scaled(h + 1))
                for c in range(NT - 1):
                    pe.matmul(K.bank(4 + (c + 1) // 2, RET_DV, P, (c + 1) % 2 * RET_DV), kz[:, c * P:(c + 1) * P],
                              cols(v, c * D + h * RET_DV, RET_DV), start=True, stop=True)
                pe.matmul(K.bank(4, RET_DV), kz_meta[:, :], cols(v_meta, h * RET_DV, RET_DV, META), start=True, stop=True)\
                    .then_inc(states.h, 1)
                gate.wait_full(pe, 0, h)
                gate_tile(h, 0)
                pe.wait_ge(*decayed(h + 1))
                pe.wait_ge(*stated(h + 1))
                for c in range(NT):
                    o = K.bank(6 + c // 2, RET_DV, P, c % 2 * RET_DV)
                    pe.matmul(o, st[:, c * P:(c + 1) * P], cols(v, c * D + h * RET_DV, RET_DV), start=True, stop=False)
                    last = pe.matmul(o, qx[:, c * P:(c + 1) * P], R[:, c * RET_DV:(c + 1) * RET_DV], start=False, stop=True)
                last.then_inc(out.h, 1)
                gate_tile(h, 1)
                pe.wait_ge(*normed(h + 1))
                for e in range(2):
                    for c in range(NT):
                        last = pe.transpose(K.bank(e, P, P, c * P), yn[:, c * RET_DV + e * P:c * RET_DV + (e + 1) * P], K.ident[:, :])
                last.then_inc(turned_y.h, 1)

        @block.scalar
        def _(act):
            with act.Fori(0, H) as h:
                act.wait_ge(*turned(h + 1))
                act.wait_ge(*loaded(16 * 7))
                act.activation(kz[:, :], K.bank(3), ACT.Copy, scale=cols(zeta, h, 1))
                act.activation(kz_meta[:, :], K.bank(2, P, META, P), ACT.Copy, scale=cols(zeta, 2 * H + h, 1, META))\
                   .then_inc(scaled.h, 1)
                act.wait_ge(*gate_first(h + 1))
                act.activation(cols(y, h * 2 * T, T), K.bank(3), ACT.Silu)
                act.wait_ge(*own(h * own_n + 19))
                act.activation(rstd[:, :], rstd[:, :], ACT.Sqrt).then_inc(rooted.h, 1)
                act.wait_ge(*gate.done(h))
                act.activation(cols(y, (h * 2 + 1) * T, T), K.bank(2), ACT.Silu).then_inc(opened.h, 1)

        @block.vector
        def _(dve):
            dve.wait_ge(*loaded(16 * 7))
            with dve.Fori(0, H) as h:
                chain = Chain(dve, own, h * own_n)
                dve.wait_ge(*swapped(h + 1))
                chain(dve.tensor_tensor(t1[:, 0:T], K.bank(0), sin[:, 0:T], ALU.mult))
                chain(dve.tensor_tensor(qs[:, :], cols(q, h * T, T), cos[:, 0:T], ALU.mult))
                chain(dve.tensor_tensor(qs[:, :], qs[:, :], t1[:, 0:T], ALU.add))
                chain(dve.tensor_tensor(t1[:, :], K.ps[:, T:2 * T + META], sin[:, :], ALU.mult))
                chain(dve.tensor_tensor(ks[:, :], cols(k, h * TM, TM), cos[:, :], ALU.mult))
                chain(dve.tensor_tensor(ks[:, :], ks[:, :], t1[:, :], ALU.add))
                chain(dve.tensor_scalar(ks[:, :], ks[:, :], RET_DK ** -0.5, None, ALU.mult))
                qx3 = qx[:, :].rearrange("p (c n) -> p c n", n=P)
                qs3 = qs[:, :].rearrange("p (c n) -> p c n", n=P)
                xi_h = cols(xi, h * P, P).unsqueeze(1).to_broadcast([P, NT, P])
                dve.tensor_tensor(qx3, qs3, xi_h, ALU.mult).then_inc(rotated.h, 1)
                dve.wait_ge(*scored(h + 1))
                decay_h = cols(decay, h * P, P).unsqueeze(1).to_broadcast([P, NT, P])
                dve.tensor_tensor(st[:, :].rearrange("p (c n) -> p c n", n=P),
                                  K.bank(0).rearrange("p (c n) -> p c n", n=P), decay_h, ALU.mult).then_inc(decayed.h, 1)
                dve.wait_ge(*states(h + 1))
                chain(dve.tensor_copy(R[:, 0:RET_DV], K.bank(4, RET_DV)))
                for c in range(1, NT):
                    ins = dve.scalar_tensor_tensor(out=R[:, c * RET_DV:(c + 1) * RET_DV], in0=R[:, (c - 1) * RET_DV:c * RET_DV],
                                                   scalar=cols(zeta, H + h, 1),
                                                   in1=K.bank(4 + c // 2, RET_DV, P, c % 2 * RET_DV), op0=ALU.mult, op1=ALU.add)
                    if c < NT - 1:
                        chain(ins)
                ins.then_inc(stated.h, 1)
                dve.wait_ge(*out(h + 1))
                for c in range(NT):
                    chain(dve.bn_stats(stats[:, 6 * c:6 * c + 6], K.bank(6 + c // 2, RET_DV, P, c % 2 * RET_DV)), c == NT - 1)
                dve.memset(stats[:, 6 * NT:6 * NT + 1], 0.0)
                for c in range(NT):
                    chain(dve.bn_aggr(mv[:, 2 * c:2 * c + 2], stats[:, 6 * c:6 * c + 6]), c == NT - 1)
                chain(dve.tensor_scalar(rstd[:, :], mv[:, 1:2 * NT:2], 1e-5, None, ALU.add))
                dve.wait_ge(*rooted(h + 1))
                chain(dve.reciprocal(rstd[:, :], rstd[:, :]))
                for c in range(NT):
                    ins = dve.tensor_scalar(yn[:, c * RET_DV:(c + 1) * RET_DV], K.bank(6 + c // 2, RET_DV, P, c % 2 * RET_DV),
                                            mv[:, 2 * c:2 * c + 1], rstd[:, c:c + 1], ALU.subtract, ALU.mult)
                ins.then_inc(normed.h, 1)
                dve.wait_ge(*turned_y(h + 1))
                dve.wait_ge(*opened(h + 1))
                for e in range(2):
                    g = cols(y, (h * 2 + e) * T, T)
                    ins = dve.scalar_tensor_tensor(out=g, in0=K.bank(e), scalar=vector(K, "ret_gn")(h * 2 + e), in1=g,
                                                   op0=ALU.mult, op1=ALU.mult)
                ins.then_inc(gated.h, 1)


def convolve(dve, chain, acc, src, taps, bias):
    chain(dve.tensor_scalar(acc, src, taps[0], bias, ALU.mult, ALU.add))
    for s in range(1, len(taps)):
        chain(dve.scalar_tensor_tensor(out=acc[:, s:T], in0=src[:, 0:T - s], scalar=taps[s], in1=acc[:, s:T],
                                       op0=ALU.mult, op1=ALU.add))


def project_conv_t(K, plan, src, stride, dst, taps, name_w, name_b, tiles):
    nc = K.nc
    convolved, read = K.sems.take(plan.groups * 2 * taps), K.sems.take(plan.groups)
    per = 2 * taps
    with ExitStack() as ctx:
        acc = K.sb(ctx, f"conv_{nc.next_id()}", 4 * T)
        block_ = ctx.enter_context(nc.Block())

        @block_.sync
        def _(sync):
            K.stream.run(sync)

        @block_.tensor
        def _(pe):
            product_t(K, plan, src, stride, 2, [lambda k: convolved(k * per)])(pe)

        @block_.vector
        def _(dve):
            for i, k, u in steps(dve, plan.groups, WEIGHT_SLOTS):
                dve.wait_ge(*plan.done(k))
                dve.wait_ge(*read(k - 1))
                chain = Chain(dve, convolved, k * per)
                for ct in range(2):
                    t = 2 * k + ct
                    w = [vector(K, name_w)((taps - 1 - s) * tiles + t) for s in range(taps)]
                    a = (u % 2) * 2 + ct
                    convolve(dve, chain, acc[:, a * T:(a + 1) * T], K.bank(a), w, vector(K, name_b)(t))

        @block_.scalar
        def _(act):
            for i, k, u in steps(act, plan.groups, WEIGHT_SLOTS):
                act.wait_ge(*convolved((k + 1) * per))
                for ct in range(2):
                    a = (u % 2) * 2 + ct
                    last = act.activation(cols(dst, (2 * k + ct) * T, T), acc[:, a * T:(a + 1) * T], ACT.Silu)
                last.then_inc(read.h, 1)


def conv_swiglu(K, norm, u, stride, x, up, down, name_w, name_b, gate_first):
    nc = K.nc
    taps, per = 3, 6
    convolved, silus = K.sems.take(up.groups * per), K.sems.take(up.groups)
    products, added = K.sems.take(up.groups), K.sems.take(down.groups)
    with ExitStack() as ctx:
        hidden = K.sb(ctx, f"ffn_hidden_{nc.next_id()}", KF * T)
        acc = K.sb(ctx, f"ffn_conv_{nc.next_id()}", 4 * T)
        norm.open(ctx)
        block_ = ctx.enter_context(nc.Block())

        @block_.sync
        def _(sync):
            K.stream.run(sync)
            K.stream.run(sync)

        @block_.tensor
        def _(pe):
            norm.tensor(pe)
            product_t(K, up, u, stride, 2, [lambda k: convolved(k * per)], norm=norm)(pe)
            pe.wait_ge(*products(up.groups))
            product_t(K, down, hidden, T, 1, [added])(pe)

        @block_.vector
        def _(dve):
            norm.vector(dve)

            def multiply(k, pair):
                dve.wait_ge(*silus(k + 1))
                dve.tensor_tensor(cols(hidden, k * T, T), acc[:, pair * 2 * T:(pair * 2 + 1) * T],
                                  acc[:, (pair * 2 + 1) * T:(pair * 2 + 2) * T], ALU.mult).then_inc(products.h, 1)
            for i, k, s in steps(dve, up.groups, WEIGHT_SLOTS):
                pair = s % 2
                dve.wait_ge(*up.done(k))
                dve.wait_ge(*products(k - 1))
                chain = Chain(dve, convolved, k * per)
                for ct in range(2):
                    t = k + ct * KF if gate_first else k + (1 - ct) * KF
                    w = [vector(K, name_w)((taps - 1 - n) * 2 * KF + t) for n in range(taps)]
                    a = pair * 2 + ct
                    convolve(dve, chain, acc[:, a * T:(a + 1) * T], K.bank(a), w, vector(K, name_b)(t))
                multiply(k, pair)
            for i, k, s in steps(dve, down.groups, WEIGHT_SLOTS):
                dve.wait_ge(*down.done(k))
                x_k = cols(x, k * stride, T)
                dve.tensor_tensor(x_k, x_k, K.bank(2 * (s % 2)), ALU.add).then_inc(added.h, 1)

        @block_.scalar
        def _(act):
            norm.scalar(act)
            for i, k, s in steps(act, up.groups, WEIGHT_SLOTS):
                a = (s % 2) * 2
                act.wait_ge(*convolved((k + 1) * per))
                act.activation(acc[:, a * T:(a + 1) * T], acc[:, a * T:(a + 1) * T], ACT.Silu).then_inc(silus.h, 1)


def weigh(K, plan, src, gate, total=None):
    nc = K.nc
    weighed = K.sems.take(plan.groups)
    with ExitStack() as ctx:
        block_ = ctx.enter_context(nc.Block())

        @block_.sync
        def _(sync):
            K.stream.run(sync)

        @block_.tensor
        def _(pe):
            product_t(K, plan, src, T, 2, [weighed])(pe)

        @block_.vector
        def _(dve):
            for i, k, u in steps(dve, plan.groups, WEIGHT_SLOTS):
                dve.wait_ge(*plan.done(k))
                for ct in range(2):
                    g = cols(gate, (k * 2 + ct) * T, T)
                    last = dve.tensor_tensor(g, g, K.bank(2 * (u % 2) + ct), ALU.mult)
                last.then_inc(weighed.h, 1)
                if total is not None:
                    dve.wait_ge(*weighed(k + 1))
                    for ct in range(2):
                        a, b = cols(total, (k * 2 + ct) * T, T), cols(gate, (k * 2 + ct) * T, T)
                        dve.tensor_tensor(a, a, b, ALU.add)


GMLP_GROUPS = 8


def spatial_gate(K, v, gu, ws, ln_w, ln_b, bs):
    nc = K.nc
    G = GMLP_GROUPS
    loaded, turned_w, masked = K.sems.take(16 * 4), K.sems.take(1), K.sems.take(2)
    N = NT * G
    measured, rooted, centred = K.sems.take(4), K.sems.take(1), K.sems.take(2 * G)
    normed, mixed, gated, biased = K.sems.take(G), K.sems.take(G), K.sems.take(G), K.sems.take(G)
    with ExitStack() as ctx:
        w_rows, w_t = K.sb(ctx, "gmlp_w", G * P), K.sb(ctx, "gmlp_w_t", G * P)
        gain, bias, token_bias = (K.sb(ctx, f"gmlp_{n}", G * P) for n in ("gain", "bias", "token_bias"))
        vn = [K.sb(ctx, f"gmlp_normed_{u}", NT * P) for u in range(2)]
        mix = K.sb(ctx, "gmlp_mixed", NT * P)
        stats, mv, rstd = K.sb(ctx, "gmlp_stats", 6 * N + 2), K.sb(ctx, "gmlp_mean_var", 2 * N), K.sb(ctx, "gmlp_rstd", N)
        block_ = ctx.enter_context(nc.Block())

        @block_.sync
        def _(sync):
            sync.dma_start(w_rows[:, :].rearrange("t (g s) -> t g s", s=P), ws.rearrange("g t s -> t g s")).then_inc(loaded.h, 16)
            for dst, src in ((gain, ln_w), (bias, ln_b), (token_bias, bs)):
                sync.dma_start(dst[:, :], src.rearrange("g n -> (g n)").partition_broadcast(P)).then_inc(loaded.h, 16)

        @block_.tensor
        def _(pe):
            pe.wait_ge(*loaded(16 * 4))
            for g in range(G):
                last = pe.transpose(K.bank(g // 4, P, P, (g % 4) * P), w_rows[:, g * P:(g + 1) * P], K.ident[:, :])
            last.then_inc(turned_w.h, 1)
            pe.wait_ge(*masked(2))
            with pe.Fori(0, G // 2) as i:
                for u in range(2):
                    g = i * 2 + u
                    pe.wait_ge(*normed(g + 1))
                    pe.wait_ge(*biased(g - 1))
                    for t in range(NT):
                        last = pe.matmul(K.bank(2 + u, P, P, t * P), vn[u][:, t * P:(t + 1) * P], cols(w_t, g * P, P), start=True, stop=True)
                    last.then_inc(mixed.h, 1)

        @block_.scalar
        def _(act):
            act.wait_ge(*measured(3))
            act.activation(rstd[:, :], rstd[:, :], ACT.Sqrt).then_inc(rooted.h, 1)

        @block_.vector
        def _(dve):
            dve.wait_ge(*turned_w(1))
            dve.tensor_copy(w_t[:, :], K.ps[:, 0:G * P]).then_inc(masked.h, 1)
            dve.wait_ge(*masked(1))
            dve.memset(w_t[64:P, :].rearrange("s (g t) -> s g t", t=P)[:, :, 0:64], 0.0).then_inc(masked.h, 1)
            dve.wait_ge(*loaded(16 * 4))
            measure = Chain(dve, measured)
            for n in range(N):
                last = dve.bn_stats(stats[:, 6 * n:6 * n + 6], v[:, n * P:(n + 1) * P])
            measure(last)
            dve.memset(stats[:, 6 * N:6 * N + 1], 0.0)
            for n in range(N):
                last = dve.bn_aggr(mv[:, 2 * n:2 * n + 2], stats[:, 6 * n:6 * n + 6])
            measure(last)
            measure(dve.tensor_scalar(rstd[:, :], mv[:, 1:2 * N:2], 1e-5, None, ALU.add), False)
            dve.wait_ge(*rooted(1))
            measure(dve.reciprocal(rstd[:, :], rstd[:, :]))

            def tiles(buf):
                return buf.rearrange("p (t n) -> p t n", n=P)

            def every_tile(row, g):
                return cols(row, g * P, P).unsqueeze(1).to_broadcast([P, NT, P])

            def normalize(g, u):
                vn3 = tiles(vn[u][:, :])
                dve.wait_ge(*mixed(g - 1))
                chain = Chain(dve, centred, g * 2)
                for t in range(NT):
                    last = dve.tensor_scalar(vn[u][:, t * P:(t + 1) * P], cols(v, t * D + g * P, P), cols(mv, (g + t * G) * 2, 1),
                                             cols(rstd, g + t * G, 1), ALU.subtract, ALU.mult)
                chain(last)
                chain(dve.tensor_tensor(vn3, vn3, every_tile(gain, g), ALU.mult))
                dve.tensor_tensor(vn3, vn3, every_tile(bias, g), ALU.add).then_inc(normed.h, 1)

            def gate(g, u):
                dve.wait_ge(*mixed(g + 1))
                dve.wait_ge(*gated(g))
                dve.tensor_tensor(tiles(mix[:, :]), tiles(K.bank(2 + u)), every_tile(token_bias, g), ALU.add).then_inc(biased.h, 1)
                dve.wait_ge(*biased(g + 1))
                gu_g = cols(gu, g * T, T)
                dve.tensor_tensor(gu_g, gu_g, mix[:, :], ALU.mult).then_inc(gated.h, 1)
            normalize(0, 0)
            with dve.Fori(0, G // 2 - 1) as i:
                for a in range(2):
                    normalize(i * 2 + (a + 1), (a + 1) % 2)
                    gate(i * 2 + a, a)
            normalize(G - 1, 1)
            gate(G - 2, 0)
            gate(G - 1, 1)


SSM_HEADS = 32
SSM_GROUPS = 4
SSM_PAIRS = SSM_HEADS // 2


def ssm_times(K, plan, u, dt_bias, a_log, acum, acum_n, dt_n, end_n, chunk_starts):
    nc = K.nc
    H = SSM_HEADS
    loaded, own, act_own, turned = K.sems.take(16 * 3), K.sems.take(12), K.sems.take(4), K.sems.take(1)
    with ExitStack() as ctx:
        z, m, dt, starts = (K.sb(ctx, f"ssm_{n}", T, H) for n in ("dt_raw", "dt_max", "dt", "starts"))
        small = K.sb(ctx, "ssm_head_values", 4, H)
        ends = K.sb(ctx, "ssm_chunk_ends", NT * P, H)
        block_ = ctx.enter_context(nc.Block())

        @block_.sync
        def _(sync):
            sync.dma_start(small[:, 0:1], dt_bias.rearrange("(h a) -> h a", a=1)).then_inc(loaded.h, 16)
            sync.dma_start(small[:, 1:2], a_log.rearrange("(h a) -> h a", a=1)).then_inc(loaded.h, 16)
            sync.dma_start(starts[:, :], chunk_starts[0:H, :]).then_inc(loaded.h, 16)
            K.stream.run(sync)

        @block_.tensor
        def _(pe):
            product_t(K, plan, u, TM, 1, [], False, H)(pe)
            pe.wait_ge(*own(10))
            for c in range(NT):
                tok = slice(c * P, (c + 1) * P)
                pe.transpose(K.bank(1, H, P, c * H), acum[:, tok], K.ident[0:H, 0:H])
                pe.transpose(K.bank(2, H, P, c * H), dt[:, tok], K.ident[0:H, 0:H])
                last = pe.matmul(K.bank(3, H, P, c * H), ends[:, tok], K.ident[0:H, 0:H], start=True, stop=True)
            last.then_inc(turned.h, 1)

        @block_.scalar
        def _(act):
            act.wait_ge(*loaded(16 * 3))
            act.activation(small[:, 2:3], small[:, 1:2], ACT.Exp).then_inc(act_own.h, 1)
            act.wait_ge(*own(3))
            act.activation(dt[:, :], dt[:, :], ACT.Exp).then_inc(act_own.h, 1)
            act.wait_ge(*act_own(2))
            act.activation(dt[:, :], dt[:, :], ACT.Ln, bias=1.0).then_inc(act_own.h, 1)
            act.wait_ge(*own(12))
            act.activation(end_n[:, :], end_n[:, :], ACT.Exp).then_inc(act_own.h, 1)

        @block_.vector
        def _(dve):
            chain = Chain(dve, own)
            dve.wait_ge(*loaded(16 * 3))
            dve.wait_ge(*plan.done(0))
            chain(dve.tensor_scalar(z[:, :], K.bank(0, rows=H), small[:, 0:1], None, ALU.add))
            chain(dve.tensor_scalar(m[:, :], z[:, :], 0.0, None, ALU.max))
            chain(dve.scalar_tensor_tensor(out=dt[:, :], in0=m[:, :], scalar=-2.0, in1=z[:, :], op0=ALU.mult, op1=ALU.add))
            dve.wait_ge(*act_own(3))
            chain(dve.tensor_tensor(dt[:, :], dt[:, :], m[:, :], ALU.add))
            chain(dve.tensor_scalar(z[:, :], dt[:, :], small[:, 2:3], -1.0, ALU.mult, ALU.mult))
            chain(dve.tensor_tensor_scan(acum[:, :], starts[:, :], z[:, :], 0.0, ALU.mult, ALU.add))
            for c in range(NT):
                chain(dve.tensor_scalar(ends[:, c * P:(c + 1) * P], K.ones[0:H, :], acum[:, (c + 1) * P - 1:(c + 1) * P],
                                        None, ALU.mult))
            dve.wait_ge(*turned(1))
            chain(dve.tensor_copy(acum_n[:, :], K.bank(1, NT * H)))
            dve.tensor_copy(dt_n[:, :], K.bank(2, NT * H))
            chain(dve.tensor_tensor(end_n[:, :], K.bank(3, NT * H), acum_n[:, :], ALU.subtract))
            dve.wait_ge(*act_own(4))
            dve.tensor_tensor(end_n[:, :], end_n[:, :], dt_n[:, :], ALU.mult)


def ssm_groups(K, bt, ct, bn, cbm, mask):
    nc = K.nc
    G = SSM_GROUPS
    turned, copied, masked, loaded = (K.sems.take(n) for n in (G, G, G, 16))
    with ExitStack() as ctx:
        m = K.sb(ctx, "ssm_causal", P)
        block_ = ctx.enter_context(nc.Block())

        @block_.sync
        def _(sync):
            sync.dma_start(m[:, :], mask).then_inc(loaded.h, 16)

        @block_.tensor
        def _(pe):
            for g in range(G):
                pe.wait_ge(*copied(g - 1))
                pe.wait_ge(*masked(g - 1))
                for c in range(NT):
                    tok = slice(g * T + c * P, g * T + (c + 1) * P)
                    pe.matmul(K.bank(2 + g % 2, P, P, c * P), bt[:, tok], ct[:, tok], start=True, stop=True)
                    last = pe.transpose(K.bank(g % 2, P, P, c * P), bt[:, tok], K.ident[:, :])
                last.then_inc(turned.h, 1)

        @block_.scalar
        def _(act):
            for g in range(G):
                act.wait_ge(*turned(g + 1))
                act.activation(bn[:, g * T:(g + 1) * T], K.bank(g % 2), ACT.Copy).then_inc(copied.h, 1)

        @block_.vector
        def _(dve):
            dve.wait_ge(*loaded(16))
            for g in range(G):
                dve.wait_ge(*turned(g + 1))
                dve.tensor_tensor(cbm[:, g * T:(g + 1) * T].rearrange("p (c n) -> p c n", n=P),
                                  K.bank(2 + g % 2).rearrange("p (c n) -> p c n", n=P),
                                  m[:, :].unsqueeze(1).to_broadcast([P, NT, P]), ALU.mult).then_inc(masked.h, 1)


def ssm_scan(K, xs, z, bn, cbm, ct, acum, acum_n, dt_n, end_n, d_skip):
    nc = K.nc
    H, NP = SSM_HEADS, SSM_PAIRS
    (picked, staged, b_staged, spread, turned, exps, floored, decays, carried, aged, states, stated, weighted, out, summed, done) = \
        (K.sems.take(NP) for _ in range(16))
    own = K.sems.take(NP * 2)
    loaded = K.sems.take(16)
    with ExitStack() as ctx:
        room = [0]

        def in_ring(width):
            room[0] += width
            return K.stream.ring[:, room[0] - width:room[0]]
        seg, E, ce = ([in_ring(2 * T) for _ in range(2)] for _ in range(3))
        x, b = ([in_ring(T) for _ in range(2)] for _ in range(2))
        xd, xe, y = ([K.sb(ctx, f"ssm_{n}_{u}", T) for u in range(2)] for n in ("x_dt", "x_end", "y_pair"))
        pick = [K.sb(ctx, f"ssm_pick_{u}", 2 * P, H) for u in range(2)]
        R = K.sb(ctx, "ssm_state", (NT - 1) * P)
        d, d_heads = K.sb(ctx, "ssm_skip", NP), K.sb(ctx, "ssm_skip_heads", H)
        block_ = ctx.enter_context(nc.Block())

        def pairs(eng, first, count):
            with eng.Fori(0, count // 2) as i:
                for a in range(2):
                    yield i * 2 + (first + a), (first + a) % 2

        @block_.sync
        def _(sync):
            sync.dma_start(d_heads[:, :], d_skip.partition_broadcast(P)).then_inc(loaded.h, 16)

        @block_.gpsimd
        def _(pool):
            def stage_b(j, u):
                pool.wait_ge(*states(j - 1))
                pool.tensor_copy(b[u], cols(bn, (j // 4) * T, T)).then_inc(b_staged.h, 1)

            def gate(j, u):
                pool.wait_ge(*summed(j + 1))
                z_j = cols(z, j * T, T)
                pool.tensor_tensor(z_j, z_j, y[u][:, :], ALU.mult).then_inc(done.h, 1)
            stage_b(0, 0)
            for j, u in pairs(pool, 1, NP - 2):
                stage_b(j, u)
                gate(j - 1, 1 - u)
            stage_b(NP - 1, 1)
            gate(NP - 2, 0)
            gate(NP - 1, 1)

        @block_.tensor
        def _(pe):
            def front(j, u):
                pe.wait_ge(*picked(j + 1))
                pe.wait_ge(*exps(j - 1))
                pe.wait_ge(*floored(j - 1))
                for h in range(2):
                    last = pe.matmul(K.bank(3 * u + h), pick[u][:, h * P:(h + 1) * P], acum[:, :], start=True, stop=True)
                last.then_inc(spread.h, 1)
                pe.wait_ge(*staged(j + 1))
                pe.wait_ge(*carried(j - 1))
                for c in range(NT):
                    last = pe.transpose(K.bank(3 * u + 2, P, P, c * P), x[u][:, c * P:(c + 1) * P], K.ident[:, :])
                last.then_inc(turned.h, 1)

            def chunk_states(j, u):
                pe.wait_ge(*carried(j + 1))
                pe.wait_ge(*b_staged(j + 1))
                pe.wait_ge(*stated(j))
                for c in range(NT - 1):
                    last = pe.matmul(K.bank(6, P, P, c * P), b[u][:, c * P:(c + 1) * P], xe[u][:, c * P:(c + 1) * P],
                                     start=True, stop=True)
                last.then_inc(states.h, 1)

            def outputs(j, u):
                pe.wait_ge(*summed(j))
                pe.wait_ge(*stated(j + 1))
                pe.wait_ge(*aged(j + 1))
                pe.wait_ge(*weighted(j + 1))
                for h in range(2):
                    rows = slice(64 * h, 64 * h + 64)
                    for c in range(NT):
                        o = K.ps[rows, 7 * T + c * P:7 * T + (c + 1) * P]
                        last = pe.matmul(o, xd[u][:, c * P + 64 * h:c * P + 64 * h + 64], seg[u][:, h * T + c * P:h * T + (c + 1) * P],
                                         start=True, stop=c == 0)
                        if c:
                            last = pe.matmul(o, R[:, (c - 1) * P + 64 * h:(c - 1) * P + 64 * h + 64],
                                             ce[u][:, h * T + c * P:h * T + (c + 1) * P], start=False, stop=True)
                last.then_inc(out.h, 1)
            front(0, 0)
            for j, u in pairs(pe, 0, NP - 2):
                chunk_states(j, u)
                front(j + 1, 1 - u)
                outputs(j, u)
            chunk_states(NP - 2, 0)
            front(NP - 1, 1)
            outputs(NP - 2, 0)
            chunk_states(NP - 1, 1)
            outputs(NP - 1, 1)

        @block_.scalar
        def _(act):
            for j, u in pairs(act, 0, NP):
                act.wait_ge(*spread(j - 1))
                act.wait_ge(*turned(j - 1))
                act.activation(pick[u][:, :].rearrange("p (h n) -> p h n", n=P),
                               cols(K.ident, j * 2, 2, H).unsqueeze(2).to_broadcast([H, 2, P]), ACT.Copy).then_inc(picked.h, 1)
                act.activation(x[u], cols(xs, j * T, T), ACT.Copy).then_inc(staged.h, 1)
                act.wait_ge(*spread(j + 1))
                act.wait_ge(*stated(j - 1))
                act.activation(E[u], K.ps[:, 3 * u * T:(3 * u + 2) * T], ACT.Exp).then_inc(exps.h, 1)
                act.wait_ge(*out(j - 1))
                for h in range(2):
                    for c in range(NT):
                        last = act.activation(seg[u][:, h * T + c * P:h * T + (c + 1) * P], K.bank(3 * u + h, P, P, c * P),
                                              ACT.Relu, bias=cols(acum_n, c * H + j * 2 + h, 1), scale=-1.0)
                last.then_inc(floored.h, 1)
                act.wait_ge(*floored(j + 1))
                act.activation(seg[u], seg[u], ACT.Exp, scale=-1.0).then_inc(decays.h, 1)

        @block_.vector
        def _(dve):
            def factors(j, u):
                dve.wait_ge(*turned(j + 1))
                dve.wait_ge(*out(j - 1))
                for dst, src in ((xd[u], dt_n), (xe[u], end_n)):
                    by_head = src[:, :].rearrange("p (c h) -> p c h", h=H)[:, :, bass.ds(j * 2, 2)].unsqueeze(3).to_broadcast([P, NT, 2, 64])
                    last = dve.tensor_tensor(dst[:, :].rearrange("p (c h n) -> p c h n", h=2, n=64),
                                             K.bank(3 * u + 2).rearrange("p (c h n) -> p c h n", h=2, n=64), by_head, ALU.mult)
                last.then_inc(carried.h, 1)
                dve.wait_ge(*exps(j + 1))
                for h in range(2):
                    last = dve.tensor_tensor(ce[u][:, h * T:(h + 1) * T], E[u][:, h * T:(h + 1) * T], cols(ct, (j // 4) * T, T), ALU.mult)
                last.then_inc(aged.h, 1)

            def state_and_scores(j, u):
                chain = Chain(dve, own, j * 2)
                dve.wait_ge(*states(j + 1))
                dve.wait_ge(*out(j))
                chain(dve.tensor_copy(R[:, 0:P], K.bank(6, P)))
                for c in range(1, NT - 1):
                    for h in range(2):
                        a, b_ = c * P + 64 * h, (c - 1) * P + 64 * h
                        last = dve.scalar_tensor_tensor(out=R[:, a:a + 64], in0=R[:, b_:b_ + 64],
                                                        scalar=E[u][:, h * T + (c + 1) * P - 1:h * T + (c + 1) * P],
                                                        in1=K.bank(6, 64, P, a), op0=ALU.mult, op1=ALU.add)
                    if c == 1:
                        chain(last)
                last.then_inc(stated.h, 1)
                dve.wait_ge(*decays(j + 1))
                for h in range(2):
                    last = dve.tensor_tensor(seg[u][:, h * T:(h + 1) * T], seg[u][:, h * T:(h + 1) * T], cols(cbm, (j // 4) * T, T), ALU.mult)
                last.then_inc(weighted.h, 1)

            def output(j, u):
                dve.wait_ge(*out(j + 1))
                dve.wait_ge(*done(j - 1))
                dve.scalar_tensor_tensor(out=y[u][:, :], in0=cols(xs, j * T, T), scalar=cols(d, j, 1), in1=K.bank(7),
                                         op0=ALU.mult, op1=ALU.add).then_inc(summed.h, 1)
            dve.wait_ge(*loaded(16))
            for a in range(2):
                last = dve.tensor_copy(d[64 * a:64 * a + 64, :], d_heads[64 * a:64 * a + 64, a:H:2])
            factors(0, 0)
            state_and_scores(0, 0)
            for j, u in pairs(dve, 1, NP - 2):
                factors(j, u)
                state_and_scores(j, u)
                output(j - 1, 1 - u)
            factors(NP - 1, 1)
            state_and_scores(NP - 1, 1)
            output(NP - 2, 0)
            output(NP - 1, 1)


def group_norm_t(K, buf, groups, tiles, gain, eps):
    nc = K.nc
    n = groups * tiles
    squared, shifted, rooted = K.sems.take(n), K.sems.take(groups), K.sems.take(groups)
    own = K.sems.take(groups)
    with ExitStack() as ctx:
        sq = K.sb(ctx, f"group_squares_{nc.next_id()}", 2 * T)
        r = K.sb(ctx, f"group_scale_{nc.next_id()}", groups * T)
        block_ = ctx.enter_context(nc.Block())
        added = K.sems.take(n)

        @block_.sync
        def _(sync):
            K.stream.ahead(sync)

        @block_.scalar
        def _(act):
            for t in range(n):
                act.wait_ge(*added(t - 1))
                act.activation(sq[:, (t % 2) * T:(t % 2 + 1) * T], buf[:, t * T:(t + 1) * T], ACT.Square).then_inc(squared.h, 1)
            for g in range(groups):
                act.wait_ge(*shifted(g + 1))
                act.activation(r[:, g * T:(g + 1) * T], r[:, g * T:(g + 1) * T], ACT.Sqrt).then_inc(rooted.h, 1)

        @block_.tensor
        def _(pe):
            for t in range(n):
                g = t // tiles
                pe.wait_ge(*squared(t + 1))
                if t % tiles == 0:
                    pe.wait_ge(*shifted(g - 1))
                pe.matmul(K.bank(g % 2), K.ones[:, :], sq[:, (t % 2) * T:(t % 2 + 1) * T], start=t % tiles == 0,
                          stop=t % tiles == tiles - 1).then_inc(added.h, 1)

        @block_.vector
        def _(dve):
            for g in range(groups):
                dve.wait_ge(*added((g + 1) * tiles))
                dve.tensor_scalar(r[:, g * T:(g + 1) * T], K.bank(g % 2), 1.0 / (tiles * P), eps, ALU.mult, ALU.add)\
                   .then_inc(shifted.h, 1)
            for g in range(groups):
                dve.wait_ge(*rooted(g + 1))
                dve.reciprocal(r[:, g * T:(g + 1) * T], r[:, g * T:(g + 1) * T]).then_inc(own.h, 1)
                dve.wait_ge(*own(g + 1))
                for t in range(g * tiles, (g + 1) * tiles):
                    b = buf[:, t * T:(t + 1) * T]
                    dve.scalar_tensor_tensor(out=b, in0=b, scalar=gain(t), in1=r[:, g * T:(g + 1) * T], op0=ALU.mult, op1=ALU.mult)


def second_block(K, d, tables, X, U, plans):
    V = lambda name: vector(K, name)
    H = SSM_HEADS
    with ExitStack() as mix:
        merged = K.sb(mix, "merged", KD * T)
        project_t(K, plans["gate_a2"], U, TM, merged, T, func=ACT.Sigmoid, bias=V("gate_bias_2"),
                  norm=RmsNorm(K, X, U, TM, V("mix_norm_w_2"), 1e-5))
        with ExitStack() as gmlp:
            gu, gv = K.sb(gmlp, "gmlp_u", KD * T), K.sb(gmlp, "gmlp_v", NT * D)
            project_t(K, plans["gmlp_u"], U, TM, gu, T, func=ACT.Gelu_apprx_tanh)
            project_n(K, plans["gmlp_v"], U, TM, gv, 256, D, func=ACT.Gelu_apprx_tanh)
            spatial_gate(K, gv, gu, d["gmlp_ws_2"][0], d["gmlp_ln_w_2"][0], d["gmlp_ln_b_2"][0], d["gmlp_bs_2"][0])
            weigh(K, plans["w_proj_a"], gu, merged)
        z = K.sb(mix, "ssm_z", 2 * KD * T)
        with ExitStack() as ssm:
            xbc = K.sb(ssm, "ssm_xbc", 3 * KD * T)
            acum = K.sb(ssm, "ssm_sums", T, H)
            acum_n, dt_n, end_n = (K.sb(ssm, f"ssm_{n}_n", NT * H) for n in ("sums", "dt", "end"))
            project_conv_t(K, plans["xbc"], U, TM, xbc, 4, "ssm_conv_w_2", "ssm_conv_b_2", 3 * KD)
            ssm_times(K, plans["dt"], U, d["ssm_dt_bias_2"][0], d["ssm_a_log_2"][0], acum, acum_n, dt_n, end_n, tables["starts"])
            project_t(K, plans["ssm_z"], U, TM, z, T, func=ACT.Silu, ring_follows=False)
            bt, ct = xbc[:, 16 * T:20 * T], xbc[:, 20 * T:24 * T]
            cbm = K.sb(ssm, "ssm_cb", 4 * T)
            bn = bt
            ssm_groups(K, bt, ct, bn, cbm, tables["causal01"])
            ssm_scan(K, xbc, z, bn, cbm, ct, acum, acum_n, dt_n, end_n, d["ssm_d_2"][0])
        group_norm_t(K, z, SSM_GROUPS, 4, V("ssm_norm_w_2"), 1e-5)
        gate_b = K.sb(mix, "gate_b2", KD * T)
        project_t(K, plans["gate_b2"], U, TM, gate_b, T, func=ACT.Sigmoid, bias=lambda t: V("gate_bias_2")(t + KD))
        weigh_wide(K, plans["w_proj_b"], z, gate_b, merged)
        add_product(K, plans["w_out2"], merged, T, X, TM)
    conv_swiglu(K, RmsNorm(K, X, U, TM, V("ffn_norm_w_2"), 1e-5), U, TM, X, plans["ffn_up2"], plans["ffn_down2"], "ffn_conv_w_2", "ffn_conv_b_2", True)
    rmsnorm_t(K, X, U, TM, V("final_norm_w_2"), 1e-5)


def weigh_wide(K, plan, src, gate, total):
    nc = K.nc
    weighed = K.sems.take(plan.groups)
    with ExitStack() as ctx:
        block_ = ctx.enter_context(nc.Block())

        @block_.sync
        def _(sync):
            K.stream.run(sync)

        @block_.tensor
        def _(pe):
            product_t(K, plan, src, T, 2, [weighed])(pe)

        @block_.vector
        def _(dve):
            for g in range(plan.groups):
                dve.wait_ge(*plan.done(g))
                a = slice(2 * g * T, 2 * (g + 1) * T)
                dve.tensor_tensor(gate[:, a], gate[:, a], K.ps[:, 2 * (g % 2) * T:2 * (g % 2 + 1) * T], ALU.mult).then_inc(weighed.h, 1)
                dve.wait_ge(*weighed(g + 1))
                dve.tensor_tensor(total[:, a], total[:, a], gate[:, a], ALU.add)


NSA_HEADS = 8
NSA_GROUPS = 2
CMP_BLOCK = 32
CMP_STRIDE = 16
CMP = (T - CMP_BLOCK) // CMP_STRIDE + 1
BUCKETS = 32
BIAS_W = 3 * P + T
HEAD = 64


def distance_bias(K, rel_bias, onehot, flip, scratch, table):
    nc = K.nc
    H, L = NSA_HEADS, 2 * T
    N = H * BIAS_W // T
    filled, loaded, made, copied, stored, landed, flipped, placed = (K.sems.take(n) for n in (1, 48, 1, 1, 16, 16, N, N))
    with ExitStack() as ctx:
        b = K.sb(ctx, "nsa_bucket_bias", H, BUCKETS + 1)
        hot = K.sb(ctx, "nsa_onehot", L, BUCKETS + 1)
        line = K.sb(ctx, "nsa_distance_bias", L, H)
        reverse, order = K.sb(ctx, "nsa_bias_reversed", H * BIAS_W), K.sb(ctx, "partition_flip", P)
        block_ = ctx.enter_context(nc.Block())

        @block_.sync
        def _(sync):
            sync.wait_ge(*filled(1))
            sync.dma_start(b[0:BUCKETS, :], rel_bias).then_inc(loaded.h, 16)
            sync.dma_start(hot[:, :], onehot).then_inc(loaded.h, 16)
            sync.dma_start(order[:, :], flip).then_inc(loaded.h, 16)
            sync.wait_ge(*copied(1))
            sync.dma_start(scratch, line[:, :]).then_inc(stored.h, 16)
            sync.wait_ge(*stored(16))
            sync.dma_start(reverse[:, :].rearrange("p (h m) -> p h m", m=BIAS_W),
                           bass.AP(scratch.tensor, 0, [[1, P], [L, H], [1, BIAS_W]])).then_inc(landed.h, 16)

        @block_.tensor
        def _(pe):
            pe.wait_ge(*loaded(48))
            for half in range(2):
                last = pe.matmul(K.bank(half, rows=H), b[:, :], hot[:, half * T:(half + 1) * T], start=True, stop=True)
            last.then_inc(made.h, 1)
            pe.wait_ge(*landed(16))
            for n in range(N):
                pe.wait_ge(*placed(n - 1))
                pe.matmul(K.bank(2 + n % 2), order[:, :], reverse[:, n * T:(n + 1) * T], start=True, stop=True).then_inc(flipped.h, 1)

        @block_.vector
        def _(dve):
            dve.memset(b[:, :], NEG).then_inc(filled.h, 1)
            dve.wait_ge(*made(1))
            dve.tensor_copy(line[:, :], K.ps[0:H, 0:L]).then_inc(copied.h, 1)
            for n in range(N):
                dve.wait_ge(*flipped(n + 1))
                dve.tensor_copy(table[:, n * T:(n + 1) * T], K.bank(2 + n % 2)).then_inc(placed.h, 1)


def compress(K, kv, kc, vc, pos, w1, w2, b2, eps, gain):
    nc = K.nc
    G = NSA_GROUPS
    M = P
    loaded = K.sems.take(16 * 12)
    turned, placed, posted, hidden, active, second, biased, squared, summed, rooted = (
        K.sems.take(n) for n in (1, 2, 2, 2, 2, 1, 1, 1, 1, 1))
    own = K.sems.take(2)
    with ExitStack() as ctx:
        w1s = K.sb(ctx, "cmp_w1", 2 * CMP_BLOCK * M)
        w2s = K.sb(ctx, "cmp_w2", 2 * P)
        rows, post = K.sb(ctx, "cmp_pos_rows", 2 * P, CMP_BLOCK), K.sb(ctx, "cmp_pos", 2 * CMP_BLOCK)
        blk = K.sb(ctx, "cmp_blocks", 2 * CMP_BLOCK * G * CMP)
        hid = K.sb(ctx, "cmp_hidden", 4 * CMP)
        bv = K.sb(ctx, "cmp_bias_v", HEAD, CMP)
        sq, r = K.sb(ctx, "cmp_squares", G * CMP), K.sb(ctx, "cmp_scale", G * CMP)
        block_ = ctx.enter_context(nc.Block())

        @block_.sync
        def _(sync):
            for i in range(2):
                w = w1[i].rearrange("(j d) m -> d j m", d=HEAD)
                for half in range(2):
                    sync.dma_start(w1s[64 * half:64 * half + 64, i * CMP_BLOCK * M:(i + 1) * CMP_BLOCK * M]
                                   .rearrange("d (j m) -> d j m", m=M), w).then_inc(loaded.h, 16)
            for i in range(2):
                for half in range(2):
                    sync.dma_start(rows[:, i * P + half * HEAD:i * P + (half + 1) * HEAD], pos[i]).then_inc(loaded.h, 16)
            for half in range(2):
                sync.dma_start(w2s[:, half * HEAD:(half + 1) * HEAD], w2[0]).then_inc(loaded.h, 16)
            sync.dma_start(w2s[:, P:P + HEAD], w2[1]).then_inc(loaded.h, 16)
            sync.dma_start(bv[:, :], b2[1, 0:HEAD].partition_broadcast(CMP)).then_inc(loaded.h, 16)

        @block_.tensor
        def _(pe):
            pe.wait_ge(*loaded(16 * 12))
            for i in range(2):
                last = pe.transpose(K.bank(0, CMP_BLOCK, P, i * CMP_BLOCK), rows[:, i * P:(i + 1) * P], K.ident[0:CMP_BLOCK, 0:CMP_BLOCK])
            last.then_inc(turned.h, 1)
            for i in range(2):
                pe.wait_ge(*posted(i + 1))
                for j in range(CMP_BLOCK):
                    c = i * CMP_BLOCK + j
                    last = pe.matmul(K.bank(1 + i, G * CMP), w1s[:, c * M:(c + 1) * M], blk[:, c * G * CMP:(c + 1) * G * CMP],
                                     start=j == 0, stop=j == CMP_BLOCK - 1)
                last.then_inc(hidden.h, 1)
            pe.wait_ge(*active(2))
            for g in range(G):
                pe.matmul(K.bank(3, CMP, P, g * CMP), w2s[:, 0:P], hid[:, g * CMP:(g + 1) * CMP], start=True, stop=True)
                last = pe.matmul(K.bank(4, HEAD, CMP, g * HEAD), hid[:, (2 + g) * CMP:(3 + g) * CMP], w2s[:, P:P + HEAD],
                                 start=True, stop=True)
            last.then_inc(second.h, 1)
            pe.wait_ge(*squared(1))
            pe.matmul(K.bank(7, G * CMP), K.head_ones[:, :], sq[:, :], start=True, stop=True).then_inc(summed.h, 1)

        @block_.scalar
        def _(act):
            for i in range(2):
                act.wait_ge(*hidden(i + 1))
                act.activation(hid[:, G * i * CMP:G * (i + 1) * CMP], K.bank(1 + i, G * CMP),
                               ACT.Gelu_apprx_tanh, bias=vector(K, "cmp_b1_3")(i)).then_inc(active.h, 1)
            act.wait_ge(*own(1))
            act.activation(sq[:, :], kc[:, :], ACT.Square).then_inc(squared.h, 1)
            act.wait_ge(*biased(1))
            act.activation(r[:, :], r[:, :], ACT.Sqrt).then_inc(rooted.h, 1)

        @block_.vector
        def _(dve):
            dve.memset(blk[:, :], 0.0).then_inc(placed.h, 1)
            dve.wait_ge(*turned(1))
            dve.tensor_copy(post[:, :], K.bank(0, 2 * CMP_BLOCK)).then_inc(placed.h, 1)
            dve.wait_ge(*placed(2))
            for i in range(2):
                by_stride = kv[:, i * T:(i + 1) * T].rearrange("p (c b) -> p b c", b=CMP_STRIDE)
                for a in range(CMP_BLOCK // CMP_STRIDE):
                    j0 = i * CMP_BLOCK + a * CMP_STRIDE
                    for g in range(G):
                        part = slice(64 * g, 64 * g + 64)
                        windows = blk[part, j0 * G * CMP:(j0 + CMP_STRIDE) * G * CMP].rearrange("p (b c) -> p b c", c=G * CMP)
                        last = dve.tensor_tensor(
                            windows[:, :, g * CMP:(g + 1) * CMP], by_stride[part, :, a:a + CMP],
                            post[part, j0:j0 + CMP_STRIDE].unsqueeze(2).to_broadcast([64, CMP_STRIDE, CMP]), ALU.add)
                last.then_inc(posted.h, 1)
            dve.wait_ge(*second(1))
            dve.tensor_scalar(kc[:, :], K.bank(3, G * CMP), vector(K, "cmp_b2_3")(0), None, ALU.add).then_inc(own.h, 1)
            for g in range(G):
                dve.tensor_tensor(vc[:, g * HEAD:(g + 1) * HEAD], K.bank(4, HEAD, CMP, g * HEAD), bv[:, :], ALU.add)
            dve.wait_ge(*summed(1))
            dve.tensor_scalar(r[:, :], K.bank(7, G * CMP), 1.0 / HEAD, eps, ALU.mult, ALU.add).then_inc(biased.h, 1)
            dve.wait_ge(*rooted(1))
            dve.reciprocal(r[:, :], r[:, :]).then_inc(own.h, 1)
            dve.wait_ge(*own(2))
            dve.scalar_tensor_tensor(out=kc[:, :], in0=kc[:, :], scalar=gain, in1=r[:, :], op0=ALU.mult, op1=ALU.mult)


def nsa_attention(K, q, k, v, kc, vc, gates, bias, y, side, side_src, side_dst):
    nc = K.nc
    PAIRS = NSA_HEADS // 2
    S = [(h, i, br) for h in range(2) for i in range(NT) for br in range(3)]
    n = len(S)
    SIDE_STEPS = n * 2 // WEIGHT_SLOTS
    assert side.slots == PAIRS // 2 * WEIGHT_SLOTS and SIDE_STEPS > KD + 2
    side_mixed, side_weights = K.sems.take(2 * side.slots), K.sems.take(1)
    q_staged, k_staged = K.sems.take(PAIRS), K.sems.take(PAIRS)
    scored, probs, turned, turned_copied, weighed = (K.sems.take(PAIRS * n) for _ in range(5))
    score_steps, out_steps = K.sems.take(PAIRS * n * 2), K.sems.take(PAIRS * n * 3)
    with ExitStack() as ctx:
        qs = K.sb(ctx, "nsa_q_pair", T)
        ks = [K.sb(ctx, "nsa_k_selected", T), K.sb(ctx, "nsa_k_window", T)]
        kcs, vcs = K.sb(ctx, "nsa_k_group_cmp", CMP), K.sb(ctx, "nsa_v_group_cmp", HEAD, CMP)
        L = [K.sb(ctx, f"nsa_scores_{a}", T) for a in range(3)]
        pt = [K.sb(ctx, f"nsa_probs_t_{a}", T) for a in range(2)]
        stat = [K.sb(ctx, f"nsa_stat_{a}", 4) for a in range(4)]
        acc = K.sb(ctx, "nsa_out_sum", HEAD)
        block_ = ctx.enter_context(nc.Block())
        @block_.sync
        def _(sync):
            K.stream.run(sync)

        def width(s):
            _, i, br = S[s]
            return (i + 1) * P if br else CMP

        @block_.gpsimd
        def _(pool):
            with pool.Fori(0, NSA_GROUPS) as g:
                with pool.Fori(0, 2) as jj:
                    j = g * 2 + jj
                    pool.wait_ge(*weighed(j * n))
                    pool.tensor_copy(ks[0][:, :], cols(k, g * T, T))
                    pool.tensor_copy(ks[1][:, :], cols(k, g * T + 2 * T, T))
                    pool.tensor_copy(kcs[:, :], cols(kc, g * CMP, CMP))
                    pool.tensor_copy(vcs[:, :], cols(vc, g * HEAD, HEAD, CMP)).then_inc(k_staged.h, 1)

        @block_.tensor
        def _(pe):
            def side_step(g, step):
                f, kt = step // SIDE_STEPS, step % SIDE_STEPS
                if kt < KD:
                    if kt == 0:
                        side.wait_full(pe, g, f)
                        pe.wait_ge(*side_mixed((g * WEIGHT_SLOTS + f - 1) * 2))
                    last = pe.matmul(K.bank(6 + f % 2), side.slot(f)[:, kt, 0:P], side_src[:, kt * TM:kt * TM + T],
                                     start=kt == 0, stop=kt == KD - 1)
                    if kt == KD - 1:
                        last.then_inc(K.stream.used, 1)

            with pe.Fori(0, NSA_GROUPS) as g:
                for jj in range(2):
                    j = g * 2 + jj
                    pe.wait_ge(*q_staged(j + 1))
                    pe.wait_ge(*k_staged(j + 1))
                    for s in range(n + 3):
                        if s < n:
                            h, i, br = S[s]
                            pe.wait_ge(*score_steps((j * n + s - 2) * 2 + 1))
                            rows = slice(64 * h, 64 * h + 64)
                            keys = ks[br - 1][rows, 0:width(s)] if br else kcs[rows, :]
                            pe.matmul(K.bank(s % 2, width(s)), qs[rows, i * P:(i + 1) * P], keys, start=True, stop=True)\
                                .then_inc(scored.h, 1)
                            side_step(g, jj * n + s)
                        if 2 <= s < n + 2:
                            t_ = s - 2
                            _, i, br = S[t_]
                            b, Ls = t_ % 2, L[t_ % 3]
                            pe.wait_ge(*probs(j * n + t_ + 1))
                            pe.wait_ge(*turned_copied(j * n + t_ - 1))
                            if br:
                                for t in range(i + 1):
                                    last = pe.transpose(K.bank(2 + b, P, P, t * P), Ls[:, t * P:(t + 1) * P], K.ident[:, :])
                            else:
                                last = pe.transpose(K.bank(2 + b, P, CMP), Ls[:, 0:CMP], K.ident[:, :])
                            last.then_inc(turned.h, 1)
                        if s >= 3:
                            t_ = s - 3
                            h, i, br = S[t_]
                            b = t_ % 2
                            pe.wait_ge(*turned_copied(j * n + t_ + 1))
                            pe.wait_ge(*out_steps((j * n + t_ - 1) * 3))
                            o = K.bank(4 + b, HEAD)
                            if br:
                                for t in range(i + 1):
                                    last = pe.matmul(o, pt[b][:, t * P:(t + 1) * P],
                                                     cols(v, t * 2 * P + (br - 1) * P + g * HEAD, HEAD), start=t == 0, stop=t == i)
                            else:
                                last = pe.matmul(o, pt[b][0:CMP, 0:P], vcs[:, :], start=True, stop=True)
                            last.then_inc(weighed.h, 1)

        @block_.vector
        def _(dve):
            c = K.column["rwkv_mix"]
            dve.tensor_scalar(K.vectors[:, c + RWKV_IN:c + 2 * RWKV_IN], K.vectors[:, c:c + RWKV_IN], -1.0, 1.0, ALU.mult, ALU.add)\
               .then_inc(side_weights.h, 1)
            dve.wait_ge(*side_weights(1))

            def mix_side(g, f):
                t = g * WEIGHT_SLOTS + f
                dve.wait_ge(*side.done(t))
                mix_with_last_token(K, dve, Chain(dve, side_mixed, t * 2), K.bank(6 + f % 2), side_dst, t)

            with dve.Fori(0, NSA_GROUPS) as g:
                for jj in range(2):
                    j = g * 2 + jj
                    for s in range(n + 3):
                        if s < n:
                            h, i, br = S[s]
                            Ls, w, st = L[s % 3], width(s), stat[s % 4]
                            at = (j * 2 + h) * BIAS_W
                            if br:
                                near = cols(bias, at + 3 * P - i * P, w)
                            else:
                                first = at + 3 * P - i * P + CMP_BLOCK - 1
                                near = bias[:, bass.ds(first, CMP, step=CMP_STRIDE)]
                            chain = Chain(dve, score_steps, (j * n + s) * 2)
                            dve.wait_ge(*scored(j * n + s + 1))
                            dve.wait_ge(*turned(j * n + s - 2))
                            chain(dve.scalar_tensor_tensor(out=Ls[:, 0:w], in0=K.bank(s % 2, w), scalar=HEAD ** -0.5, in1=near,
                                                           op0=ALU.mult, op1=ALU.add))
                            chain(dve.tensor_reduce(st[:, 0:1], Ls[:, 0:w], AX.X, ALU.max, negate=True), False)
                        if s < n and (jj * n + s) % SIDE_STEPS == KD + 1:
                            mix_side(g, (jj * n + s) // SIDE_STEPS)
                        if s >= 3:
                            t_ = s - 3
                            h, i, br = S[t_]
                            b, st = t_ % 2, stat[t_ % 4]
                            chain = Chain(dve, out_steps, (j * n + t_) * 3)
                            dve.wait_ge(*weighed(j * n + t_ + 1))
                            chain(dve.reciprocal(st[:, 2:3], st[:, 1:2]))
                            gate = cols(gates, i * 3 * NSA_HEADS + (j * 2 + h) * 3 + br, 1)
                            chain(dve.tensor_tensor(st[:, 3:4], st[:, 2:3], gate, ALU.mult))
                            o, scale = K.bank(4 + b, HEAD), st[:, 3:4]
                            if br == 0:
                                chain(dve.tensor_scalar(acc[:, :], o, scale, None, ALU.mult))
                            else:
                                dst = acc[:, :] if br == 1 else cols(y, i * T + (j * 2 + h) * HEAD, HEAD)
                                chain(dve.scalar_tensor_tensor(out=dst, in0=o, scalar=scale, in1=acc[:, :], op0=ALU.mult, op1=ALU.add))

        @block_.scalar
        def _(act):
            with act.Fori(0, PAIRS) as j:
                act.wait_ge(*scored(j * n))
                act.activation(qs[:, :], cols(q, j * T, T), ACT.Copy).then_inc(q_staged.h, 1)
                for s in range(n + 2):
                    if s >= 2:
                        b, (_, i, br) = (s - 2) % 2, S[s - 2]
                        act.wait_ge(*turned(j * n + s - 1))
                        act.wait_ge(*weighed(j * n + s - 3))
                        if br:
                            last = act.activation(pt[b][:, 0:(i + 1) * P], K.bank(2 + b, (i + 1) * P), ACT.Copy)
                        else:
                            last = act.activation(pt[b][0:CMP, 0:P], K.bank(2 + b, P, CMP), ACT.Copy)
                        last.then_inc(turned_copied.h, 1)
                    if s < n:
                        Ls, w, st = L[s % 3], width(s), stat[s % 4]
                        act.wait_ge(*score_steps((j * n + s) * 2 + 2))
                        act.activation(Ls[:, 0:w], Ls[:, 0:w], ACT.Exp, bias=st[:, 0:1], accum_out=st[:, 1:2]).then_inc(probs.h, 1)


RWKV_IN = 14


def mix_with_last_token(K, dve, chain, bank, dst, t):
    stay, shift = vector(K, "rwkv_mix")(RWKV_IN + t), vector(K, "rwkv_mix")(t)
    chain(dve.tensor_scalar(cols(dst, t * T, T), bank, stay, None, ALU.mult))
    dst_s = cols(dst, t * T + 1, T - 1)
    chain(dve.scalar_tensor_tensor(out=dst_s, in0=bank[:, 0:T - 1], scalar=shift, in1=dst_s, op0=ALU.mult, op1=ALU.add))


RWKV_TILES = 4
CHUNK = 64
E_HALF = float(np.exp(-0.5))


def rwkv_features(K, d, starts64, rw, A, R, B, C, ends, gate, bonus):
    nc = K.nc
    N = RWKV_TILES
    loaded = K.sems.take(16 * 4)
    lora, mixed, acts, own = K.sems.take(2), K.sems.take(3 * N), K.sems.take(7 * N), K.sems.take(17 * N)
    pe_sums = K.sems.take(2 * N)
    V = lambda name: vector(K, name)
    with ExitStack() as ctx:
        w2a2 = K.sb(ctx, "rwkv_lora_w", N * P)
        g2 = K.sb(ctx, "rwkv_lora_g", N * P)
        starts = K.sb(ctx, "rwkv_chunk_starts", T)
        lw, cl, a, kk, sq, t1, k2 = (K.sb(ctx, f"rwkv_{n}", T) for n in ("log_w", "log_sum", "a", "kk", "squares", "tmp", "k2"))
        e_pos, e_neg, e_ex = (K.sb(ctx, f"rwkv_{n}", T) for n in ("w_run", "w_inv", "w_before"))
        low, glow = rw[:, 12 * T:13 * T], rw[:, 13 * T:14 * T]
        block_ = ctx.enter_context(nc.Block())

        @block_.sync
        def _(sync):
            sync.dma_start(w2a2[0:64, :], d["w2_3"][0]).then_inc(loaded.h, 16)
            sync.dma_start(w2a2[64:P, :], d["a2_3"][0]).then_inc(loaded.h, 16)
            sync.dma_start(g2[:, :], d["g2_3"][0]).then_inc(loaded.h, 16)
            sync.dma_start(starts[:, :], starts64).then_inc(loaded.h, 16)

        @block_.tensor
        def _(pe):
            pe.wait_ge(*loaded(16 * 4))
            pe.wait_ge(*lora(2))
            for t in range(N):
                f = slice(t * P, (t + 1) * P)
                b = 3 * (t % 2)
                pe.wait_ge(*acts((t - 1) * 7))
                pe.matmul(K.bank(b), w2a2[0:64, f], low[0:64, :], start=True, stop=True).then_inc(mixed.h, 1)
                pe.matmul(K.bank(b + 1), w2a2[64:P, f], low[64:P, :], start=True, stop=True).then_inc(mixed.h, 1)
                pe.matmul(K.bank(b + 2), g2[:, f], glow, start=True, stop=True).then_inc(mixed.h, 1)
                pe.wait_ge(*acts(t * 7 + 4))
                pe.matmul(K.bank(6), K.head_ones[:, :], sq[:, :], start=True, stop=True).then_inc(pe_sums.h, 1)
                pe.wait_ge(*own(t * 17 + 11))
                pe.matmul(K.bank(7), K.head_ones[:, :], t1[:, :], start=True, stop=True).then_inc(pe_sums.h, 1)

        @block_.scalar
        def _(act):
            act.activation(low[0:64, :], low[0:64, :], ACT.Tanh).then_inc(lora.h, 1)
            act.activation(glow, glow, ACT.Sigmoid).then_inc(lora.h, 1)
            for t in range(N):
                b = 3 * (t % 2)
                act.wait_ge(*mixed(t * 3 + 3))
                act.wait_ge(*own(t * 17))
                act.wait_ge(*pe_sums(t * 2))
                act.activation(lw[:, :], K.bank(b), ACT.Sigmoid, bias=V("w0_3")(t)).then_inc(acts.h, 1)
                act.activation(a[:, :], K.bank(b + 1), ACT.Sigmoid, bias=V("a0_3")(t)).then_inc(acts.h, 1)
                act.activation(gate[:, t * T:(t + 1) * T], K.bank(b + 2), ACT.Copy).then_inc(acts.h, 1)
                act.wait_ge(*own(t * 17 + 1))
                act.activation(sq[:, :], kk[:, :], ACT.Square).then_inc(acts.h, 1)
                act.wait_ge(*own(t * 17 + 4))
                act.activation(e_pos[:, :], cl[:, :], ACT.Exp)
                act.activation(e_neg[:, :], cl[:, :], ACT.Exp, scale=-1.0)
                act.activation(e_ex[:, :], lw[:, :], ACT.Exp).then_inc(acts.h, 1)
                act.wait_ge(*pe_sums(t * 2 + 1))
                act.activation(sq[:, :], K.bank(6), ACT.Sqrt).then_inc(acts.h, 1)
                act.wait_ge(*pe_sums(t * 2 + 2))
                act.activation(lw[:, :], K.bank(7), ACT.Copy).then_inc(acts.h, 1)

        @block_.vector
        def _(dve):
            dve.wait_ge(*loaded(16 * 4))
            for t in range(N):
                f = slice(t * T, (t + 1) * T)
                r, k, v = (rw[:, (i * N + t) * T:(i * N + t + 1) * T] for i in range(3))
                chain = Chain(dve, own, t * 17)
                chain(dve.tensor_scalar(kk[:, :], k, V("k_k_3")(t), None, ALU.mult))
                dve.wait_ge(*acts(t * 7 + 1))
                chain(dve.tensor_scalar(lw[:, :], lw[:, :], -E_HALF, None, ALU.mult))
                chain(dve.tensor_tensor_scan(cl[:, :], starts[:, :], lw[:, :], 0.0, ALU.mult, ALU.add))
                chain(dve.tensor_tensor(lw[:, :], cl[:, :], lw[:, :], ALU.subtract))
                dve.wait_ge(*acts(t * 7 + 2))
                chain(dve.tensor_scalar(k2[:, :], a[:, :], -1.0, V("k_a_3")(t), ALU.add, ALU.mult))
                chain(dve.scalar_tensor_tensor(out=k2[:, :], in0=k2[:, :], scalar=1.0, in1=k, op0=ALU.add, op1=ALU.mult))
                dve.wait_ge(*acts(t * 7 + 6))
                chain(dve.tensor_scalar(sq[:, :], sq[:, :], 1e-12, None, ALU.max))
                chain(dve.reciprocal(sq[:, :], sq[:, :]))
                chain(dve.tensor_tensor(kk[:, :], kk[:, :], sq[:, :], ALU.mult))
                chain(dve.tensor_tensor(a[:, :], a[:, :], kk[:, :], ALU.mult))
                chain(dve.scalar_tensor_tensor(out=t1[:, :], in0=r, scalar=V("r_k_3")(t), in1=k2[:, :], op0=ALU.mult, op1=ALU.mult), False)
                chain(dve.scalar_tensor_tensor(out=A[:, f], in0=kk[:, :], scalar=-1.0, in1=e_ex[:, :], op0=ALU.mult, op1=ALU.mult), False)
                chain(dve.tensor_tensor(B[:, f], a[:, :], e_neg[:, :], ALU.mult), False)
                chain(dve.tensor_tensor(C[:, f], k2[:, :], e_neg[:, :], ALU.mult), False)
                chain(dve.tensor_tensor(R[:, f], r, e_pos[:, :], ALU.mult), False)
                chain(dve.tensor_copy(ends[:, t * 8:(t + 1) * 8], e_pos[:, CHUNK - 1:T:CHUNK]), False)
                dve.wait_ge(*acts(t * 7 + 7))
                chain(dve.tensor_tensor(bonus[:, f], lw[:, :], v, ALU.mult))


def rwkv_scan(K, A, R, B, C, v, ends, masks, y):
    nc = K.nc
    N = RWKV_TILES
    W = 2 * NT * P
    LEVELS = 3
    PE_N, DVE_N, ACT_N = 27, 45, 9
    CHUNKS = T // CHUNK
    CHUNK_MM, CHUNK_OWN = 3 * CHUNKS + 1, 4 * CHUNKS
    mm, own, acted = K.sems.take(N * PE_N), K.sems.take(N * DVE_N), K.sems.take(N * ACT_N)
    staged, staged_ar, done = K.sems.take(N), K.sems.take(N), K.sems.take(N)
    chunk_mm, chunk_own = K.sems.take(N * CHUNK_MM), K.sems.take(N * CHUNK_OWN)
    loaded = K.sems.take(16)

    def blk(buf, h, c):
        return buf[:, (h * NT + c) * P:(h * NT + c + 1) * P]

    with ExitStack() as ctx:
        m = K.sb(ctx, "rwkv_masks", 6 * P)
        ar = K.sb(ctx, "rwkv_a_r", 2 * T)
        b, c_, vs = K.sb(ctx, "rwkv_b_pair", T), K.sb(ctx, "rwkv_c_pair", T), K.sb(ctx, "rwkv_v_pair", T)
        bn, cn, vn = K.sb(ctx, "rwkv_b_n", T), K.sb(ctx, "rwkv_c_n", T), K.sb(ctx, "rwkv_v_n", T)
        ba, ca = K.sb(ctx, "rwkv_ba_br", 2 * W), K.sb(ctx, "rwkv_ca_cr", 2 * W)
        bat = K.sb(ctx, "rwkv_ba_t", W)
        p1, p1t, p2, p2t, inv, invt = (K.sb(ctx, f"rwkv_{n}", W) for n in ("p1", "p1t", "p2", "p2t", "inv", "inv_t"))
        states = [K.sb(ctx, f"rwkv_state_{i}", P) for i in range(2)]
        aged = K.sb(ctx, "rwkv_state_aged", P)
        wsb, usb = K.sb(ctx, "rwkv_w_chunk", P), K.sb(ctx, "rwkv_u_chunk", P)
        block_ = ctx.enter_context(nc.Block())

        def wide(buf, n=P):
            return buf.rearrange("p (x n) -> p x n", n=n)

        def spread(tiles, i, n=1, over=2 * NT):
            return tiles[:, i * P:(i + n) * P].unsqueeze(1).to_broadcast([P, over, n * P])

        def head(buf, h, n=P):
            return buf[:, h * NT * n:(h + 1) * NT * n]

        def banks(i, n=1):
            return K.ps[:, i * T:(i + n) * T]

        @block_.sync
        def _(sync):
            sync.dma_start(m[:, :], masks).then_inc(loaded.h, 16)

        @block_.gpsimd
        def _(pool):
            with pool.Fori(0, N) as j:
                pool.wait_ge(*mm((j - 1) * PE_N + 7))
                pool.tensor_copy(b[:, :], cols(B, j * T, T))
                pool.tensor_copy(c_[:, :], cols(C, j * T, T))
                pool.tensor_copy(vs[:, :], cols(v, j * T, T)).then_inc(staged.h, 1)

        @block_.tensor
        def _(pe):
            def each(h, bank, left, right, width=P):
                for c in range(NT):
                    x = bank * T + c * width
                    last = pe.matmul(K.ps[:, x:x + width], left(h, c), right(h, c), start=True, stop=True)
                return last

            def whole(buf):
                return lambda h, c: blk(buf, h, c)

            def half(buf, stride=P, width=P):
                return lambda h, c: buf[64 * h:64 * h + 64, c * stride:c * stride + width]

            with pe.Fori(0, N) as j:
                at, act_at = j * DVE_N, j * ACT_N
                pe.wait_ge(*staged(j + 1))
                pe.wait_ge(*staged_ar(j + 1))
                ar_pair = half(ar, 2 * P, 2 * P)
                for h in range(2):
                    each(h, 2 * h, half(b), ar_pair, 2 * P).then_inc(mm.h, 1)
                for h in range(2):
                    each(h, 4 + h, half(ar, 2 * P), half(b)).then_inc(mm.h, 1)
                each(0, 6, half(c_), ar_pair, 2 * P).then_inc(mm.h, 1)
                pe.wait_ge(*own(at + 1))
                each(1, 0, half(c_), ar_pair, 2 * P).then_inc(mm.h, 1)
                pe.wait_ge(*own(at + 3))
                for i, src in enumerate((b, c_, vs)):
                    for c in range(NT):
                        last = pe.transpose(K.bank(2 + i, P, P, c * P), src[:, c * P:(c + 1) * P], K.ident[:, :])
                last.then_inc(mm.h, 1)
                pe.wait_ge(*own(at + 10))
                pe.wait_ge(*acted(act_at + 1))
                q, qt, s, st = p1, p1t, p2, p2t
                for lev in range(LEVELS):
                    for h in range(2):
                        if lev:
                            pe.wait_ge(*own(at + 5 + 6 * lev + h))
                            pe.wait_ge(*acted(act_at + 2 * lev + h))
                        each(h, 4 * h, whole(qt), whole(q))
                        each(h, 4 * h + 1, whole(q), whole(qt)).then_inc(mm.h, 1)
                    for h in range(2):
                        pe.wait_ge(*own(at + 11 + 6 * lev + h))
                        pe.wait_ge(*acted(act_at + 2 + 2 * lev + h))
                        each(h, 4 * h + 2, whole(st), whole(inv))
                        each(h, 4 * h + 3, whole(s), whole(invt)).then_inc(mm.h, 1)
                    q, qt, s, st = s, st, q, qt
                for h in range(2):
                    pe.wait_ge(*own(at + 28 + 4 * h))
                    each(h, 4 * h, whole(qt), whole(inv))
                    each(h, 4 * h + 1, whole(q), whole(invt)).then_inc(mm.h, 1)
                for h in range(2):
                    pe.wait_ge(*own(at + 33 + h))
                    pe.wait_ge(*acted(act_at + 8 + h))
                    each(h, 4 * h + 2, whole(invt), whole(s))
                    each(h, 4 * h + 3, whole(inv), whole(st)).then_inc(mm.h, 1)
                for h in range(2):
                    pe.wait_ge(*own(at + 37 + 3 * h))
                    each(h, 4 * h, whole(qt), whole(inv)).then_inc(mm.h, 1)
                for h in range(2):
                    pe.wait_ge(*own(at + 41 + h))
                    each(h, 4 * h + 2, whole(invt), whole(s)).then_inc(mm.h, 1)

                pe.wait_ge(*own(at + 45))
                for n in range(CHUNKS):
                    c, o = n // 2, CHUNK * (n % 2)
                    S = states[n % 2]
                    tok, at_n = slice(o, o + CHUNK), j * CHUNK_OWN + 4 * n
                    if n:
                        pe.wait_ge(*chunk_own(at_n))
                    pe.matmul(K.ps[tok, 0:P], ar[:, c * 2 * P + o:c * 2 * P + o + CHUNK], S[:, :], start=True, stop=False,
                              skip_group_check=True)
                    for h in range(2):
                        x = (h * NT + c) * 2 * P
                        last = pe.matmul(K.ps[tok, 64 * h:64 * h + 64], ca[:, x + o:x + o + CHUNK],
                                         vn[:, c * P + 64 * h:c * P + 64 * h + 64], start=False, stop=h == 1, skip_group_check=True)
                    last.then_inc(chunk_mm.h, 1)
                    pe.wait_ge(*chunk_own(at_n + 2))
                    for h in range(2):
                        last = pe.matmul(K.ps[tok, T + 64 * h:T + 64 * h + 64], blk(inv, h, c)[:, tok],
                                         wsb[:, 64 * h:64 * h + 64], start=True, stop=True)
                    last.then_inc(chunk_mm.h, 1)
                    grown = K.bank(3, P)
                    pe.matmul(grown, cn[tok, c * P:(c + 1) * P], vn[tok, c * P:(c + 1) * P], start=True, stop=False)
                    pe.wait_ge(*chunk_own(at_n + 3))
                    pe.matmul(grown, bn[tok, c * P:(c + 1) * P], usb[tok, :], start=False, stop=True).then_inc(chunk_mm.h, 1)
                    y_at = 2 * T + n * CHUNK
                    pe.matmul(K.ps[:, y_at:y_at + CHUNK], S[:, :], ar[:, (c * 2 + 1) * P + o:(c * 2 + 1) * P + o + CHUNK],
                              start=True, stop=False, skip_group_check=True)
                    for h in range(2):
                        x = (h * NT + c) * 2 * P + P + o
                        out = K.ps[64 * h:64 * h + 64, y_at:y_at + CHUNK]
                        pe.matmul(out, usb[:, 64 * h:64 * h + 64], ba[:, x:x + CHUNK], start=False, stop=False, skip_group_check=True)
                        last = pe.matmul(out, vn[:, c * P + 64 * h:c * P + 64 * h + 64], ca[:, x:x + CHUNK], start=False,
                                         stop=h == 1, skip_group_check=True)
                last.then_inc(chunk_mm.h, 1)

        @block_.scalar
        def _(act):
            with act.Fori(0, N) as j:
                def copy(n, dst, src):
                    act.wait_ge(*mm(j * PE_N + n))
                    act.activation(dst, src, ACT.Copy).then_inc(acted.h, 1)
                act.wait_ge(*done(j))
                for i, src in enumerate((A, R)):
                    last = act.activation(ar[:, :].rearrange("p (c i n) -> p c i n", i=2, n=P)[:, :, i, :],
                                          cols(src, j * T, T).rearrange("p (c n) -> p c n", n=P), ACT.Copy)
                last.then_inc(staged_ar.h, 1)
                act.wait_ge(*mm(j * PE_N + 7))
                act.activation(bn[:, :], K.bank(2), ACT.Copy)
                act.activation(cn[:, :], K.bank(3), ACT.Copy)
                act.activation(vn[:, :], K.bank(4), ACT.Copy).then_inc(acted.h, 1)
                for lev in range(LEVELS):
                    for h in range(2):
                        copy(8 + 4 * lev + h, head(p2t if lev % 2 == 0 else p1t, h), banks(4 * h + 1))
                for h in range(2):
                    copy(20 + h, head(p1t, h), banks(4 * h + 1))

        @block_.vector
        def _(dve):
            dve.wait_ge(*loaded(16))
            with dve.Fori(0, N) as j:
                own_of, after_of = (lambda n: own(j * DVE_N + n)), (lambda n: mm(j * PE_N + n))
                chain = Chain(dve, own, j * DVE_N)

                def after(n):
                    dve.wait_ge(*after_of(n))

                def masked(dst, src, i):
                    return dve.tensor_tensor(wide(dst), src, spread(m, i, over=dst.shape[1] // P), ALU.mult)

                def masked_pair(dst, h, first_bank):
                    return dve.tensor_tensor(wide(head(dst, h, 2 * P), 2 * P), wide(banks(first_bank, 2), 2 * P),
                                             spread(m, 0, 2, NT), ALU.mult)

                def grow(buf, h, bank):
                    return dve.tensor_tensor(head(buf, h), head(buf, h), banks(bank), ALU.add)

                def ba_of(h):
                    return wide(head(ba, h, 2 * P), 2 * P)[:, :, 0:P]
                for h in range(2):
                    after(1 + h)
                    chain(masked_pair(ba, h, 2 * h), False)
                for h in range(2):
                    after(3 + h)
                    chain(masked(head(bat, h), wide(banks(4 + h)), 2), False)
                dve.wait_ge(*own_of(2))
                chain(masked(p1[:, :], wide(ba[:, :], 2 * P)[:, :, 0:P], 3), False)
                dve.wait_ge(*own_of(4))
                chain(masked(p1t[:, :], wide(bat[:, :]), 3), False)
                dve.wait_ge(*own_of(5))
                chain(dve.tensor_tensor(wide(inv[:, :]), wide(p1[:, :]), spread(K.ident, 0), ALU.add), False)
                dve.wait_ge(*own_of(6))
                chain(dve.tensor_tensor(wide(invt[:, :]), wide(p1t[:, :]), spread(K.ident, 0), ALU.add), False)
                after(5)
                chain(masked_pair(ca, 0, 6), False)
                after(6)
                chain(masked_pair(ca, 1, 0))
                for lev in range(LEVELS):
                    for h in range(2):
                        after(8 + 4 * lev + h)
                        chain(dve.tensor_copy(head(p2 if lev % 2 == 0 else p1, h), banks(4 * h)), False)
                    for h in range(2):
                        after(10 + 4 * lev + h)
                        if lev:
                            dve.wait_ge(*own_of(8 + 6 * lev + 2 * h))
                        chain(grow(inv, h, 4 * h + 2), False)
                        chain(grow(invt, h, 4 * h + 3), False)
                        if lev == LEVELS - 1:
                            chain(masked(head(p2, h), ba_of(h), 4), False)
                            chain(masked(head(p2t, h), wide(head(bat, h)), 4), False)
                for h in range(2):
                    after(20 + h)
                    chain(dve.tensor_copy(head(p1, h), banks(4 * h)), False)
                for h in range(2):
                    after(22 + h)
                    dve.wait_ge(*own_of(26 + 4 * h))
                    chain(grow(inv, h, 4 * h + 2), False)
                    chain(grow(invt, h, 4 * h + 3), False)
                    chain(masked(head(p2t, h), wide(head(bat, h)), 5), False)
                for h in range(2):
                    after(24 + h)
                    chain(dve.tensor_copy(head(p1, h), banks(4 * h)), False)
                dve.wait_ge(*own_of(38))
                for h in range(2):
                    after(26 + h)
                    chain(grow(inv, h, 4 * h + 2), False)
                for buf in (wsb, usb, *states):
                    last = dve.memset(buf[:, :], 0.0)
                chain(last)
                for n in range(CHUNKS):
                    o = CHUNK * (n % 2)
                    tok = slice(o, o + CHUNK)
                    S, S_next = states[n % 2], states[(n + 1) % 2]
                    chunk = Chain(dve, chunk_own, j * CHUNK_OWN + 4 * n)
                    chunk(dve.tensor_scalar(aged[:, :], S[:, :], cols(ends, j * 8 + n, 1), None, ALU.mult), False)
                    dve.wait_ge(*chunk_mm(j * CHUNK_MM + 3 * n + 1))
                    chunk(dve.tensor_copy(wsb[tok, :], K.ps[tok, 0:P]), False)
                    dve.wait_ge(*chunk_mm(j * CHUNK_MM + 3 * n + 2))
                    chunk(dve.tensor_copy(usb[tok, :], K.ps[tok, T:T + P]))
                    dve.wait_ge(*chunk_mm(j * CHUNK_MM + 3 * n + 3))
                    for h in range(2):
                        feat = slice(64 * h, 64 * h + 64)
                        last = dve.scalar_tensor_tensor(out=S_next[feat, feat], in0=K.ps[feat, 3 * T + 64 * h:3 * T + 64 * h + 64],
                                                        scalar=cols(ends, j * 8 + n, 1, 64, 64 * h), in1=aged[feat, feat],
                                                        op0=ALU.mult, op1=ALU.add)
                    chunk(last)
                dve.wait_ge(*chunk_mm((j + 1) * CHUNK_MM))
                dve.tensor_copy(cols(y, j * T, T), K.bank(2)).then_inc(done.h, 1)


def rwkv_output(K, y, bonus, gate, dst):
    nc = K.nc
    N = RWKV_TILES
    PER = 5
    summed, centred, squared, spreads = (K.sems.take(N) for _ in range(4))
    shifted, rooted, own = K.sems.take(N), K.sems.take(N), K.sems.take(PER * N)
    V = lambda name: vector(K, name)
    with ExitStack() as ctx:
        sq, r = K.sb(ctx, "rwkv_y_squares", N * T), K.sb(ctx, "rwkv_y_scale", N * T)
        block_ = ctx.enter_context(nc.Block())

        def tile(buf, t):
            return buf[:, t * T:(t + 1) * T]

        @block_.tensor
        def _(pe):
            for t in range(N):
                pe.matmul(K.bank(t), K.head_ones[:, :], tile(y, t), start=True, stop=True).then_inc(summed.h, 1)
            for t in range(N):
                pe.wait_ge(*squared(t + 1))
                pe.matmul(K.bank(N + t), K.head_ones[:, :], tile(sq, t), start=True, stop=True).then_inc(spreads.h, 1)

        @block_.scalar
        def _(act):
            for t in range(N):
                act.wait_ge(*centred(t + 1))
                act.activation(tile(sq, t), tile(y, t), ACT.Square).then_inc(squared.h, 1)
            for t in range(N):
                act.wait_ge(*shifted(t + 1))
                act.activation(tile(r, t), tile(r, t), ACT.Sqrt).then_inc(rooted.h, 1)

        @block_.vector
        def _(dve):
            for t in range(N):
                dve.wait_ge(*summed(t + 1))
                dve.scalar_tensor_tensor(out=tile(y, t), in0=K.bank(t), scalar=-1.0 / HEAD, in1=tile(y, t), op0=ALU.mult,
                                         op1=ALU.add).then_inc(centred.h, 1)
            for t in range(N):
                dve.wait_ge(*spreads(t + 1))
                dve.tensor_scalar(tile(r, t), K.bank(N + t), 1.0 / HEAD, 64e-5, ALU.mult, ALU.add).then_inc(shifted.h, 1)
            for t in range(N):
                chain = Chain(dve, own, t * PER)
                dve.wait_ge(*rooted(t + 1))
                chain(dve.reciprocal(tile(r, t), tile(r, t)))
                chain(dve.tensor_tensor(tile(y, t), tile(y, t), tile(r, t), ALU.mult))
                chain(dve.tensor_scalar(tile(y, t), tile(y, t), V("ln_x_w_3")(t), V("ln_x_b_3")(t), ALU.mult, ALU.add))
                chain(dve.tensor_tensor(tile(y, t), tile(y, t), tile(bonus, t), ALU.add))
                chain(dve.tensor_tensor(tile(dst, t), tile(y, t), tile(gate, t), ALU.mult), False)


def third_block(K, d, tables, X, U, plans, scratch):
    V = lambda name: vector(K, name)
    with ExitStack() as mix:
        mixed = K.sb(mix, "mixer_out", KD * T)
        rw = K.sb(mix, "rwkv_in", RWKV_IN * T)
        with ExitStack() as nsa:
            qkv = K.sb(nsa, "nsa_q_cmp", 6 * T)
            k = K.sb(nsa, "nsa_k", 4 * T)
            v = K.sb(nsa, "nsa_v", NT * 2 * P)
            gates = K.sb(nsa, "nsa_gates", NT * 3 * NSA_HEADS)
            kc, vc = K.sb(nsa, "nsa_k_cmp", NSA_GROUPS * CMP), K.sb(nsa, "nsa_v_cmp", NSA_GROUPS * HEAD, CMP)
            project_t(K, plans["nsa_q"], U, TM, qkv, T, norm=RmsNorm(K, X, U, TM, V("norm1_g_3"), 1e-6))
            project_t(K, plans["nsa_k"], U, TM, k, T)
            project_n(K, plans["nsa_v"], U, TM, v, 2 * P, 2 * P)
            project_n(K, plans["nsa_gates"], U, TM, gates, 3 * NSA_HEADS, 3 * NSA_HEADS, func=ACT.Sigmoid)
            head_norm_t(K, [(qkv[:, t * T:(t + 1) * T], V("q_norm_g_3")(0), False) for t in range(4)]
                        + [(k[:, t * T:(t + 1) * T], V("k_norm_g_3")(1 + t // 2), False) for t in range(4)], tables, 1e-6)
            compress(K, qkv[:, 4 * T:6 * T], kc, vc, d["cmp_pos_3"][0], d["cmp_w1_3"][0], d["cmp_w2_3"][0],
                     d["cmp_b2_3"][0], 1e-6, V("k_norm_g_3")(0))
            bias = K.sb(nsa, "nsa_bias", NSA_HEADS * BIAS_W)
            distance_bias(K, d["rel_bias_3"], tables["bucket_onehot"], tables["flip"], scratch, bias)
            hide_uncompressed(K, gates, tables["cmp_seen"])
            y = K.sb(nsa, "nsa_y", NT * T)
            nsa_attention(K, qkv, k, v, kc, vc, gates, bias, y, plans["rwkv_in_first"], U, rw)
            turn_tokens(K, y, mixed, NT)
        with ExitStack() as rwkv:
            bonus, gate = K.sb(rwkv, "rwkv_bonus", NT * T), K.sb(rwkv, "rwkv_gate", NT * T)
            ends = K.sb(rwkv, "rwkv_w_ends", RWKV_TILES * 8)
            project_shift_t(K, plans["rwkv_in"], U, TM, rw, plans["rwkv_in_first"].slots)
            A, B = U[:, 0:4 * T], U[:, 4 * T:8 * T]
            R, C = rw[:, 0:4 * T], rw[:, 4 * T:8 * T]
            rwkv_features(K, d, tables["starts64"], rw, A, R, B, C, ends, gate, bonus)
            y = mixed[:, 4 * T:8 * T]
            rwkv_scan(K, A, R, B, C, rw[:, 8 * T:12 * T], ends, tables["chunk_masks"], y)
            rwkv_output(K, y, bonus, gate, y)
        add_product(K, plans["w_out3"], mixed, T, X, TM)
    conv_swiglu(K, RmsNorm(K, X, U, TM, V("norm2_g_3"), 1e-6), U, TM, X, plans["ffn_up3"], plans["ffn_down3"], "conv_w_3", "conv_b_3", False)


def hide_uncompressed(K, gates, seen):
    nc = K.nc
    loaded = K.sems.take(16)
    with ExitStack() as ctx:
        mask = K.sb(ctx, "cmp_seen", 1)
        block_ = ctx.enter_context(nc.Block())

        @block_.sync
        def _(sync):
            sync.dma_start(mask[:, :], seen).then_inc(loaded.h, 16)

        @block_.vector
        def _(dve):
            dve.wait_ge(*loaded(16))
            g = gates[:, 0:3 * NSA_HEADS:3]
            dve.tensor_scalar(g, g, mask[:, 0:1], None, ALU.mult)


def project_shift_t(K, plan, src, stride, dst, first):
    nc = K.nc
    per = 4
    shifted = K.sems.take(plan.groups * per)
    with ExitStack() as ctx:
        block_ = ctx.enter_context(nc.Block())

        @block_.sync
        def _(sync):
            K.stream.run(sync)

        @block_.tensor
        def _(pe):
            product_t(K, plan, src, stride, 2, [lambda k: shifted(k * per)])(pe)

        @block_.vector
        def _(dve):
            for i, k, u in steps(dve, plan.groups, WEIGHT_SLOTS):
                dve.wait_ge(*plan.done(k))
                chain = Chain(dve, shifted, k * per)
                for ct in range(2):
                    mix_with_last_token(K, dve, chain, K.bank((u % 2) * 2 + ct), dst, first + 2 * k + ct)


def rows_of(ap, n=None):
    return ap.rearrange("(r p) -> r p", p=P)


def first_block(K, d, tables, X, U, plans):
    nc = K.nc
    V = lambda name: vector(K, name)
    swiglu(K, RmsNorm(K, X, U, TM, V("norm_ffn1"), 1e-6, meta=True), U, TM, X, plans["ffn1_up"], plans["ffn1_down"], meta=True)
    with ExitStack() as mix:
        q = ya = K.sb(mix, "fox_q_then_y_t", KD * T)
        gates = K.sb(mix, "mix_gates", 2 * KD * T)
        with ExitStack() as fox:
            v = K.sb(fox, "fox_v", NT * D)
            v_meta = K.sb(fox, "fox_v_meta", D, META)
            with ExitStack() as qk:
                k = K.sb(qk, "fox_k", KD * TM)
                ncB = K.sb(qk, "fox_forget", FOX_HEADS * TM)
                project_t(K, plans["fox_q"], U, TM, q, T, norm=RmsNorm(K, X, U, TM, V("norm_mix"), 1e-6, meta=True))
                project_t(K, plans["fox_k"], U, TM, k, TM, meta=True)
                project_n(K, plans["fox_v"], U, TM, v, 256, D, v_meta)
                forget_sums(K, plans["fox_f"], U, d["b_forget"][0], ncB)
                head_norm_t(K, [(q[:, t * T:(t + 1) * T], V("fox_q_norm")(0), False) for t in range(KD)]
                            + [(k[:, t * TM:(t + 1) * TM], V("fox_k_norm")(0), True) for t in range(KD)], tables, 1e-6)
                fox_attention(K, q, k, v, v_meta, ncB, plans["gates1"], U, gates)
            turn_tokens(K, q, ya, KD, lambda t, j: j * T + t * P)
        yb = K.sb(mix, "ret_y_t", KD * T)
        with ExitStack() as ret:
            q, k = K.sb(ret, "ret_q_t", RET_HEADS * T), K.sb(ret, "ret_k_t", RET_HEADS * TM)
            v, v_meta = K.sb(ret, "ret_v", NT * D), K.sb(ret, "ret_v_meta", D, META)
            project_t(K, plans["ret_q"], U, TM, q, T)
            project_t(K, plans["ret_k"], U, TM, k, TM, meta=True)
            project_n(K, plans["ret_v"], U, TM, v, 256, D, v_meta)
            retention(K, q, k, v, v_meta, yb, tables, plans["ret_g"], U)
        gated_sum(K, plans["w_o_fox"], ya, plans["w_o_ret"], yb, gates, V("b_gate"))
        add_product(K, plans["w_out1"], gates, T, X, TM)
    swiglu(K, RmsNorm(K, X, U, TM, V("norm_ffn2"), 1e-6), U, TM, X, plans["ffn2_up"], plans["ffn2_down"])


def block(start, step=256, width=256):
    return lambda k: [(0, width, k * step + start)]


def pair(second):
    return lambda k: [(0, P, k * P), (P, P, k * P + second)]


def plan_weights(K, d):
    S, plans = K.stream, {}

    def add(name, weights, kt, slots, columns, width=256, ksplit=1):
        plans[name] = Product(S, weights, kt, slots, columns, width, ksplit)

    w = d["w_in"][0]
    add("ffn1_up", d["w_ffn1_in"][0], KD, KF, pair(FF))
    add("ffn1_down", d["w_ffn1_out"][0], KF // 2, 2 * KD, block(0, P, P), P, 2)
    add("fox_q", w, KD, 4, block(0))
    add("fox_k", w, KD, 4, block(1024))
    add("fox_v", w, KD, 4, block(2048))
    add("fox_f", w, KD, 1, block(3072, 0, FOX_HEADS), FOX_HEADS)
    add("gates1", w, KD, 8, block(6160))
    add("ret_q", w, KD, 2, block(3088))
    add("ret_k", w, KD, 2, block(3600))
    add("ret_v", w, KD, 4, block(4112))
    add("ret_g", w, KD, 4, block(5136))
    add("w_o_fox", d["w_o_fox"][0], KD, 4, block(0))
    add("w_o_ret", d["w_o_ret"][0], KD, 4, block(0))
    add("w_out1", d["w_out"][0], KD, 4, block(0))
    add("ffn2_up", d["w_ffn2_in"][0], KD, KF, pair(FF))
    add("ffn2_down", d["w_ffn2_out"][0], KF // 2, 2 * KD, block(0, P, P), P, 2)
    w = d["w_in_2"][0]
    add("gate_a2", w, KD, 4, block(0))
    add("gmlp_u", w, KD, 4, block(2048))
    add("gmlp_v", w, KD, 4, block(3072))
    add("w_proj_a", d["w_proj_a_2"][0], KD, 4, block(0))
    add("xbc", w, KD, 12, block(6144))
    add("dt", w, KD, 1, block(9216, 0, SSM_HEADS), SSM_HEADS)
    add("ssm_z", w, KD, 8, block(4096))
    add("gate_b2", w, KD, 4, block(1024))
    add("w_proj_b", d["w_proj_b_2"][0], KD, 8, block(0), 256, 2)
    add("w_out2", d["w_out_2"][0], KD, 4, block(0))
    add("ffn_up2", d["ffn_w_up_2"][0], KD, KF, pair(FF))
    add("ffn_down2", d["ffn_w_down_2"][0], KF // 2, 2 * KD, block(0, P, P), P, 2)
    w = d["w_in_3"][0]
    add("nsa_q", w, KD, 3, block(0))
    add("nsa_k", w, KD, 2, lambda k: [(HEAD * i, HEAD, 768 + 256 * k + HEAD * (i // 2)) for i in range(4)])
    add("nsa_v", w, KD, 1, lambda k: [(0, P, 896), (P, P, 1152)])
    add("nsa_gates", w, KD, 1, block(1280, 0, 3 * NSA_HEADS), 3 * NSA_HEADS)
    add("rwkv_in_first", w, KD, 8, block(1304, P, P), P)
    add("rwkv_in", w, KD, 3, block(1304 + 8 * P))
    add("w_out3", d["w_out_3"][0], KD, 4, block(0))
    add("ffn_up3", d["ffn_up_3"][0], KD, KF, lambda k: [(0, P, k * P + FF), (P, P, k * P)])
    add("ffn_down3", d["ffn_down_3"][0], KF // 2, 2 * KD, block(0, P, P), P, 2)
    return plans


def write_t(K, buf, stride, out):
    nc = K.nc
    turned, copied, written = K.sems.take(KD), K.sems.take(KD), K.sems.take(16 * NT)
    with ExitStack() as ctx:
        rows = K.sb(ctx, f"out_rows_{nc.next_id()}", NT * D)
        blk = ctx.enter_context(nc.Block())

        @blk.tensor
        def _(pe):
            for n in range(2 * NT):
                t, half = n // 2, n % 2
                pe.wait_ge(*copied(n - 1))
                for j in range(4):
                    f = half * 4 + j
                    last = pe.transpose(K.bank(n % 2, P, P, j * P), buf[:, f * stride + t * P:f * stride + (t + 1) * P], K.ident[:, :])
                last.then_inc(turned.h, 1)

        @blk.vector
        def _(dve):
            for n in range(2 * NT):
                dve.wait_ge(*turned(n + 1))
                dve.tensor_copy(rows[:, n * T:(n + 1) * T], K.bank(n % 2)).then_inc(copied.h, 1)

        @blk.sync
        def _(sync):
            for t in range(NT):
                sync.wait_ge(*copied(2 * t + 2))
                sync.dma_start(out[t * P:(t + 1) * P, :], rows[:, t * D:(t + 1) * D]).then_inc(written.h, 16)
            sync.wait_ge(*written(16 * NT))


def setup(K, tables):
    nc = K.nc
    K.ident = K.sb(K.ctx, "identity", P)
    K.ones = K.sb(K.ctx, "ones", P)
    K.head_ones = K.sb(K.ctx, "head_ones", P)
    K.causal = K.sb(K.ctx, "causal_mask", P)
    with ExitStack() as ctx:
        block_ = ctx.enter_context(nc.Block())

        @block_.vector
        def _(dve):
            dve.memset(K.ones[:, :], 1.0)

        @block_.gpsimd
        def _(pool):
            for h in K.sems.all + K.stream.full + [K.stream.used]:
                pool.sem_inc(h, CREDIT)
    landed = K.sems.take(16 * 3)
    with ExitStack() as ctx:
        block_ = ctx.enter_context(nc.Block())

        @block_.sync
        def _(sync):
            for dst, name in ((K.ident, "ident"), (K.head_ones, "head_ones"), (K.causal, "causal")):
                sync.dma_start(dst[:, :], tables[name]).then_inc(landed.h, 16)
            sync.wait_ge(*landed(16 * 3))


def three_blocks_kernel(nc, d, tables, scratch, out):
    with ExitStack() as ctx:
        K = Kernel(nc, ctx)
        setup(K, tables)
        plans = plan_weights(K, d)
        vec = []

        def add(name, ap, n):
            vec.append((name, ap, n))
        for name in ("norm_ffn1", "norm_mix", "norm_ffn2", "ret_gn"):
            add(name, rows_of(d[name][0]), KD)
        add("b_gate", rows_of(d["b_gate"][0]), 2 * KD)
        add("fox_q_norm", d["fox_q_norm"], 1)
        add("fox_k_norm", d["fox_k_norm"], 1)
        for name, n in (("mix_norm_w_2", KD), ("gate_bias_2", 2 * KD), ("ssm_conv_b_2", 3 * KD), ("ssm_norm_w_2", 2 * KD),
                        ("ffn_norm_w_2", KD), ("ffn_conv_b_2", 2 * KF)):
            ap = d[name][0]
            add(name, ap.rearrange("a (r p) -> (a r) p", p=P) if name == "gate_bias_2" else rows_of(ap), n)
        add("final_norm_w_2", rows_of(d["final_norm_w_2"]), KD)
        add("ssm_conv_w_2", d["ssm_conv_w_2"][0].rearrange("k (r p) -> (k r) p", p=P), 4 * 3 * KD)
        add("ffn_conv_w_2", d["ffn_conv_w_2"][0].rearrange("k (r p) -> (k r) p", p=P), 3 * 2 * KF)
        for name, n in (("norm1_g_3", KD), ("norm2_g_3", KD), ("conv_b_3", 2 * KF), ("w0_3", 4), ("a0_3", 4), ("k_k_3", 4),
                        ("k_a_3", 4), ("ln_x_w_3", 4), ("ln_x_b_3", 4)):
            add(name, rows_of(d[name][0]), n)
        add("r_k_3", d["r_k_3"][0].rearrange("(t h) n -> t (h n)", h=2), 4)
        add("rwkv_mix", rows_of(d["rwkv_mu_3"][0]), RWKV_IN)
        add("rwkv_mix_rest", rows_of(d["rwkv_mu_3"][0]), RWKV_IN)
        add("cmp_b1_3", d["cmp_b1_3"][0], 2)
        add("cmp_b2_3", d["cmp_b2_3"][0], 2)
        add("q_norm_g_3", d["q_norm_g_3"], 1)
        add("k_norm_g_3", d["k_norm_g_3"][0], 3)
        add("conv_w_3", d["conv_w_3"][0].rearrange("k (r p) -> (k r) p", p=P), 3 * 2 * KF)
        load_vectors(K, vec)
        X = K.sb(ctx, "residual", KD * TM)
        U = K.sb(ctx, "normalized", KD * TM)
        load_x(K, d["x"][0], d["meta_tokens"], X, TM)
        first_block(K, d, tables, X, U, plans)
        second_block(K, d, tables, X, U, plans)
        third_block(K, d, tables, U, X, plans, scratch)
        write_t(K, U, TM, out[0])


def shape_tables():
    f = np.float32
    t = {"ident": np.eye(P, dtype=f), "head_ones": np.kron(np.eye(2, dtype=f), np.ones((64, 64), f))}
    a = np.arange(P)
    t["head_gather"] = (np.arange(2 * HEAD_ROWS - 2)[None, :] == HEAD_ROWS - 2 + a[:, None] // 64).astype(f)
    t["head_scatter"] = (np.arange(HEAD_ROWS)[:, None] == np.arange(HEAD_ROWS // 2 * P)[None, :] // 64).astype(f)
    t["causal"] = np.where(a[None, :] <= a[:, None], 0, NEG).astype(f)
    t["causal01"] = (a[None, :] >= a[:, None]).astype(f)
    t["starts"] = np.broadcast_to(np.arange(T) % P != 0, (P, T)).astype(f)
    d_ = 511 - np.arange(2 * T)
    n = np.maximum(d_, 0)
    large = 16 + (np.log(np.maximum(n, 1).astype(f) / f(16)) / f(np.log(128 / 16)) * f(16)).astype(np.int32)
    bucket = np.where(d_ < 0, BUCKETS, np.where(n < 16, n, np.minimum(large, BUCKETS - 1)))
    t["bucket_onehot"] = (np.arange(BUCKETS + 1)[:, None] == bucket[None, :]).astype(f)
    t["cmp_seen"] = (a[:, None] >= CMP_BLOCK - 1).astype(f)
    to, fr = a[None, :], a[:, None]
    near = [fr // w == to // w for w in (16, 32, 64)]
    t["chunk_masks"] = np.concatenate([near[2] & (fr < to), near[2] & (fr <= to), near[2] & (fr > to), near[0],
                                       near[1] & ~near[0], near[2] & ~near[1]], axis=1).astype(f)
    t["starts64"] = np.broadcast_to(np.arange(T) % CHUNK != 0, (P, T)).astype(f)
    t["flip"] = np.ascontiguousarray(np.eye(P, dtype=f)[::-1])
    t["swap"] = np.roll(np.eye(P, dtype=f), P // 2, axis=0)
    pos = np.concatenate([META + np.arange(T), np.arange(META)]).astype(f)
    half = P // 2
    inv = (f(10000.0) ** (-np.arange(half, dtype=f) / f(half))).astype(f)
    ang = (inv[:, None] * pos[None, :]).astype(f).astype(np.float64)
    t["rope_cos"] = np.concatenate([np.cos(ang), np.cos(ang)]).astype(f)
    t["rope_sin"] = np.concatenate([-np.sin(ang), np.sin(ang)]).astype(f)
    lg = np.log1p(-np.exp2(-5.0 - np.arange(4)))
    gap = a[None, :] - a[:, None]
    t["decay"] = np.concatenate([np.where(gap >= 0, np.exp(g * np.maximum(gap, 0)), 0) for g in lg], axis=1).astype(f)
    t["xi"] = np.concatenate([np.broadcast_to(np.exp(g * (a + 1.0)), (P, P)) for g in lg], axis=1).astype(f)
    t["zeta"] = np.concatenate([np.stack([np.exp(g * (P - 1 - a)) for g in lg], 1),
                                np.broadcast_to(np.exp(lg * P), (P, 4))], axis=1).astype(f)
    t["zeta_meta"] = np.stack([np.exp(g * (META - 1 - np.arange(META))) for g in lg], 1).astype(f)
    return t


def kernel(**inputs):
    import concourse.bacc as bacc
    from concourse.bass_utils import run_bass_kernel_spmd

    nc = bacc.Bacc("TRN2", target_bir_lowering=False, num_devices=1)
    arrays = {f"in_{name}": np.ascontiguousarray(a) for name, a in inputs.items()}
    for name in ("fox_q_norm", "fox_k_norm", "q_norm_g_3", "k_norm_g_3", "cmp_b2_3"):
        a = arrays[f"in_{name}"]
        arrays[f"in_{name}"] = np.ascontiguousarray(np.concatenate([a, a], axis=-1))
    tables = {f"table_{name}": np.ascontiguousarray(a) for name, a in shape_tables().items()}

    def declare(name, a):
        return nc.dram_tensor(name, a.shape, mybir.dt.from_np(a.dtype), kind="ExternalInput").ap()
    d = {name[3:]: declare(name, a) for name, a in arrays.items()}
    tb = {name[6:]: declare(name, a) for name, a in tables.items()}
    out = nc.dram_tensor("out", (1, T, D), F32, kind="ExternalOutput").ap()
    scratch = nc.dram_tensor("distance_bias_line", (NSA_HEADS, 2 * T), F32, kind="Internal").ap()
    three_blocks_kernel(nc, d, tb, scratch, out)
    r = run_bass_kernel_spmd(nc, [{**arrays, **tables}], core_ids=[0])
    return r.results[0]["out"]
```
